# Optimizing a Trainium2 kernel written in Bass

```python
import math
import jax, jax.numpy as jnp
from jax import lax
import numpy as np

D_MODEL = 1024
BATCH = 1
SEQ = 1024
DEPTH = 1

CHUNK = 64
D_MIX = D_MODEL
D_ATTN = D_MIX // 2
D_SSM = D_MIX - D_ATTN
HEAD_DIM = 64
N_Q_HEADS = D_ATTN // HEAD_DIM
N_KV_HEADS = 2
GQA_GROUP = N_Q_HEADS // N_KV_HEADS
D_KV = N_KV_HEADS * HEAD_DIM
WINDOW = 128
WINDOW_CHUNKS = WINDOW // CHUNK
SSM_GROUP_CH = 16
N_SSM_GROUPS = D_SSM // SSM_GROUP_CH
SSM_STATE = 64
D_IN_PROJ = D_ATTN + 2 * D_KV + D_SSM
D_FF = 2816
EPS = 1e-6
DT_MIN = 1e-3
DT_MAX = 1e-1

kernel_name = "hymba_swa_sink_s5_macaron"

def rms_norm(x, g):
    xf = x.astype(jnp.float32)
    y = xf * lax.rsqrt(jnp.mean(xf * xf, axis=-1, keepdims=True) + EPS)
    return (y * g.astype(jnp.float32)).astype(x.dtype)

def swiglu(h, w_gate, w_up, w_down):
    return (jax.nn.silu(h @ w_gate) * (h @ w_up)) @ w_down

def alibi_slopes():
    h = np.arange(1, N_Q_HEADS + 1, dtype=np.float32)
    return jnp.asarray(2.0 ** (-8.0 * h / N_Q_HEADS), dtype=jnp.float32)

def banded_sink_attention(q, k, v, sink):
    bsz, L = q.shape[0], q.shape[1]
    nc = L // CHUNK
    kw = WINDOW_CHUNKS * CHUNK
    q = q.reshape(bsz, nc, CHUNK, N_KV_HEADS, GQA_GROUP, HEAD_DIM)
    k = k.reshape(bsz, nc, CHUNK, N_KV_HEADS, HEAD_DIM)
    v = v.reshape(bsz, nc, CHUNK, N_KV_HEADS, HEAD_DIM)
    pad = ((0, 0), (WINDOW_CHUNKS - 1, 0), (0, 0), (0, 0), (0, 0))
    kp = jnp.pad(k, pad)
    vp = jnp.pad(v, pad)
    k_win = jnp.concatenate([kp[:, w:w + nc] for w in range(WINDOW_CHUNKS)], axis=2)
    v_win = jnp.concatenate([vp[:, w:w + nc] for w in range(WINDOW_CHUNKS)], axis=2)
    scores = jnp.einsum('bnqkgd,bnskd->bkgnqs', q, k_win,
                        preferred_element_type=jnp.float32) * (HEAD_DIM ** -0.5)
    qi = jnp.arange(CHUNK, dtype=jnp.float32)[:, None]
    kj = jnp.arange(kw, dtype=jnp.float32)[None, :] - (WINDOW_CHUNKS - 1) * CHUNK
    dist = jnp.abs(qi - kj)
    slopes = alibi_slopes().reshape(N_KV_HEADS, GQA_GROUP, 1, 1, 1)
    scores = scores - slopes * dist
    cidx = jnp.arange(nc)[:, None]
    kblk = (jnp.arange(kw) // CHUNK)[None, :]
    valid = (cidx + kblk - (WINDOW_CHUNKS - 1)) >= 0
    scores = jnp.where(valid[:, None, :], scores, -jnp.inf)
    sink_b = sink.astype(jnp.float32).reshape(N_KV_HEADS, GQA_GROUP, 1, 1, 1)
    m = jnp.maximum(jnp.max(scores, axis=-1, keepdims=True), sink_b)
    p = jnp.exp(scores - m)
    p = p / (jnp.sum(p, axis=-1, keepdims=True) + jnp.exp(sink_b - m))
    o = jnp.einsum('bkgnqs,bnskd->bnqkgd', p.astype(v.dtype), v_win)
    return o.reshape(bsz, L, D_ATTN)

def s5_ssm_glu(u, a_re, a_im, b_re, b_im, c_re, c_im, d_skip, log_dt, w_glu, b_glu):
    bsz, L = u.shape[0], u.shape[1]
    f32 = jnp.float32
    uf = u.astype(f32).reshape(bsz, L, N_SSM_GROUPS, SSM_GROUP_CH)
    lam = lax.complex(a_re.astype(f32), a_im.astype(f32))
    dt = jnp.exp(log_dt.astype(f32))[:, None]
    lam_bar = jnp.exp(lam * dt)
    b = lax.complex(b_re.astype(f32), b_im.astype(f32))
    b_bar = ((lam_bar - 1.0) / lam)[..., None] * b
    c = lax.complex(c_re.astype(f32), c_im.astype(f32))
    bu = jnp.einsum('blgh,gph->blgp', uf.astype(jnp.complex64), b_bar)
    a = jnp.broadcast_to(lam_bar[None, None], bu.shape)

    def combine(e1, e2):
        a1, s1 = e1
        a2, s2 = e2
        return a1 * a2, a2 * s1 + s2

    _, states = lax.associative_scan(combine, (a, bu), axis=1)
    y = jnp.real(jnp.einsum('blgp,ghp->blgh', states, c))
    y = y + d_skip.astype(f32).reshape(N_SSM_GROUPS, SSM_GROUP_CH) * uf
    y = y.reshape(bsz, L, D_SSM).astype(u.dtype)
    z = jax.nn.gelu(y)
    return z * jax.nn.sigmoid(z @ w_glu + b_glu)

def setup_inputs(seed: int = 0) -> dict:
    key = jax.random.key(seed)
    ks = jax.random.split(key, 32)
    f32 = jnp.float32

    def nrm(k, shape, scale):
        return jax.random.normal(k, shape, f32) * scale

    def gain(k, shape):
        return 1.0 + 0.02 * jax.random.normal(k, shape, f32)

    Ld = DEPTH
    G, P, H = N_SSM_GROUPS, SSM_STATE, SSM_GROUP_CH
    n = jnp.arange(P, dtype=f32)
    a_re = -0.5 + 0.01 * jax.random.normal(ks[7], (Ld, G, P), f32)
    a_im = jnp.pi * n[None, None, :] + 0.01 * jax.random.normal(ks[8], (Ld, G, P), f32)
    log_dt = jax.random.uniform(ks[15], (Ld, G), f32,
                                minval=math.log(DT_MIN), maxval=math.log(DT_MAX))
    return {
        "x": jax.random.normal(ks[0], (BATCH, SEQ, D_MODEL), f32),
        "ff1_norm": gain(ks[1], (Ld, D_MODEL)),
        "ff1_w_gate": nrm(ks[2], (Ld, D_MODEL, D_FF), D_MODEL ** -0.5),
        "ff1_w_up": nrm(ks[3], (Ld, D_MODEL, D_FF), D_MODEL ** -0.5),
        "ff1_w_down": nrm(ks[4], (Ld, D_FF, D_MODEL), D_FF ** -0.5),
        "mix_norm": gain(ks[5], (Ld, D_MODEL)),
        "w_in": nrm(ks[6], (Ld, D_MODEL, D_IN_PROJ), D_MODEL ** -0.5),
        "sink": nrm(ks[9], (Ld, N_Q_HEADS), 0.5),
        "a_re": a_re,
        "a_im": a_im,
        "b_re": nrm(ks[10], (Ld, G, P, H), (2.0 * H) ** -0.5),
        "b_im": nrm(ks[11], (Ld, G, P, H), (2.0 * H) ** -0.5),
        "c_re": nrm(ks[12], (Ld, G, H, P), (2.0 * P) ** -0.5),
        "c_im": nrm(ks[13], (Ld, G, H, P), (2.0 * P) ** -0.5),
        "d_skip": nrm(ks[14], (Ld, D_SSM), 1.0),
        "log_dt": log_dt,
        "w_glu": nrm(ks[16], (Ld, D_SSM, D_SSM), D_SSM ** -0.5),
        "b_glu": nrm(ks[17], (Ld, D_SSM), 0.01),
        "attn_out_norm": gain(ks[18], (Ld, D_ATTN)),
        "ssm_out_norm": gain(ks[19], (Ld, D_SSM)),
        "w_out": nrm(ks[20], (Ld, D_MIX, D_MODEL), D_MIX ** -0.5),
        "ff2_norm": gain(ks[21], (Ld, D_MODEL)),
        "ff2_w_gate": nrm(ks[22], (Ld, D_MODEL, D_FF), D_MODEL ** -0.5),
        "ff2_w_up": nrm(ks[23], (Ld, D_MODEL, D_FF), D_MODEL ** -0.5),
        "ff2_w_down": nrm(ks[24], (Ld, D_FF, D_MODEL), D_FF ** -0.5),
        "final_norm": gain(ks[25], (D_MODEL,)),
    }

def reference(x, ff1_norm, ff1_w_gate, ff1_w_up, ff1_w_down, mix_norm, w_in, sink,
              a_re, a_im, b_re, b_im, c_re, c_im, d_skip, log_dt, w_glu, b_glu,
              attn_out_norm, ssm_out_norm, w_out, ff2_norm, ff2_w_gate, ff2_w_up,
              ff2_w_down, final_norm):
    bsz, L = x.shape[0], x.shape[1]
    for l in range(DEPTH):
        x = x + 0.5 * swiglu(rms_norm(x, ff1_norm[l]), ff1_w_gate[l], ff1_w_up[l], ff1_w_down[l])
        h = rms_norm(x, mix_norm[l])
        proj = h @ w_in[l]
        q = proj[..., :D_ATTN].reshape(bsz, L, N_Q_HEADS, HEAD_DIM)
        k = proj[..., D_ATTN:D_ATTN + D_KV].reshape(bsz, L, N_KV_HEADS, HEAD_DIM)
        v = proj[..., D_ATTN + D_KV:D_ATTN + 2 * D_KV].reshape(bsz, L, N_KV_HEADS, HEAD_DIM)
        u = proj[..., D_ATTN + 2 * D_KV:]
        attn = banded_sink_attention(q, k, v, sink[l])
        ssm = s5_ssm_glu(u, a_re[l], a_im[l], b_re[l], b_im[l], c_re[l], c_im[l],
                         d_skip[l], log_dt[l], w_glu[l], b_glu[l])
        mixed = jnp.concatenate([rms_norm(attn, attn_out_norm[l]),
                                 rms_norm(ssm, ssm_out_norm[l])], axis=-1)
        x = x + mixed @ w_out[l]
        x = x + 0.5 * swiglu(rms_norm(x, ff2_norm[l]), ff2_w_gate[l], ff2_w_up[l], ff2_w_down[l])
    return rms_norm(x, final_norm)


_drawn_inputs = setup_inputs


def setup_inputs(seed=0):
    import zlib

    import numpy as np

    out = dict(_drawn_inputs(seed))
    spreads = {}
    factors = {'ff1_norm': 5.355,
     'mix_norm': 2.817,
     'sink': 21.36,
     'a_re': 200.0,
     'b_glu': 44.19,
     'attn_out_norm': 140.424,
     'ssm_out_norm': 137.013,
     'ff2_norm': 29.832,
     'final_norm': 21.904,
     'a_im': 34.328,
     'b_re': 49.16,
     'b_im': 47.88,
     'c_re': 48.328,
     'c_im': 48.0,
     'log_dt': 36.784}
    for name, (base, spread) in spreads.items():
        noise = np.random.default_rng([zlib.crc32(name.encode()), seed]).standard_normal(out[name].shape)
        drawn = base * np.exp(spread * noise) if base else spread * noise
        out[name] = __import__('jax').numpy.asarray(drawn.astype(out[name].dtype))
    for name, factor in factors.items():
        out[name] = (out[name] * factor).astype(out[name].dtype)
    return out
```

```python
import math
from contextlib import ExitStack

import numpy as np
import concourse.bass as bass
from concourse import mybir

F32 = mybir.dt.float32
F32R = mybir.dt.float32r
I32 = mybir.dt.int32
ALU = mybir.AluOpType
ACT = mybir.ActivationFunctionType
AX = mybir.AxisListType

P = 128
D = 1024
L = 1024
F = 2816
KD = D // P
HALF = 512
NCH = F // P // 2
HD = 64
NKV = 2
GQ = 4
CHUNK = 64
DA = 512
DS = 512
NG = 32
GH = 16
NS = 64
NJ = NG // 2
T = P // GH
NC = L // T
EPS = 1e-6

WS = 3
RS = 2

UNITS_FFN = 6 * NCH
U_FF1 = 0
U_IN = U_FF1 + UNITS_FFN
N_IN = 10
U_GLU = U_IN + N_IN
N_GLU = 2
U_OUT = U_GLU + N_GLU
N_OUT = KD
U_FF2 = U_OUT + N_OUT
N_UNITS = U_FF2 + UNITS_FFN

UNIT_DMAS = [1] * N_UNITS
for _u in range(U_IN + 6, U_IN + N_IN):
    UNIT_DMAS[_u] = 2
for _u in range(U_OUT, U_OUT + N_OUT):
    UNIT_DMAS[_u] = 3


def loads_until(unit):
    return 16 * sum(UNIT_DMAS[u] for u in range(unit % RS, unit + 1, RS))


NORM_TILES = [KD, KD, DA // P, DS // P, KD, KD]
N_FF1, N_MIX, N_ATT, N_SSM, N_FF2, N_END = range(6)


def squares_before(norm):
    return sum(2 * t for t in NORM_TILES[:norm])


NORMED = [N_FF1, N_MIX, N_ATT, N_SSM, N_FF2]


def split_before(norm):
    return sum(2 * NORM_TILES[n] for n in NORMED if n < norm)


TWO_PI_1 = 6.28125
TWO_PI_2 = 0.00193500518798828125
TWO_PI_3 = 2 * math.pi - TWO_PI_1 - TWO_PI_2
LN2_1 = 0.693359375
LN2_2 = math.log(2.0) - LN2_1
MAGIC = 1.5 * 2 ** 23

PREP_STEPS = 153
LINKS_PER_BATCH = 127
NORM_SCALE = [1 / D, 1 / D, 1 / DA, 0.25 / DS, 1 / D, 1 / D]
CONST_DMAS = 5 + 2 + 1 + 8 + 1


def src_of(tile, permuted):
    return tile.rearrange("p (t c) -> p t c", c=NC) if permuted else tile


def by_chunk(tile):
    return tile.rearrange("p (n q) -> p n q", q=CHUNK)


def att_tile(q, g, h):
    return q[:, h * 8:(h + 1) * 8, g, :]


def dst_of(tensor, k, h, permuted):
    if permuted:
        return tensor[:, k, :].rearrange("p (c t) -> p t c", t=T)[:, 4 * h:4 * h + 4, :]
    return tensor[:, k, h * HALF:(h + 1) * HALF]


def block_kernel(nc, x, ff1_norm, ff1_w_gate, ff1_w_up, ff1_w_down, mix_norm, w_in, sink, a_re, a_im,
                 b_re, b_im, c_re, c_im, d_skip, log_dt, w_glu, b_glu, attn_out_norm, ssm_out_norm,
                 w_out, ff2_norm, ff2_w_gate, ff2_w_up, ff2_w_down, final_norm, ident_c, bias_c, out):
    ctx = ExitStack()

    ctx.enter_context(nc.allow_non_contiguous_dma(reason="vectors of a few KB"))

    base = (nc.sbuf_base + 31) // 32 * 32
    KB = 1024

    def at(name, off, shape, dt=F32):
        return nc.alloc_sbuf_tensor_at(name, shape, dt, offset=base + off)

    a_x, a_h, a_w = 0, 32 * KB, 96 * KB
    a_a = a_w + 32 * KB
    a_t = a_a + 24 * KB
    a_s = a_t + 34 * KB

    xT = at("xT", a_x, [P, KD, L])
    hT_hi = at("hT_hi", a_h, [P, KD, L], F32R)
    hT_lo = at("hT_lo", a_h + 32 * KB, [P, KD, L], F32R)
    x_in = at("x_in", a_h + 32 * KB, [P, KD, D])
    w_hi = [at(f"w_hi{s}", a_w + 4 * KB * s, [P, 1024], F32R) for s in range(WS)]
    w_lo = [at(f"w_lo{s}", a_w + 12 * KB + 4 * KB * s, [P, 1024], F32R) for s in range(WS)]
    raw = [at(f"raw{s}", a_w + 24 * KB + 4 * KB * s, [P, 1024]) for s in range(RS)]
    aT_hi = at("aT_hi", a_a, [P, 4, HALF], F32R)
    aT_lo = at("aT_lo", a_a + 8 * KB, [P, 4, HALF], F32R)
    sg = at("sg", a_a + 16 * KB, [P, 4, HALF])
    def norm_scratch(name, off):
        return (at("rstd" + name, off, [P, L]), at("nwt" + name, off + 4 * KB, [P, 2, HALF]),
                at("std" + name, off + 8 * KB, [P, HALF]), at("nvar" + name, off + 10 * KB, [P, HALF]),
                at("htmp" + name, off + 12 * KB, [P, 2, HALF]))

    scratch_ff = norm_scratch("_ff", a_a)
    scratch_mix = norm_scratch("_mix", a_t + 18 * KB)

    def scratch(norm):
        return scratch_mix if norm in (N_ATT, N_SSM) else scratch_ff

    qT = at("qT", a_a, [P, L // CHUNK, GQ, CHUNK])
    kTp = at("kTp", a_a + 16 * KB, [P, CHUNK + L])
    CL = at("CL", a_t, [P, 2, NJ, (T + 1) * GH])
    Et = at("Et", a_t + 18 * KB, [P, NJ, 2, P])
    vTp = at("vTp", a_t + 18 * KB, [P, CHUNK + L])
    yT = at("yT", a_t + 18 * KB, [P, 4, L])
    zT = at("zT", a_t, [P, 4, L])
    u8 = at("u8", a_h, [P, NG, NC])
    Mt = at("Mt", a_h + 16 * KB, [P, NG, P])
    tr = at("tr", a_h + 32 * KB, [P, NJ, NC])
    ti = at("ti", a_h + 40 * KB, [P, NJ, NC])
    kst = at("kst", a_h + 32 * KB, [GH, NG, P])
    csn = at("csn", a_h + 48 * KB, [P, 2, NJ, NC])
    ebs = at("ebs", a_h + 48 * KB, [P, 2, NJ, P])
    off = [a_s]

    def small(name, shape, dt=F32):
        t = at(name, off[0], shape, dt)
        n = 4
        for s in shape[1:]:
            n *= s
        off[0] += (n + 31) // 32 * 32
        return t

    ident = small("ident", [P, P])
    ones = small("ones", [P, P])
    gains = small("gains", [P, 40])
    G_COL = {N_FF1: 0, N_MIX: 8, N_ATT: 16, N_SSM: 20, N_FF2: 24, N_END: 32}
    eps_t = small("eps_t", [P, 1])
    bglu = small("bglu", [P, 4])
    bglu_h = small("bglu_h", [P, 4])
    sinkt = small("sinkt", [P, 2, 2, 2])
    par = small("par", [P, 3, NJ])
    NPAR = 40
    pw = at("pw", a_a + 16 * KB, [P, NPAR, NJ])
    pwi = at("pwi", a_a + 20 * KB, [P, 2, NJ], I32)
    lam = small("lam", [P, 3, T + 1, NJ])
    rot8 = small("rot8", [P, 2, NJ])
    dec8 = small("dec8", [P, NJ])
    dsk = small("dsk", [GH, NG])
    zero = small("zero", [P, (T - 1) * GH])
    unit = small("unit", [P, 2, 4, 1])
    mark = small("mark", [P, 1])
    Bb = small("Bb", [P, 2, NJ, GH])
    mx = small("mx", [P, 8])
    nm = small("nm", [P, 8])
    esk = small("esk", [P, 8])
    ssum = small("ssum", [P, 8])
    rden = small("rden", [P, 8])
    a_v = off[0]
    b_raw = at("b_raw", a_v, [P, 2, NJ, GH])
    c_in = at("c_in", a_v + 2 * KB, [P, 2, 4, 2, NS])
    CT = at("CT", a_v + 6 * KB, [P, 2, NJ, GH])
    ptmp = at("ptmp", a_v + 8 * KB, [P, 2, 256])
    EBb = at("EBb", a_v + 2 * KB, [P, 2, 4, P])
    ssq = at("ssq", a_v + 10 * KB, [P, L])
    sqt = at("sqt", a_v + 2 * KB, [P, 2, HALF])
    cur = at("cur", a_v, [P, 2, 4, GH + T + 1 + 1])
    bc_tmp = at("bc_tmp", a_v + 8 * KB, [P, 2, NJ, GH])
    gth = at("gth", a_v + 6 * KB, [P, 2, HALF])
    ust = [at(f"ust{i}", a_v + 4 * KB * i, [P, T, NC]) for i in range(2)]
    dgl = at("dgl", a_v + 12 * KB, [GH, NG, GH])
    vwin = at("vwin", a_v, [P, 2 * 8, P])
    biast = at("biast", a_a + 20 * KB + 512, [P, NKV, 256])
    sco = at("sco", a_v + 8 * KB, [P, 2, 2, 2, P])
    pts = at("pts", a_h + 32 * KB, [P, 2, 2, 2, P])
    rtm = at("rtm", a_v + 8 * KB, [P, 3, HALF])
    osb = at("osb", a_h, [P, 2, D])
    assert base + a_v + 14 * KB <= nc.sbuf_usable_end, (base + a_v + 14 * KB, nc.sbuf_usable_end)

    bank = [ctx.enter_context(nc.psum_tensor(f"bank{i}", [P, HALF], F32)) for i in range(8)]

    u_d = nc.dram_tensor("u_scratch", (DS, T, NC), F32, kind="Internal").ap()
    y_d = nc.dram_tensor("y_scratch", (DS, T, NC), F32, kind="Internal").ap()
    eb_d = nc.dram_tensor("eb_scratch", (P, 2, NJ, P), F32, kind="Internal").ap()
    cs_d = nc.dram_tensor("cs_scratch", (P, 2, NJ, NC), F32, kind="Internal").ap()
    k_d = nc.dram_tensor("k_scratch", (NG, GH, (2 * T - 1) * GH), F32, kind="Internal").ap()

    def sem(name):
        return ctx.enter_context(nc.semaphore(name))

    x_loaded = [sem(f"x_loaded{h}") for h in range(2)]
    consts_loaded = sem("consts_loaded")
    ident_loaded = sem("ident_loaded")
    params_loaded = sem("params_loaded")
    c_loaded = sem("c_loaded")
    consts_set = sem("consts_set")
    raw_loaded = [sem(f"raw_loaded{s}") for s in range(RS)]
    w_hi_done = sem("w_hi_done")
    w_lo_done = sem("w_lo_done")
    xt_done = sem("xt_done")
    xt_act = sem("xt_act")
    xt_dve = sem("xt_dve")
    sq_done = sem("sq_done")
    ssq_done = sem("ssq_done")
    sum_ready = sem("sum_ready")
    std_done = sem("std_done")
    rstd_done = sem("rstd_done")
    h_tmp = sem("h_tmp")
    h_hi = sem("h_hi")
    h_lo = sem("h_lo")
    ff_out = sem("ff_out")
    gate_taken = sem("gate_taken")
    up_taken = sem("up_taken")
    a_hi_done = sem("a_hi_done")
    a_lo_done = sem("a_lo_done")
    down_taken = sem("down_taken")
    ct_ready = sem("ct_ready")
    ct_taken = sem("ct_taken")
    prep_chain = sem("prep_chain")
    newton = sem("newton")
    pads_set = sem("pads_set")
    pool_chain = sem("pool_chain")
    eb_stored = sem("eb_stored")
    zero_stored = sem("zero_stored")
    proj_out = sem("proj_out")
    proj_taken = sem("proj_taken")
    u_stored = sem("u_stored")
    u8_loaded = sem("u8_loaded")
    eb_loaded = sem("eb_loaded")
    cs_loaded = sem("cs_loaded")
    bias_loaded = sem("bias_loaded")
    v_ready = sem("v_ready")
    v_taken = sem("v_taken")
    e_ready = sem("e_ready")
    e_taken = sem("e_taken")
    k_ready = sem("k_ready")
    k_taken = sem("k_taken")
    k_act = sem("k_act")
    diag_chain = sem("diag_chain")
    k_stored = sem("k_stored")
    m_loaded = sem("m_loaded")
    inj_ready = sem("inj_ready")
    state_chain = sem("state_chain")
    state_done = sem("state_done")
    y_ready = sem("y_ready")
    y_taken = sem("y_taken")
    y_stored = sem("y_stored")
    yt_loaded = sem("yt_loaded")
    s_ready = sem("s_ready")
    s_biased = sem("s_biased")
    att_chain = sem("att_chain")
    max_done = sem("max_done")
    exp_done = sem("exp_done")
    p_done = sem("p_done")
    pt_ready = sem("pt_ready")
    pt_taken = sem("pt_taken")
    o_ready = sem("o_ready")
    o_taken = sem("o_taken")
    z_done = sem("z_done")
    z_hi = sem("z_hi")
    z_lo = sem("z_lo")
    glu_out = sem("glu_out")
    glu_tanh = sem("glu_tanh")
    glu_done = sem("glu_done")
    mix_out = sem("mix_out")
    mix_taken = sem("mix_taken")
    fin_tmp = sem("fin_tmp")
    fin_ready = sem("fin_ready")
    fin_taken = sem("fin_taken")
    out_stored = [sem(f"out_stored{i}") for i in range(2)]

    FF = {0: (ff1_w_gate, ff1_w_up, ff1_w_down), 1: (ff2_w_gate, ff2_w_up, ff2_w_down)}
    U_OF = (U_FF1, U_FF2)
    OUTS_FFN = 24 * NCH

    def wk(t, k):
        return t[:, k * P:(k + 1) * P]

    def hs(h):
        return slice(h * HALF, (h + 1) * HALF)

    block = ctx.enter_context(nc.Block())

    @block.sync
    def _(sp):
        def load_unit(u, src, dst=None, wait=None):
            if wait is not None:
                sp.wait_ge(w_lo_done, wait)
            sp.dma_start(raw[u % RS][:, :] if dst is None else dst, src).then_inc(raw_loaded[u % RS], 16)

        def cols(w, f):
            return w.rearrange("(k p) f -> p k f", p=P)[:, :, f]

        def as3(u):
            return raw[u % RS][:, :].rearrange("p (k m) -> p k m", k=8)

        def gate_or_up(u, w, f, wait):
            load_unit(u, cols(w, bass.ds(f * P, P)), as3(u), wait)

        def down(u, w, f, wait):
            load_unit(u, w[bass.ds(f * P, P), :], None, wait)

        def ffn_loads(which):
            wg, wu, wd = (w[0] for w in FF[which])
            b = U_OF[which]
            for n, (w, f) in enumerate(((wg, 0), (wg, 1), (wu, 0), (wu, 1))):
                gate_or_up(b + n, w, f, b + n - RS + 1 if b + n >= RS else None)
            with sp.Fori(0, NCH - 1) as i:
                b0 = b + 4
                for n, (w, f) in enumerate(((wg, 2), (wg, 3), (wd, 0), (wd, 1), (wu, 2), (wu, 3))):
                    wait = i * 6 + (b0 + n - RS + 1)
                    (down if w is wd else gate_or_up)(b0 + n, w, i * 2 + f, wait)
            for n in range(2):
                u = b + UNITS_FFN - 2 + n
                down(u, wd, 2 * (NCH - 1) + n, u - RS + 1)

        sp.dma_start(ident[:, :], ident_c).then_inc(ident_loaded, 16)
        for t in range(KD):
            sp.dma_start(x_in[:, t, :], x[0, t * P:(t + 1) * P, :]).then_inc(x_loaded[t // 4], 16)
        ffn_loads(0)

        w = w_in[0]
        for n in range(N_IN):
            u = U_IN + n
            if n < 4:
                load_unit(u, cols(w, slice(768 + n * P, 768 + (n + 1) * P)), as3(u), u - RS + 1)
            elif n < 6:
                load_unit(u, cols(w, slice(512 + (n - 4) * P, 512 + (n - 3) * P)), as3(u), u - RS + 1)
            else:
                sp.wait_ge(w_lo_done, u - RS + 1)
                for kv in range(NKV):
                    c0 = kv * GQ * HD + (n - 6) * HD
                    sp.dma_start(as3(u)[:, :, kv * HD:(kv + 1) * HD],
                                 cols(w, slice(c0, c0 + HD))).then_inc(raw_loaded[u % RS], 16)
            if n >= 2 and n < 6:
                i = n - 2
                sp.wait_ge(proj_taken, 2 * i + 2)
                sp.dma_start(u_d[i * P:(i + 1) * P, :, :], ust[i % 2][:, :, :]).then_inc(u_stored, 16)
        for n in range(N_GLU):
            u = U_GLU + n
            load_unit(u, cols(w_glu[0], slice(n * 256, (n + 1) * 256)),
                      raw[u % RS][:, :].rearrange("p (k m) -> p k m", k=4), u - RS + 1)
        def load_out_unit(n):
            u = U_OUT + n
            sp.wait_ge(w_lo_done, u - RS + 1)
            for kv in range(NKV):
                src = w_out[0][kv * GQ * HD:(kv + 1) * GQ * HD, n * P:(n + 1) * P]
                sp.dma_start(as3(u)[kv * HD:(kv + 1) * HD, 0:4, :],
                             src.rearrange("(g d) m -> d g m", d=HD)).then_inc(raw_loaded[u % RS], 16)
            sp.dma_start(as3(u)[:, 4:8, :],
                         w_out[0][DA:, n * P:(n + 1) * P].rearrange("(k p) m -> p k m", p=P)
                         ).then_inc(raw_loaded[u % RS], 16)

        load_out_unit(0)
        load_out_unit(1)
        sp.wait_ge(proj_out, 2 * N_IN)
        sp.wait_ge(eb_stored, 4 * 32)
        sp.dma_start(ebs[:, :, :, :], eb_d).then_inc(eb_loaded, 16)
        sp.dma_start(biast[:, :, :], bias_c).then_inc(bias_loaded, 16)
        sp.wait_ge(u_stored, 64)
        u_v = u_d.rearrange("(g h) t c -> t h g c", h=GH)
        for t in range(T):
            sp.dma_start(u8[t * GH:(t + 1) * GH, :, :], u_v[t]).then_inc(u8_loaded, 16)
        sp.wait_ge(k_taken, 8)
        sp.wait_ge(zero_stored, 64)
        sp.dma_start(k_d.rearrange("g h c -> h g c")[:, :, (T - 1) * GH:], kst[:, :, :]).then_inc(k_stored, 16)
        sp.wait_ge(e_taken, 8)
        sp.dma_start(csn[:, :, :, :], cs_d).then_inc(cs_loaded, 16)
        sp.wait_ge(k_stored, 16)
        for t in range(T):
            c0 = (T - 1 - t) * GH
            sp.dma_start(Mt[t * GH:(t + 1) * GH, :, :],
                         k_d.rearrange("g h c -> h g c")[:, :, c0:c0 + P]).then_inc(m_loaded, 16)
        sp.wait_ge(y_taken, 8)
        y_v = y_d.rearrange("(g h) t c -> t h g c", h=GH)
        for t in range(T):
            sp.dma_start(y_v[t], u8[t * GH:(t + 1) * GH, :, :]).then_inc(y_stored, 16)
        sp.wait_ge(y_stored, 16 * T)
        sp.dma_start(yT[:, :, :].rearrange("p i (t c) -> p i t c", t=T),
                     y_d.rearrange("(i p) t c -> p i t c", p=P)).then_inc(yt_loaded, 16)
        for n in range(2, N_OUT):
            load_out_unit(n)
        ffn_loads(1)
        for t in range(KD):
            sp.wait_ge(fin_taken, 2 * t + 2)
            sp.dma_start(out[0, t * P:(t + 1) * P, :], osb[:, t % 2, :]).then_inc(out_stored[t % 2], 16)
        for i in range(2):
            sp.wait_ge(out_stored[i], 16 * KD // 2)

    @block.tensor
    def _(pe):
        def mm3(o, wh, wl, rh, rl, first, last):
            nc.tensor.matmul(o, wl, rh, start=first, stop=False)
            nc.tensor.matmul(o, wh, rl, start=False, stop=False)
            return nc.tensor.matmul(o, wh, rh, start=False, stop=last)

        def norm_sum(norm):
            for h in range(2):
                n = squares_before(norm)
                kt = NORM_TILES[norm]
                pe.wait_ge(ssq_done, n + (h + 1) * kt if norm in (N_FF1, N_ATT, N_SSM) else n + 2 * kt - 1 + h)
                if norm or h:
                    pe.wait_ge(rstd_done, 2 * norm + h)
                nc.tensor.matmul(bank[7][:, :], ones[:, :], ssq[:, hs(h)], start=True,
                                 stop=True).then_inc(sum_ready, 1)

        def wide_unit(u_done, slot, banks, waits, done, norm=None):
            for h in range(2):
                for s, v in waits[h]:
                    pe.wait_ge(s, v)
                if h == 0:
                    pe.wait_ge(w_lo_done, u_done)
                for k in range(KD):
                    if norm is not None:
                        pe.wait_ge(h_lo, split_before(norm) + h * KD + k + 1)
                    last = mm3(bank[banks[h]][:, :], wk(w_hi[slot], k), wk(w_lo[slot], k),
                               hT_hi[:, k, hs(h)], hT_lo[:, k, hs(h)], k == 0, k == KD - 1)
                last.then_inc(done, 1)

        def ffn(which, norm):
            b = U_OF[which]
            g0 = 4 * NCH * which
            d0 = 16 * NCH * which
            for f in range(2):
                wide_unit(b + f + 1, (b + f) % WS, (2 * f, 2 * f + 1), ([], []), ff_out,
                          norm if f == 0 else None)
            for f in range(2):
                waits = [[(gate_taken, g0 + 2 * f + h + 1)] for h in range(2)]
                wide_unit(b + 2 + f + 1, (b + 2 + f) % WS, (2 * f, 2 * f + 1), waits, ff_out)

            def down(units_ready, slots, a_ready, d_base):
                pe.wait_ge(w_lo_done, units_ready)
                pe.wait_ge(a_lo_done, a_ready)
                for n in range(16):
                    d, h = n // 2, n % 2
                    if n >= 3:
                        pe.wait_ge(down_taken, d_base + (n - 2))
                    o = bank[4 + n % 3][:, :]
                    for f in range(2):
                        last = mm3(o, wk(w_hi[slots[f]], d), wk(w_lo[slots[f]], d),
                                   aT_hi[:, 2 * f + h, :], aT_lo[:, 2 * f + h, :], f == 0, f == 1)
                    last.then_inc(ff_out, 1)

            def body(i, dbase):
                ub = b + 4
                for f in range(2):
                    waits = [[(up_taken, i * 4 + (g0 + 2 * f + h + 1))] for h in range(2)]
                    wide_unit(i * 6 + (ub + f + 1), (ub + f) % WS, (2 * f, 2 * f + 1), waits, ff_out)
                down(i * 6 + (ub + 4), ((ub + 2) % WS, (ub + 3) % WS), i * 4 + (g0 + 4), dbase)
                for f in range(2):
                    waits = [[(gate_taken, i * 4 + (g0 + 4 + 2 * f + h + 1))] for h in range(2)]
                    wide_unit(i * 6 + (ub + 4 + f + 1), (ub + 4 + f) % WS, (2 * f, 2 * f + 1), waits, ff_out)

            with pe.Fori(0, NCH - 1) as i:
                body(i, i * 16 + d0)
            u = b + UNITS_FFN - 2
            down(u + 2, (u % WS, (u + 1) % WS), g0 + 4 * NCH, d0 + 16 * (NCH - 1))

        pe.wait_ge(ident_loaded, 16)
        for t in range(KD):
            pe.wait_ge(x_loaded[t // 4], 64)
            for kh in range(2):
                if t >= 4:
                    pe.wait_ge((xt_act, xt_dve)[kh], t - 3)
                for kk in range(4):
                    k = 4 * kh + kk
                    last = nc.tensor.transpose(bank[(2 * t + kh) % 8][:, kk * P:(kk + 1) * P],
                                               x_in[:, t, k * P:(k + 1) * P], ident[:, :])
                last.then_inc(xt_done, 1)
        pe.wait_ge(xt_act, KD)
        pe.wait_ge(xt_dve, KD)
        pe.wait_ge(c_loaded, 64)
        for ri in range(2):
            for i in range(4):
                last = nc.tensor.transpose(bank[ri][:, i * P:(i + 1) * P],
                                           c_in[:, ri, i, :, :].rearrange("p a s -> p (a s)"), ident[:, :])
            last.then_inc(ct_ready, 1)
        pe.wait_ge(consts_set, 1)
        norm_sum(N_FF1)
        pe.wait_ge(ct_taken, 4)
        ffn(0, N_FF1)

        norm_sum(N_MIX)
        for n in range(N_IN):
            u = U_IN + n
            waits = [[(proj_taken, 2 * n + h - 3)] if n >= 2 else [] for h in range(2)]
            if n == 0:
                waits = [[(up_taken, 4 * NCH)], []]
            wide_unit(u + 1, u % WS, ((2 * n) % 4, (2 * n + 1) % 4), waits, proj_out, N_MIX if n == 0 else None)

        pe.wait_ge(proj_taken, 2 * N_IN)
        pe.wait_ge(pads_set, 1)
        for b in range(4):
            for m in range(4):
                n = 4 * b + m
                last = nc.tensor.transpose(bank[b][:, m * P:(m + 1) * P], vTp[:, CHUNK * n:CHUNK * n + P],
                                           ident[:, :])
            last.then_inc(v_ready, 1)
        for b in range(8):
            j0, g2 = 4 * (b // 2), b % 2
            r = slice(g2 * NS, (g2 + 1) * NS)
            if b >= 4:
                pe.wait_ge(k_taken, b - 3)
            for jj in range(4):
                for ri in range(2):
                    last = nc.tensor.matmul(bank[4 + b % 4][0:GH, jj * P:(jj + 1) * P], Bb[r, ri, j0 + jj, :],
                                            CL[r, ri, j0 + jj, 0:P], start=ri == 0, stop=ri == 1)
            last.then_inc(k_ready, 1)
        pe.wait_ge(eb_loaded, 16)
        pe.wait_ge(v_taken, 4)
        for b in range(8):
            if b >= 4:
                pe.wait_ge(e_taken, b - 3)
            for jj in range(2):
                for ri in range(2):
                    m = 2 * jj + ri
                    last = nc.tensor.transpose(bank[b % 4][:, m * P:(m + 1) * P], ebs[:, ri, 2 * b + jj, :],
                                               ident[:, :])
            last.then_inc(e_ready, 1)
        pe.wait_ge(e_taken, 8)
        pe.wait_ge(k_taken, 8)
        pe.wait_ge(u8_loaded, 16 * T)
        for b in range(4):
            for ri in range(2):
                for jj in range(4):
                    j = 4 * b + jj
                    for g2 in range(2):
                        last = nc.tensor.matmul(bank[2 * b + ri][g2 * NS:(g2 + 1) * NS, jj * P:(jj + 1) * P],
                                                Et[:, j, ri, g2 * NS:(g2 + 1) * NS], u8[:, 2 * j + g2, :],
                                                start=True, stop=True)
            last.then_inc(inj_ready, 1)
        pe.wait_ge(m_loaded, 16 * T)
        for b in range(4):
            pe.wait_ge(state_done, b + 1)
            for jj in range(4):
                j = 4 * b + jj
                for g2 in range(2):
                    g = 2 * j + g2
                    r = slice(g2 * NS, (g2 + 1) * NS)
                    o = bank[2 * b + g2][:, jj * P:(jj + 1) * P]
                    nc.tensor.matmul(o, Mt[:, g, :], u8[:, g, :], start=True, stop=False)
                    nc.tensor.matmul(o, CL[r, 0, j, GH:], tr[r, j, :], start=False, stop=False)
                    last = nc.tensor.matmul(o, CL[r, 1, j, GH:], ti[r, j, :], start=False, stop=True)
                    if jj == 3:
                        last.then_inc(y_ready, 1)

        def scores(m):
            pe.wait_ge(y_taken, 8)
            for kv in range(NKV):
                if m >= 2:
                    pe.wait_ge(s_biased, 4 * m - 4)
                r = slice(kv * HD, (kv + 1) * HD)
                for nn in range(2):
                    n = 2 * m + nn
                    for a in range(2):
                        o = bank[2 * (m % 2) + kv][:, (2 * nn + a) * P:(2 * nn + a + 1) * P]
                        last = nc.tensor.matmul(o, qT[r, n, 2 * a:2 * a + 2, :].rearrange("p g q -> p (g q)"),
                                                kTp[r, n * CHUNK:n * CHUNK + P], start=True, stop=True)
                last.then_inc(s_ready, 1)

        def weighted(m):
            pe.wait_ge(p_done, m + 1)
            if m >= 1:
                pe.wait_ge(pt_taken, 2 * m)
            for kv in range(NKV):
                for nn in range(2):
                    for a in range(2):
                        o = bank[4 + kv][:, (2 * nn + a) * P:(2 * nn + a + 1) * P]
                        last = nc.tensor.transpose(o, sco[:, kv, nn, a, :], ident[:, :])
                last.then_inc(pt_ready, 1)
            if m >= 1:
                pe.wait_ge(o_taken, m)
            pe.wait_ge(pt_taken, 2 * m + 2)
            for nn in range(2):
                for kv in range(NKV):
                    last = nc.tensor.matmul(bank[6][kv * HD:(kv + 1) * HD, nn * 256:(nn + 1) * 256],
                                            vwin[:, 2 * m + nn, kv * HD:(kv + 1) * HD],
                                            pts[:, kv, nn, :, :].rearrange("p a q -> p (a q)"),
                                            start=True, stop=True)
            last.then_inc(o_ready, 1)

        scores(0)
        for m in range(8):
            if m < 7:
                scores(m + 1)
            weighted(m)

        for n in range(N_GLU):
            u = U_GLU + n
            pe.wait_ge(w_lo_done, u + 1)
            for mm in range(2):
                for h in range(2):
                    o = 4 * n + 2 * mm + h
                    if o == 0:
                        pe.wait_ge(s_biased, 32)
                    if o >= 4:
                        pe.wait_ge(glu_tanh, o - 3)
                    for k in range(4):
                        if n == 0 and mm == 0:
                            pe.wait_ge(z_lo, 4 * h + k + 1)
                        c0 = k * 256 + mm * P
                        last = mm3(bank[o % 4][:, :], w_hi[u % WS][:, c0:c0 + P], w_lo[u % WS][:, c0:c0 + P],
                                   hT_hi[:, 4 + k, hs(h)], hT_lo[:, 4 + k, hs(h)], k == 0, k == 3)
                    last.then_inc(glu_out, 1)
        norm_sum(N_ATT)
        norm_sum(N_SSM)
        for n in range(N_OUT):
            u = U_OUT + n
            waits = [[(mix_taken, 2 * n + h - 3)] if n >= 2 else [(glu_tanh, 8), (glu_done, 8)]
                     for h in range(2)]
            if n == 0:
                waits[0].append((h_lo, split_before(N_FF2)))
            wide_unit(u + 1, u % WS, ((2 * n) % 4, (2 * n + 1) % 4), waits, mix_out)

        norm_sum(N_FF2)
        pe.wait_ge(mix_taken, 16)
        ffn(1, N_FF2)

        norm_sum(N_END)
        pe.wait_ge(down_taken, 32 * NCH)
        for t in range(KD):
            for kh in range(2):
                o = 2 * t + kh
                if kh == 0:
                    pe.wait_ge(fin_tmp, 8 * (t // 4 + 1))
                if o >= 4:
                    pe.wait_ge(fin_taken, o - 3)
                for kk in range(4):
                    k = 4 * kh + kk
                    last = nc.tensor.transpose(bank[o % 4][:, kk * P:(kk + 1) * P],
                                               xT[:, k, t * P:(t + 1) * P], ident[:, :])
                last.then_inc(fin_ready, 1)

    @block.scalar
    def _(act):
        def split_hi(u, wait_out, raw_value):
            act.wait_ge(raw_loaded[u % RS], raw_value)
            for s, v in wait_out:
                act.wait_ge(s, v)
            act.activation(w_hi[u % WS][:, :], raw[u % RS][:, :], ACT.Copy).then_inc(w_hi_done, 1)

        def square(norm, n, src, as_src=lambda v: v):
            c = squares_before(norm) + n
            if c >= 2:
                act.wait_ge(ssq_done, c - 1)
            act.activation(as_src(sqt[:, c % 2, :]), src, ACT.Square).then_inc(sq_done, 1)

        def norm_std(norm, h):
            act.wait_ge(sum_ready, 2 * norm + h + 1)
            if norm or h:
                act.wait_ge(rstd_done, 2 * norm + h)
            act.activation(scratch(norm)[2][:, :], bank[7][:, :], ACT.Sqrt, bias=eps_t[:, 0:1],
                           scale=NORM_SCALE[norm]).then_inc(std_done, 1)

        def norm_hi(norm, tile0, permuted=False):
            for h in range(2):
                norm_std(norm, h)
                for k in range(NORM_TILES[norm]):
                    c = split_before(norm) + h * NORM_TILES[norm] + k
                    act.wait_ge(h_tmp, c + 1)
                    act.activation(dst_of(hT_hi, tile0 + k, h, permuted), src_of(scratch(norm)[4][:, c % 2, :], permuted),
                                   ACT.Copy).then_inc(h_hi, 1)

        def ffn(which):
            b = U_OF[which]
            o0 = OUTS_FFN * which
            g0 = 4 * NCH * which

            def take_gate(i4, bnk, ob):
                act.wait_ge(ff_out, ob)
                if not (isinstance(i4, int) and i4 == 0):
                    act.wait_ge(a_lo_done, i4 - 4 + bnk + 1)
                act.activation(sg[:, bnk, :], bank[bnk][:, :], ACT.Silu).then_inc(gate_taken, 1)

            def a_hi(i4, bnk):
                act.wait_ge(up_taken, i4 + bnk + 1)
                act.activation(aT_hi[:, bnk, :], sg[:, bnk, :], ACT.Copy).then_inc(a_hi_done, 1)

            def split(off_u, i, ob):
                u = b + off_u
                split_hi(u, [(ff_out, ob)], i * 48 + loads_until(u))

            for f in range(2):
                if f == 1:
                    split_hi(b + 3, [(ff_out, o0 + 2)], loads_until(b + 3))
                for h in range(2):
                    take_gate(g0, 2 * f + h, o0 + 2 * f + h + 1)
            split_hi(b + 4, [(ff_out, o0 + 4)], loads_until(b + 4))
            for f in range(2):
                if f == 1:
                    split_hi(b + 5, [(ff_out, o0 + 6)], loads_until(b + 5))
                for h in range(2):
                    a_hi(g0, 2 * f + h)

            with act.Fori(0, NCH - 1) as i:
                ob = i * 24 + (o0 + 8)
                i4 = i * 4 + (g0 + 4)
                split(6, i, ob)
                for h in range(2):
                    take_gate(i4, h, ob + h + 1)
                split(7, i, ob + 2)
                for h in range(2):
                    take_gate(i4, 2 + h, ob + 2 + h + 1)
                split(8, i, ob + 4)
                split(9, i, ob + 20)
                split(10, i, ob + 20)
                for h in range(2):
                    a_hi(i4, h)
                split(11, i, ob + 22)
                for h in range(2):
                    a_hi(i4, 2 + h)

        for col, g, kt in ((0, ff1_norm[0], 8), (8, mix_norm[0], 8), (20, ssm_out_norm[0], 4),
                           (24, ff2_norm[0], 8), (32, final_norm, 8)):
            act.dma_start(gains[:, col:col + kt], g.rearrange("(k p) -> p k", p=P)).then_inc(consts_loaded, 16)
        for kv in range(NKV):
            act.dma_start(gains[kv * HD:(kv + 1) * HD, 16:20],
                          attn_out_norm[0][kv * 256:(kv + 1) * 256].rearrange("(g d) -> d g", d=HD)
                          ).then_inc(consts_loaded, 16)
        act.dma_start(bglu[:, :], b_glu[0].rearrange("(k p) -> p k", p=P)).then_inc(consts_loaded, 16)
        for g2 in range(2):
            for nn in range(2):
                for kv in range(NKV):
                    src = sink[0].rearrange("(v a g) -> g v a", v=2, g=2)[g2, kv].partition_broadcast(HD)
                    act.dma_start(sinkt[g2 * HD:(g2 + 1) * HD, kv, nn, :], src).then_inc(consts_loaded, 16)
        act.dma_start(dsk[:, :], d_skip[0].rearrange("(g h) -> h g", h=GH)).then_inc(consts_loaded, 16)
        for n, a in enumerate((a_re, a_im)):
            for g2 in range(2):
                act.dma_start(par[g2 * NS:(g2 + 1) * NS, n, :],
                              a[0].rearrange("(j g) p -> g p j", g=2)[g2]).then_inc(params_loaded, 16)
        for g2 in range(2):
            act.dma_start(par[g2 * NS:(g2 + 1) * NS, 2, :],
                          log_dt[0].rearrange("(j g) -> g j", g=2)[g2].partition_broadcast(NS)
                          ).then_inc(params_loaded, 16)
        for n, b in enumerate((b_re, b_im)):
            for g2 in range(2):
                act.dma_start(b_raw[g2 * NS:(g2 + 1) * NS, n, :, :],
                              b[0].rearrange("(j g) p h -> g p j h", g=2)[g2]).then_inc(params_loaded, 16)
        for n, c in enumerate((c_re, c_im)):
            for a in range(2):
                act.dma_start(c_in[:, n, :, a, :],
                              c[0].rearrange("(i g) h p -> (g h) i p", g=8)).then_inc(c_loaded, 16)

        for t in range(KD):
            act.wait_ge(xt_done, 2 * t + 1)
            act.activation(xT[:, 0:4, t * P:(t + 1) * P],
                           bank[(2 * t) % 8][:, :].rearrange("p (k m) -> p k m", k=4), ACT.Copy
                           ).then_inc(xt_act, 1)
        for ri in range(2):
            act.wait_ge(ct_ready, ri + 1)
            for g2 in range(2):
                r = slice(g2 * NS, (g2 + 1) * NS)
                src = bank[ri][r, :].rearrange("p (j g h) -> p g j h", g=2, h=GH)[:, g2]
                act.activation(CT[r, ri, :, :], src, ACT.Copy).then_inc(ct_taken, 1)
        for h in range(2):
            for k in range(KD):
                act.wait_ge(xt_act, 4 * h + 4)
                act.wait_ge(xt_dve, 4 * h + 4)
                square(N_FF1, h * KD + k, xT[:, k, hs(h)])
        act.wait_ge(consts_loaded, CONST_DMAS * 16)
        act.wait_ge(consts_set, 1)
        for u in range(WS):
            split_hi(u, [], loads_until(u))
            if u == 0:
                norm_hi(N_FF1, 0)
        ffn(0)

        def squares_behind(norm, taken, taken0):
            for n in range(16):
                act.wait_ge(taken, taken0 + n + 1)
                square(norm, n, xT[:, n // 2, hs(n % 2)])

        split_hi(U_IN, [(ff_out, OUTS_FFN - 16)], loads_until(U_IN))
        act.wait_ge(eb_stored, 4 * 32)
        squares_behind(N_MIX, down_taken, 16 * (NCH - 1))
        o_end = OUTS_FFN
        split_hi(U_IN + 1, [(ff_out, o_end)], loads_until(U_IN + 1))
        split_hi(U_IN + 2, [(ff_out, o_end)], loads_until(U_IN + 2))
        norm_hi(N_MIX, 0)

        for n in range(N_IN):
            u = U_IN + n
            if n:
                nxt = u + 2
                if nxt < U_FF2:
                    split_hi(nxt, [(proj_out, 2 * n)], loads_until(nxt))
            for h in range(2):
                act.wait_ge(proj_out, 2 * n + h + 1)
                src = bank[(2 * n + h) % 4][:, :]
                if n < 4:
                    if n >= 2:
                        act.wait_ge(u_stored, 16 * (n - 1))
                    dst = ust[n % 2][:, :, h * 64:(h + 1) * 64]
                    src = src.rearrange("p (c t) -> p t c", t=T)
                elif n < 6:
                    dst = (kTp, vTp)[n - 4][:, CHUNK + h * HALF:CHUNK + (h + 1) * HALF]
                else:
                    dst = att_tile(qT, n - 6, h)
                    src = by_chunk(src)
                act.activation(dst, src, ACT.Copy).then_inc(proj_taken, 1)
        split_hi(U_OUT, [(proj_out, 2 * N_IN)], loads_until(U_OUT))

        for b_ in range(8):
            act.wait_ge(k_ready, b_ + 1)
            j0, g2 = 4 * (b_ // 2), b_ % 2
            dst = kst[:, :, :].rearrange("p (j g) m -> p g j m", g=2)[:, g2, j0:j0 + 4, GH:]
            act.activation(dst, bank[4 + b_ % 4][0:GH, :].rearrange("p (j m) -> p j m", j=4)[:, :, GH:],
                           ACT.Copy).then_inc(k_act, 1)
        for b_ in range(8):
            act.wait_ge(e_ready, b_ + 1)
            act.activation(Et[:, 2 * b_:2 * b_ + 2, :, :],
                           bank[b_ % 4][:, :].rearrange("p (j r m) -> p j r m", j=2, r=2), ACT.Copy
                           ).then_inc(e_taken, 1)
        for o in range(8):
            b_, g2 = o // 2, o % 2
            act.wait_ge(y_ready, o + 1)
            dst = u8[:, :, :].rearrange("p (j g) c -> p g j c", g=2)[:, g2, 4 * b_:4 * b_ + 4, :]
            act.activation(dst, bank[o][:, :].rearrange("p (j c) -> p j c", j=4), ACT.Copy
                           ).then_inc(y_taken, 1)
        for m in range(8):
            act.wait_ge(max_done, m + 1)
            for s in range(8):
                kv, nn, a = s // 4, s // 2 % 2, s % 2
                act.activation(sco[:, kv, nn, a, :], sco[:, kv, nn, a, :], ACT.Exp, bias=nm[:, s:s + 1],
                               scale=1.0, accum_out=ssum[:, s:s + 1])
            act.activation(esk[:, :], esk[:, :], ACT.Exp).then_inc(exp_done, 1)
            for kv in range(NKV):
                act.wait_ge(pt_ready, 2 * m + kv + 1)
                if m:
                    act.wait_ge(o_ready, m)
                act.activation(pts[:, kv, :, :, :].rearrange("p n a q -> p (n a q)"), bank[4 + kv][:, :],
                               ACT.Copy).then_inc(pt_taken, 1)
            act.wait_ge(o_ready, m + 1)
            act.activation(qT[:, 2 * m:2 * m + 2, :, :].rearrange("p n g q -> p (n g q)"), bank[6][:, :], ACT.Copy
                           ).then_inc(o_taken, 1)
        act.wait_ge(yt_loaded, 16)
        for h in range(2):
            for k in range(4):
                act.activation(zT[:, k, hs(h)], yT[:, k, hs(h)], ACT.Gelu_apprx_tanh).then_inc(z_done, 1)
                act.wait_ge(z_done, 4 * h + k + 1)
                act.activation(hT_hi[:, 4 + k, hs(h)], zT[:, k, hs(h)], ACT.Copy).then_inc(z_hi, 1)
        for o in range(8):
            mt, h = o // 2, o % 2
            act.wait_ge(glu_out, o + 1)
            if o >= 2:
                act.wait_ge(glu_done, o - 1)
            act.activation(gth[:, o % 2, :], bank[o % 4][:, :], ACT.Tanh, bias=bglu_h[:, mt:mt + 1],
                           scale=0.5).then_inc(glu_tanh, 1)
        for h in range(2):
            for k in range(4):
                act.wait_ge(o_taken, 8)
                square(N_ATT, h * 4 + k, att_tile(qT, k, h), by_chunk)
        norm_hi(N_ATT, 0)
        for h in range(2):
            for k in range(4):
                act.wait_ge(glu_done, 8)
                square(N_SSM, h * 4 + k, zT[:, k, hs(h)])
        norm_hi(N_SSM, 4, True)
        split_hi(U_OUT + 1, [(glu_out, 4)], loads_until(U_OUT + 1))
        split_hi(U_OUT + 2, [(glu_out, 8)], loads_until(U_OUT + 2))
        for n in range(N_OUT):
            if n:
                nxt = U_OUT + n + 2
                split_hi(nxt, [(mix_out, 2 * n)], loads_until(nxt))
            for h in range(2):
                m = 2 * n + h
                act.wait_ge(mix_taken, m + 1)
                square(N_FF2, m, xT[:, n, hs(h)])
        split_hi(U_FF2 + 2, [(mix_out, 16)], loads_until(U_FF2 + 2))
        norm_hi(N_FF2, 0)
        ffn(1)
        squares_behind(N_END, down_taken, 16 * (2 * NCH - 1))
        for h in range(2):
            norm_std(N_END, h)
        for o in range(0, 16, 2):
            act.wait_ge(fin_ready, o + 1)
            act.wait_ge(fin_taken, o)
            t = o // 2
            if t >= 2:
                act.wait_ge(out_stored[t % 2], 16 * (t // 2))
            act.activation(osb[:, t % 2, 0:HALF], bank[o % 4][:, :], ACT.Copy).then_inc(fin_taken, 1)

    @block.vector
    def _(dve):
        def split_lo(u, count):
            dve.wait_ge(w_hi_done, count)
            dve.tensor_tensor(w_lo[u % WS][:, :], raw[u % RS][:, :], w_hi[u % WS][:, :].bitcast(F32),
                              ALU.subtract).then_inc(w_lo_done, 1)

        def norm_rstd(norm, h):
            rstd, nwt, std, nvar, _ = scratch(norm)
            r = rstd[:, hs(h)]
            n0 = 5 * (2 * norm + h)
            dve.wait_ge(std_done, 2 * norm + h + 1)
            dve.tensor_scalar(nvar[:, :], bank[7][:, :], NORM_SCALE[norm], EPS, ALU.mult, ALU.add
                              ).then_inc(newton, 1)
            dve.reciprocal(r, std[:, :]).then_inc(newton, 1)
            dve.wait_ge(newton, n0 + 2)
            dve.tensor_tensor(nwt[:, 0, :], r, r, ALU.mult).then_inc(newton, 1)
            dve.wait_ge(newton, n0 + 3)
            dve.tensor_tensor(nwt[:, 1, :], nwt[:, 0, :], nvar[:, :], ALU.mult).then_inc(newton, 1)
            dve.wait_ge(newton, n0 + 4)
            dve.tensor_scalar(nwt[:, 0, :], nwt[:, 1, :], -0.5, 1.5, ALU.mult, ALU.add).then_inc(newton, 1)
            dve.wait_ge(newton, n0 + 5)
            dve.tensor_tensor(r, r, nwt[:, 0, :], ALU.mult).then_inc(rstd_done, 1)
            dve.wait_ge(rstd_done, 2 * norm + h + 1)

        def norm_split(norm, src, tile0, permuted=False):
            kt = NORM_TILES[norm]
            rstd, htmp = scratch(norm)[0], scratch(norm)[4]
            c0 = split_before(norm)

            def lo(i):
                h, k = i // kt, i % kt
                dve.wait_ge(h_hi, c0 + i + 1)
                dve.tensor_tensor(dst_of(hT_lo, tile0 + k, h, permuted),
                                  src_of(htmp[:, (c0 + i) % 2, :], permuted),
                                  dst_of(hT_hi, tile0 + k, h, permuted).bitcast(F32),
                                  ALU.subtract).then_inc(h_lo, 1)

            for h in range(2):
                norm_rstd(norm, h)
                for k in range(kt):
                    i = h * kt + k
                    g = gains[:, G_COL[norm] + k:G_COL[norm] + k + 1]
                    if i >= 2:
                        dve.wait_ge(h_lo, c0 + i - 1)
                    s_, v = (att_tile(src, k, h), by_chunk) if norm == N_ATT else (src[:, k, hs(h)], lambda v: v)
                    dve.scalar_tensor_tensor(v(htmp[:, (c0 + i) % 2, :]), s_, g, v(rstd[:, hs(h)]),
                                             ALU.mult, ALU.mult).then_inc(h_tmp, 1)
                    if k:
                        lo(i - 1)
                lo(h * kt + kt - 1)

        def ffn(which):
            b = U_OF[which]
            o0 = OUTS_FFN * which
            g0 = 4 * NCH * which
            d0 = 16 * NCH * which

            def take_up(i4, bnk, ob):
                dve.wait_ge(ff_out, ob)
                dve.wait_ge(gate_taken, i4 + bnk + 1)
                dve.tensor_tensor(sg[:, bnk, :], sg[:, bnk, :], bank[bnk][:, :], ALU.mult).then_inc(up_taken, 1)

            def a_lo(i4, bnk):
                dve.wait_ge(a_hi_done, i4 + bnk + 1)
                dve.tensor_tensor(aT_lo[:, bnk, :], sg[:, bnk, :], aT_hi[:, bnk, :].bitcast(F32),
                                  ALU.subtract).then_inc(a_lo_done, 1)

            def take_down(ob):
                for n in range(16):
                    dve.wait_ge(ff_out, ob + (n + 1))
                    xs = xT[:, n // 2, hs(n % 2)]
                    dve.scalar_tensor_tensor(xs, bank[4 + n % 3][:, :], 0.5, xs, ALU.mult, ALU.add
                                             ).then_inc(down_taken, 1)

            def ups(i4, ob, middle):
                take_up(i4, 0, ob + 1)
                take_up(i4, 1, ob + 2)
                a_lo(i4, 0)
                a_lo(i4, 1)
                middle()
                take_up(i4, 2, ob + 3)
                take_up(i4, 3, ob + 4)
                a_lo(i4, 2)
                a_lo(i4, 3)

            split_lo(b + 3, b + 4)
            split_lo(b + 4, b + 5)
            ups(g0, o0 + 4, lambda: split_lo(b + 5, b + 6))
            with dve.Fori(0, NCH - 1) as i:
                ob = i * 24 + (o0 + 8)
                i4 = i * 4 + (g0 + 4)
                for n in (6, 7, 8):
                    split_lo(b + n, i * 6 + (b + n + 1))
                take_down(ob + 4)
                for n in (9, 10):
                    split_lo(b + n, i * 6 + (b + n + 1))
                ups(i4, ob + 20, lambda: split_lo(b + 11, i * 6 + (b + 12)))
            if which == 0:
                split_lo(U_IN, U_IN + 1)
            take_down(o0 + OUTS_FFN - 16)

        for t in range(KD):
            dve.wait_ge(xt_done, 2 * t + 2)
            dve.tensor_copy(xT[:, 4:8, t * P:(t + 1) * P],
                            bank[(2 * t + 1) % 8][:, :].rearrange("p (k m) -> p k m", k=4)).then_inc(xt_dve, 1)

        chain = [0]

        def link(ins):
            chain[0] += 1
            ins.then_inc(prep_chain, 1)
            dve.wait_ge(prep_chain, chain[0])

        slot = [0]

        def new():
            slot[0] += 1
            assert slot[0] <= NPAR, slot
            return pw[:, slot[0] - 1, :]

        def tt(o, a, b_, op):
            link(dve.tensor_tensor(o, a, b_, op))

        def ts(o, a, s1, op1, s2=None, op2=None):
            if op2 is None:
                link(dve.tensor_scalar(o, a, s1, None, op1))
            else:
                link(dve.tensor_scalar(o, a, s1, s2, op1, op2))

        def stt(o, a, s1, b_, op1, op2):
            link(dve.scalar_tensor_tensor(o, a, s1, b_, op1, op2))

        t0, t1, t2 = new(), new(), new()
        nrm, red, pol, two = new(), new(), new(), new()

        def exp_parts(xv):
            ts(t0, xv, -150.0, ALU.max, 100.0, ALU.min)
            ts(nrm, t0, 1 / math.log(2.0), ALU.mult, MAGIC, ALU.add)
            ts(nrm, nrm, MAGIC, ALU.subtract)
            stt(red, nrm, -LN2_1, t0, ALU.mult, ALU.add)
            stt(red, nrm, -LN2_2, red, ALU.mult, ALU.add)
            ts(pol, red, 1 / 5040, ALU.mult)
            for c in (1 / 720, 1 / 120, 1 / 24, 1 / 6, 1 / 2, 1.0):
                stt(pol, pol, c, red, ALU.add, ALU.mult)
            ts(t1, nrm, -126.0, ALU.max, 127.0, ALU.min)
            tt(t2, nrm, t1, ALU.subtract)
            ts(pwi[:, 0, :], t1, 127.0, ALU.add)
            ts(pwi[:, 1, :], t2, 127.0, ALU.add)
            ts(pwi[:, :, :], pwi[:, :, :], 23, ALU.logical_shift_left)
            tt(two, pwi[:, 0, :].bitcast(F32), pwi[:, 1, :].bitcast(F32), ALU.mult)

        dve.wait_ge(params_loaded, 16 * 10)
        are, aim = par[:, 0, :], par[:, 1, :]
        dt, xr, th = new(), new(), new()
        exp_parts(par[:, 2, :])
        stt(dt, pol, 1.0, two, ALU.add, ALU.mult)
        tt(xr, are, dt, ALU.mult)
        tt(th, aim, dt, ALU.mult)
        exp_parts(xr)
        em1, mag = new(), new()
        tt(t0, two, pol, ALU.mult)
        stt(em1, two, -1.0, t0, ALU.add, ALU.add)
        tt(mag, two, t0, ALU.add)
        ts(nrm, th, 1 / (2 * math.pi), ALU.mult, MAGIC, ALU.add)
        ts(nrm, nrm, MAGIC, ALU.subtract)
        stt(red, nrm, -TWO_PI_1, th, ALU.mult, ALU.add)
        stt(red, nrm, -TWO_PI_2, red, ALU.mult, ALU.add)
        stt(red, nrm, -TWO_PI_3, red, ALU.mult, ALU.add)
        ts(red, red, 3.2, ALU.min, -3.2, ALU.max)
        q, q2, sn, cs = new(), new(), new(), new()
        ts(q, red, 0.25, ALU.mult)
        tt(q2, q, q, ALU.mult)
        ts(sn, q2, 1 / 362880, ALU.mult)
        for c in (-1 / 5040, 1 / 120, -1 / 6):
            stt(sn, sn, c, q2, ALU.add, ALU.mult)
        stt(sn, sn, 1.0, q, ALU.add, ALU.mult)
        ts(cs, q2, -1 / 3628800, ALU.mult)
        for c in (1 / 40320, -1 / 720, 1 / 24, -1 / 2):
            stt(cs, cs, c, q2, ALU.add, ALU.mult)
        ts(cs, cs, 1.0, ALU.add)
        s2_, c2_, sth, cth, cm1 = new(), new(), new(), new(), new()
        stt(s2_, sn, 2.0, cs, ALU.mult, ALU.mult)
        tt(t0, sn, sn, ALU.mult)
        ts(c2_, t0, -2.0, ALU.mult, 1.0, ALU.add)
        stt(sth, s2_, 2.0, c2_, ALU.mult, ALU.mult)
        tt(t0, s2_, s2_, ALU.mult)
        ts(cm1, t0, -2.0, ALU.mult)
        ts(cth, cm1, 1.0, ALU.add)
        er, ei, cr, ci, inv = new(), new(), new(), new(), new()
        tt(t0, em1, cth, ALU.mult)
        tt(er, t0, cm1, ALU.add)
        tt(ei, mag, sth, ALU.mult)
        lr = [lam[:, 0, k, :] for k in range(T + 1)]
        li = [lam[:, 1, k, :] for k in range(T + 1)]
        link(dve.memset(lr[0], 1.0))
        link(dve.memset(li[0], 0.0))
        tt(lr[1], mag, cth, ALU.mult)
        tt(li[1], mag, sth, ALU.mult)
        for k in range(1, T):
            tt(t0, lr[k], lr[1], ALU.mult)
            tt(t1, li[k], li[1], ALU.mult)
            tt(lr[k + 1], t0, t1, ALU.subtract)
            tt(t0, lr[k], li[1], ALU.mult)
            tt(t1, li[k], lr[1], ALU.mult)
            tt(li[k + 1], t0, t1, ALU.add)
        ts(lam[:, 2, :, :], lam[:, 1, :, :], -1.0, ALU.mult)
        tt(t0, are, are, ALU.mult)
        tt(t1, aim, aim, ALU.mult)
        tt(t0, t0, t1, ALU.add)
        link(dve.reciprocal(inv, t0))
        tt(t0, er, are, ALU.mult)
        tt(t1, ei, aim, ALU.mult)
        tt(t0, t0, t1, ALU.add)
        tt(cr, t0, inv, ALU.mult)
        tt(t0, ei, are, ALU.mult)
        tt(t1, er, aim, ALU.mult)
        tt(t0, t0, t1, ALU.subtract)
        tt(ci, t0, inv, ALU.mult)
        pr, pi = cth, sth
        for n in range(3):
            nr = rot8[:, 0, :] if n == 2 else new()
            ni = rot8[:, 1, :] if n == 2 else new()
            tt(t0, pr, pr, ALU.mult)
            tt(t1, pi, pi, ALU.mult)
            tt(nr, t0, t1, ALU.subtract)
            stt(ni, pr, 2.0, pi, ALU.mult, ALU.mult)
            pr, pi = nr, ni
        tt(t0, mag, mag, ALU.mult)
        tt(t0, t0, t0, ALU.mult)
        tt(dec8[:, :], t0, t0, ALU.mult)

        def wide(v, n=GH):
            return v.unsqueeze(2).to_broadcast([P, NJ, n])

        for o, (c0, c1, op) in enumerate(((cr, ci, ALU.subtract), (ci, cr, ALU.add))):
            tt(bc_tmp[:, 0, :, :], b_raw[:, 0, :, :], wide(c0), ALU.mult)
            tt(bc_tmp[:, 1, :, :], b_raw[:, 1, :, :], wide(c1), ALU.mult)
            tt(Bb[:, o, :, :], bc_tmp[:, 0, :, :], bc_tmp[:, 1, :, :], op)
        dve.wait_ge(consts_loaded, CONST_DMAS * 16)
        ts(bglu_h[:, :], bglu[:, :], 0.5, ALU.mult)
        link(dve.tensor_scalar(gains[:, 20:24], gains[:, 20:24], 0.5, None, ALU.mult))
        assert chain[0] == PREP_STEPS, chain

        for u in range(WS):
            split_lo(u, u + 1)
            if u == 0:
                norm_split(N_FF1, xT, 0)
        ffn(0)
        split_lo(U_IN + 1, U_IN + 2)
        split_lo(U_IN + 2, U_IN + 3)
        norm_split(N_MIX, xT, 0)
        for n in range(1, N_IN):
            split_lo(U_IN + n + 2, U_IN + n + 3)
        split_lo(U_OUT, U_OUT + 1)

        dve.wait_ge(u_stored, 64)
        for b in range(4):
            dve.wait_ge(v_ready, b + 1)
            dve.tensor_copy(vwin[:, 4 * b:4 * b + 4, :], bank[b][:, :].rearrange("p (n m) -> p n m", n=4)
                            ).then_inc(v_taken, 1)
        dve.tensor_tensor(dgl[:, :, :], ident[0:GH, 0:GH].unsqueeze(1).to_broadcast([GH, NG, GH]),
                          dsk[:, :].unsqueeze(2).to_broadcast([GH, NG, GH]), ALU.mult).then_inc(diag_chain, 1)
        dve.wait_ge(diag_chain, 1)
        for b in range(8):
            dve.wait_ge(k_ready, b + 1)
            dve.wait_ge(k_act, b + 1)
            j0, g2 = 4 * (b // 2), b % 2
            dst = kst[:, :, :].rearrange("p (j g) m -> p g j m", g=2)[:, g2, j0:j0 + 4, 0:GH]
            dg = dgl[:, :, :].rearrange("p (j g) m -> p g j m", g=2)[:, g2, j0:j0 + 4, :]
            dve.tensor_tensor(dst, bank[4 + b % 4][0:GH, :].rearrange("p (j m) -> p j m", j=4)[:, :, 0:GH],
                              dg, ALU.add).then_inc(k_taken, 1)

        sc = [0]

        def step(ins):
            sc[0] += 1
            ins.then_inc(state_chain, 1)

        def steps_done():
            dve.wait_ge(state_chain, sc[0])

        dve.wait_ge(cs_loaded, 16)
        dve.wait_ge(k_stored, 16)
        for b in range(4):
            js = slice(4 * b, 4 * b + 4)
            re, im = bank[2 * b][:, :], bank[2 * b + 1][:, :]
            c_ = csn[:, 0, js, :].rearrange("p j c -> p (j c)")
            s_ = csn[:, 1, js, :].rearrange("p j c -> p (j c)")
            trb = tr[:, js, :].rearrange("p j c -> p (j c)")
            tib = ti[:, js, :].rearrange("p j c -> p (j c)")
            r0, r1, r2 = (rtm[:, i, :] for i in range(3))
            dve.wait_ge(inj_ready, b + 1)
            if b:
                steps_done()
            step(dve.tensor_tensor(r0, c_, re, ALU.mult))
            step(dve.tensor_tensor(r1, s_, im, ALU.mult))
            steps_done()
            step(dve.tensor_tensor(trb, r0, r1, ALU.add))
            steps_done()
            step(dve.tensor_tensor(r0, c_, im, ALU.mult))
            step(dve.tensor_tensor(r1, s_, re, ALU.mult))
            steps_done()
            step(dve.tensor_tensor(tib, r0, r1, ALU.subtract))
            steps_done()
            for j in range(4 * b, 4 * b + 4):
                for t_ in (tr, ti):
                    step(dve.tensor_tensor_scan(t_[:, j, :], dec8[:, j:j + 1].to_broadcast([P, NC]),
                                                t_[:, j, :], 0.0, ALU.mult, ALU.add))
            steps_done()
            step(dve.tensor_tensor(r0, s_, trb, ALU.mult))
            step(dve.tensor_tensor(r1, c_, tib, ALU.mult))
            step(dve.tensor_tensor(r2, s_, tib, ALU.mult))
            steps_done()
            step(dve.tensor_tensor(r0, r0, r1, ALU.add))
            steps_done()
            step(dve.tensor_tensor(r1, c_, trb, ALU.mult))
            steps_done()

            def sh(v):
                return v.rearrange("p (j c) -> p j c", j=4)[:, :, 0:NC - 1]

            step(dve.tensor_tensor(tr[:, js, 1:], sh(r1), sh(r2), ALU.subtract))
            step(dve.tensor_copy(ti[:, js, 1:], sh(r0)))
            steps_done()
            step(dve.memset(tr[:, js, 0:1], 0.0))
            step(dve.memset(ti[:, js, 0:1], 0.0))
            steps_done()
            dve.memset(ssum[:, 0:1], 0.0).then_inc(state_done, 1)

        dve.wait_ge(bias_loaded, 16)
        ac = [0]

        def astep(ins):
            ac[0] += 1
            ins.then_inc(att_chain, 1)
            dve.wait_ge(att_chain, ac[0])

        sco8 = sco[:, :, :, :, :].rearrange("p v n a k -> p (v n a) k")
        sink8 = sinkt[:, :, :, :].rearrange("p v n a -> p (v n a)")
        for m in range(8):
            for kv in range(NKV):
                dve.wait_ge(s_ready, 2 * m + kv + 1)
                if m and kv == 0:
                    dve.wait_ge(pt_ready, 2 * m)
                for nn in range(2):
                    dve.scalar_tensor_tensor(sco[:, kv, nn, :, :].rearrange("p a k -> p (a k)"),
                                             bank[2 * (m % 2) + kv][:, nn * 256:(nn + 1) * 256], HD ** -0.5,
                                             biast[:, kv, :], ALU.mult, ALU.add).then_inc(s_biased, 1)
            dve.wait_ge(s_biased, 4 * m + 4)
            if m == 0:
                astep(dve.memset(sco[:, :, 0, :, 0:CHUNK], -1e30))
            astep(dve.reduce_max(mx[:, :], sco8, AX.X))
            astep(dve.tensor_tensor(mx[:, :], mx[:, :], sink8, ALU.max))
            astep(dve.tensor_scalar(nm[:, :], mx[:, :], -1.0, None, ALU.mult))
            dve.tensor_tensor(esk[:, :], sink8, mx[:, :], ALU.subtract).then_inc(max_done, 1)
            dve.wait_ge(exp_done, m + 1)
            astep(dve.tensor_tensor(ssum[:, :], ssum[:, :], esk[:, :], ALU.add))
            astep(dve.reciprocal(rden[:, :], ssum[:, :]))
            dve.tensor_tensor(sco8, sco8, rden[:, :].unsqueeze(2).to_broadcast([P, 8, P]), ALU.mult
                              ).then_inc(p_done, 1)

        for h in range(2):
            for k in range(4):
                dve.wait_ge(z_hi, 4 * h + k + 1)
                dve.tensor_tensor(hT_lo[:, 4 + k, hs(h)], zT[:, k, hs(h)], hT_hi[:, 4 + k, hs(h)].bitcast(F32),
                                  ALU.subtract).then_inc(z_lo, 1)
        for o in range(8):
            zs = zT[:, o // 2, hs(o % 2)]
            dve.wait_ge(glu_tanh, o + 1)
            dve.scalar_tensor_tensor(zs, gth[:, o % 2, :], 1.0, zs, ALU.add, ALU.mult).then_inc(glu_done, 1)
        norm_split(N_ATT, qT, 0)
        norm_split(N_SSM, zT, 4, True)
        split_lo(U_OUT + 1, U_OUT + 2)
        split_lo(U_OUT + 2, U_OUT + 3)
        for n in range(N_OUT):
            if n:
                split_lo(U_OUT + n + 2, U_OUT + n + 3)
            for h in range(2):
                m = 2 * n + h
                dve.wait_ge(mix_out, m + 1)
                xs = xT[:, n, hs(h)]
                dve.tensor_tensor(xs, xs, bank[m % 4][:, :], ALU.add).then_inc(mix_taken, 1)
        split_lo(U_FF2 + 2, U_FF2 + 3)
        norm_split(N_FF2, xT, 0)
        ffn(1)
        rstd = scratch(N_END)[0]
        for h in range(2):
            norm_rstd(N_END, h)
            for k in range(KD):
                xs = xT[:, k, hs(h)]
                g = gains[:, G_COL[N_END] + k:G_COL[N_END] + k + 1]
                dve.scalar_tensor_tensor(xs, xs, g, rstd[:, hs(h)], ALU.mult, ALU.mult).then_inc(fin_tmp, 1)
        for o in range(1, 16, 2):
            t = o // 2
            dve.wait_ge(fin_ready, o + 1)
            dve.wait_ge(fin_taken, o)
            if t >= 2:
                dve.wait_ge(out_stored[t % 2], 16 * (t // 2))
            dve.tensor_copy(osb[:, t % 2, HALF:], bank[o % 4][:, :]).then_inc(fin_taken, 1)

    @block.gpsimd
    def _(pool):
        def add_squares(norm, half_major):
            kt = NORM_TILES[norm]
            c0 = squares_before(norm)
            for n in range(2 * kt):
                h = n // kt if half_major else n % 2
                first = n % kt == 0 if half_major else n < 2
                pool.wait_ge(sq_done, c0 + n + 1)
                if first and norm:
                    pool.wait_ge(sum_ready, 2 * norm)
                s = sqt[:, (c0 + n) % 2, :]
                if first:
                    pool.tensor_copy(ssq[:, hs(h)], s).then_inc(ssq_done, 1)
                else:
                    pool.wait_ge(ssq_done, c0 + n - (0 if half_major else 1))
                    pool.tensor_tensor(ssq[:, hs(h)], ssq[:, hs(h)], s, ALU.add).then_inc(ssq_done, 1)

        pool.memset(ones[:, :], 1.0)
        pool.memset(zero[:, :], 0.0)
        pool.memset(unit[:, 0, :, :], 1.0)
        pool.memset(unit[:, 1, :, :], 0.0)
        pool.memset(eps_t[:, :], EPS).then_inc(consts_set, 1)
        pool.wait_ge(consts_set, 1)
        zv = k_d.rearrange("(n g) h c -> n (g h) c", g=8)
        for n in range(4):
            pool.dma_start(zv[n][:, 0:(T - 1) * GH], zero[:, :]).then_inc(zero_stored, 16)
        add_squares(N_FF1, True)

        pc = [0]

        def link(ins):
            pc[0] += 1
            ins.then_inc(pool_chain, 1)
            pool.wait_ge(pool_chain, pc[0])

        def over_h(v, n):
            return v.unsqueeze(2).to_broadcast([P, n, GH])

        pool.wait_ge(prep_chain, PREP_STEPS)
        pool.wait_ge(ct_taken, 4)
        pt = [ptmp[:, i, :].rearrange("p (j h) -> p j h", h=GH) for i in range(2)]
        for k in range(T + 1):
            for o, (n0, n1) in enumerate(((0, 1), (2, 0))):
                link(pool.tensor_tensor(pt[0], CT[:, 0, :, :], over_h(lam[:, n0, k, :], NJ), ALU.mult))
                link(pool.tensor_tensor(pt[1], CT[:, 1, :, :], over_h(lam[:, n1, k, :], NJ), ALU.mult))
                link(pool.tensor_tensor(CL[:, o, :, k * GH:(k + 1) * GH], pt[0], pt[1], ALU.subtract))
        base_links = pc[0]

        cB = cur[:, :, :, 0:GH]
        cL = cur[:, :, :, GH:GH + T + 1]
        cR = cur[:, :, :, GH + T + 1]
        per = LINKS_PER_BATCH
        with pool.Fori(0, NJ // 4) as i:
            nl = [0]

            def ilink(ins):
                nl[0] += 1
                ins.then_inc(pool_chain, 1)
                pool.wait_ge(pool_chain, i * per + (base_links + nl[0]))

            def passed():
                pool.tensor_tensor(mark[:, :], unit[:, 0, 0, :], unit[:, 0, 0, :], ALU.mult)

            for ri in range(2):
                ilink(pool.tensor_copy(cB[:, ri], Bb[:, ri, bass.ds(i * 4, 4), :]))
                ilink(pool.tensor_copy(cL[:, ri].rearrange("p j k -> p k j"),
                                       lam[:, ri, :, bass.ds(i * 4, 4)]))
                ilink(pool.tensor_copy(cR[:, ri], rot8[:, ri, bass.ds(i * 4, 4)]))
            q = [ptmp[:, n, 0:4 * GH].rearrange("p (j h) -> p j h", h=GH) for n in range(2)]
            for t in range(T):
                e = T - 1 - t
                for o, (n0, n1, op) in enumerate(((0, 1, ALU.subtract), (1, 0, ALU.add))):
                    ilink(pool.tensor_tensor(q[0], cB[:, 0], over_h(cL[:, n0, :, e], 4), ALU.mult))
                    ilink(pool.tensor_tensor(q[1], cB[:, 1], over_h(cL[:, n1, :, e], 4), ALU.mult))
                    ilink(pool.tensor_tensor(EBb[:, o, :, t * GH:(t + 1) * GH], q[0], q[1], op))
            passed()
            pool.dma_start(eb_d[:, :, bass.ds(i * 4, 4), :], EBb[:, :, :, :]).then_inc(eb_stored, 16)
            pool.wait_ge(eb_stored, i * 32 + 16)
            ilink(pool.tensor_tensor(EBb[:, :, :, 0:1], unit[:, :, :, :], unit[:, :, :, :], ALU.mult))
            n = 1
            while n < NC:
                v = [ptmp[:, m, 0:4 * n].rearrange("p (j c) -> p j c", j=4) for m in range(2)]
                w = [cR[:, m, :].unsqueeze(2).to_broadcast([P, 4, n]) for m in range(2)]
                R = [EBb[:, m, :, 0:n] for m in range(2)]
                for o, (n0, n1, op) in enumerate(((0, 1, ALU.subtract), (1, 0, ALU.add))):
                    ilink(pool.tensor_tensor(v[0], R[0], w[n0], ALU.mult))
                    ilink(pool.tensor_tensor(v[1], R[1], w[n1], ALU.mult))
                    ilink(pool.tensor_tensor(EBb[:, o, :, n:2 * n], v[0], v[1], op))
                if 2 * n < NC:
                    a, b_ = ptmp[:, 0, 0:4], ptmp[:, 1, 0:4]
                    c_ = ptmp[:, 0, 4:8]
                    ilink(pool.tensor_tensor(a, cR[:, 0], cR[:, 0], ALU.mult))
                    ilink(pool.tensor_tensor(b_, cR[:, 1], cR[:, 1], ALU.mult))
                    ilink(pool.tensor_tensor(c_, cR[:, 0], cR[:, 1], ALU.mult))
                    ilink(pool.tensor_tensor(cR[:, 0], a, b_, ALU.subtract))
                    ilink(pool.tensor_tensor(cR[:, 1], c_, c_, ALU.add))
                n *= 2
            passed()
            pool.dma_start(cs_d[:, :, bass.ds(i * 4, 4), :], EBb[:, :, :, :]).then_inc(eb_stored, 16)
            pool.wait_ge(eb_stored, i * 32 + 32)
            assert nl[0] == per, nl

        add_squares(N_MIX, False)
        pool.wait_ge(h_lo, split_before(N_ATT))
        pool.memset(kTp[:, 0:CHUNK], 0.0)
        pool.memset(vTp[:, 0:CHUNK], 0.0).then_inc(pads_set, 1)
        add_squares(N_ATT, True)
        add_squares(N_SSM, True)
        add_squares(N_FF2, False)
        add_squares(N_END, False)

    ctx.close()


_INS = ["x", "ff1_norm", "ff1_w_gate", "ff1_w_up", "ff1_w_down", "mix_norm", "w_in", "sink", "a_re", "a_im",
        "b_re", "b_im", "c_re", "c_im", "d_skip", "log_dt", "w_glu", "b_glu", "attn_out_norm",
        "ssm_out_norm", "w_out", "ff2_norm", "ff2_w_gate", "ff2_w_up", "ff2_w_down", "final_norm"]


def alibi_bias():
    q = np.arange(CHUNK)[:, None]
    key = np.arange(2 * CHUNK)[None, :] - CHUNK
    dist = np.abs(q - key).astype(np.float32)
    out = np.zeros((2, CHUNK, NKV, 2, 2 * CHUNK), np.float32)
    for g2 in range(2):
        for kv in range(NKV):
            for a in range(2):
                head = kv * GQ + 2 * a + g2
                out[g2, :, kv, a, :] = -np.float32(2.0 ** -(head + 1)) * dist
    return out.reshape(P, NKV, 2 * 2 * CHUNK)


def kernel(**inputs):
    import numpy as _np
    import concourse.bacc as _bacc
    from concourse import mybir as _mybir
    from concourse.bass_utils import run_bass_kernel_spmd as _run

    nc = _bacc.Bacc("TRN2", target_bir_lowering=False, num_devices=1)
    arrays, args = {}, []
    host = [(name, _np.ascontiguousarray(inputs[name])) for name in _INS]
    host += [("ident", _np.eye(P, dtype=_np.float32)), ("bias", alibi_bias())]
    for name, a in host:
        arrays[f"in_{name}_dram"] = a
        args.append(nc.dram_tensor(f"in_{name}_dram", a.shape, _mybir.dt.from_np(a.dtype),
                                   kind="ExternalInput").ap())
    args.append(nc.dram_tensor("out_0_dram", (1, L, D), _mybir.dt.float32, kind="ExternalOutput").ap())
    block_kernel(nc, *args)
    r = _run(nc, [arrays], core_ids=[0])
    return r.results[0]["out_0_dram"]
```

```python
import math
from contextlib import ExitStack

import numpy as np
import concourse.bass as bass
from concourse import mybir

F32 = mybir.dt.float32
F32R = mybir.dt.float32r
I32 = mybir.dt.int32
ALU = mybir.AluOpType
ACT = mybir.ActivationFunctionType
AX = mybir.AxisListType

P = 128
D = 1024
L = 1024
F = 2816
KD = D // P
HALF = 512
NCH = F // P // 2
HD = 64
NKV = 2
GQ = 4
CHUNK = 64
DA = 512
DS = 512
NG = 32
GH = 16
NS = 64
NJ = NG // 2
T = P // GH
NC = L // T
EPS = 1e-6

WS = 3
RS = 2

UNITS_FFN = 6 * NCH
U_FF1 = 0
U_IN = U_FF1 + UNITS_FFN
N_IN = 10
U_GLU = U_IN + N_IN
N_GLU = 2
U_OUT = U_GLU + N_GLU
N_OUT = 2 * KD
U_FF2 = U_OUT + N_OUT
N_UNITS = U_FF2 + UNITS_FFN

UNIT_DMAS = [1] * N_UNITS
for _u in range(U_IN + 6, U_IN + N_IN):
    UNIT_DMAS[_u] = 2
for _u in range(U_OUT, U_OUT + N_OUT):
    UNIT_DMAS[_u] = 3


def loads_until(unit):
    return 16 * sum(UNIT_DMAS[u] for u in range(unit % RS, unit + 1, RS))


NORM_TILES = [KD, KD, DA // P, DS // P, KD, KD]
N_FF1, N_MIX, N_ATT, N_SSM, N_FF2, N_END = range(6)


def squares_before(norm):
    return sum(2 * t for t in NORM_TILES[:norm])


NORMED = [N_FF1, N_MIX, N_ATT, N_SSM, N_FF2]


def norm_order(norm):
    kt = NORM_TILES[norm]
    sq = [("S", i) for i in range(2 * kt)]
    ap = [("A", i) for i in range(2 * kt)]
    if norm == N_FF1:
        return sq[:kt] + [("R", 0)] + ap[:kt] + sq[kt:] + [("R", 1)] + ap[kt:]
    if norm == N_END:
        return sq[:10] + [("R", 0)] + sq[10:] + [("R", 1)]
    out = sq[:10] + [("R", 0)]
    for i in range(6):
        out += [ap[i], sq[10 + i]]
    return out + ap[6:8] + [("R", 1)] + ap[8:]


def steps(text):
    return [(s[0], int(s[1])) for s in text.split()]


MIXER_PE = steps("S0 K0 S1 K1 K2 S2 T0 E0 E1 E2 E3 K3 E4 V0 K4 K5 E5 E6 S3 T1 E7 K6 K7 I0 S4 T2 V1 I1 S5 T3 V2 I2 "
    "V3 T4 Y0 S6 I3 S7 V4 Y1 T5 Y2 Y3 V5 T6 V6 T7 V7")
MIXER_ACT = steps("k0 X0 k1 k2 X1 C0 e0 e1 e2 e3 e4 k3 k4 k5 X2 O0 e5 e6 C1 e7 k6 X3 k7 O1 C2 X4 O2 C3 y0 X5 O3 C4 "
    "X6 O4 g0 y1 C5 y2 X7 g1 y3 O5 C6 g2 O6 C7 g3 O7")
MIXER_DVE = steps("A0 A1 B0 d0 d1 d2 B1 d3 A2 d4 d5 A3 d6 B2 B3 d7 R0 A4 R1 B4 R2 A5 A6 R3 B5 A7 z0 B6 z1 B7 z2 z3")
ROUND = [(step, i) for step in MIXER_PE if step[0] in "KEIY" for i in range(1 if step[0] in "KE" else 2)]


def round_bank(kind, b, i=0):
    return 5 + ROUND.index(((kind, b), i)) % 3


GATED = ([("S", N_ATT, i) for i in range(8)] + [("G", 0), ("G", 1), ("R", N_ATT, 0), ("G", 2)]
         + [("A", N_ATT, i) for i in range(4)] + [("G", 3), ("W", 1), ("R", N_ATT, 1), ("G", 4)]
         + [("A", N_ATT, i) for i in range(4, 8)] + [("G", 5), ("S", N_SSM, 0), ("S", N_SSM, 1), ("S", N_SSM, 2)]
         + [("G", 6), ("S", N_SSM, 3), ("G", 7), ("S", N_SSM, 4), ("S", N_SSM, 5), ("W", 2), ("R", N_SSM, 0)]
         + [("S", N_SSM, 6), ("S", N_SSM, 7)] + [("A", N_SSM, i) for i in range(4)] + [("R", N_SSM, 1)]
         + [("A", N_SSM, i) for i in range(4, 8)])

X_BANK = [0, 1, 2, 3, 4, 5, 6, 7] + [1, 2, 3, 4, 5, 6, 1, 2]

IN_ORDER = [(0, 0), (1, 0), (2, 0), (0, 1), (1, 1), (2, 1)] + [(n, h) for n in range(3, N_IN) for h in range(2)]
END_IN = [IN_ORDER.index((n, 1)) + 1 for n in range(N_IN)]
FIRST = [("G", 0, 0), ("G", 1, 0), ("U", 0, 0), ("G", 0, 1), ("G", 1, 1), ("U", 0, 1), ("U", 1, 0), ("U", 1, 1)]
FIRST_GATES = {0: 1, 2: 2, 1: 3, 3: 4}


def split_before(norm):
    return sum(2 * NORM_TILES[n] for n in NORMED if n < norm)


TWO_PI_1 = 6.28125
TWO_PI_2 = 0.00193500518798828125
TWO_PI_3 = 2 * math.pi - TWO_PI_1 - TWO_PI_2
LN2_1 = 0.693359375
LN2_2 = math.log(2.0) - LN2_1
MAGIC = 1.5 * 2 ** 23

LINKS_PER_BATCH = 127
NORM_SCALE = [1 / D, 1 / D, 1 / DA, 0.25 / DS, 1 / D, 1 / D]
CONST_DMAS = 5 + 2 + 1 + 8 + 1


def src_of(tile, permuted):
    return tile.rearrange("p (t c) -> p t c", c=NC) if permuted else tile


def by_chunk(tile):
    return tile.rearrange("p (n q) -> p n q", q=CHUNK)


def att_tile(q, g, h):
    return q[:, h * 8:(h + 1) * 8, g, :]


def dst_of(tensor, k, h, permuted):
    if permuted:
        return tensor[:, k, :].rearrange("p (c t) -> p t c", t=T)[:, 4 * h:4 * h + 4, :]
    return tensor[:, k, h * HALF:(h + 1) * HALF]


def block_kernel(nc, x, ff1_norm, ff1_w_gate, ff1_w_up, ff1_w_down, mix_norm, w_in, sink, a_re, a_im,
                 b_re, b_im, c_re, c_im, d_skip, log_dt, w_glu, b_glu, attn_out_norm, ssm_out_norm,
                 w_out, ff2_norm, ff2_w_gate, ff2_w_up, ff2_w_down, final_norm, ident_c, bias_c, out):
    ctx = ExitStack()

    ctx.enter_context(nc.allow_non_contiguous_dma(reason="vectors of a few KB"))

    base = (nc.sbuf_base + 31) // 32 * 32
    KB = 1024

    def at(name, off, shape, dt=F32):
        return nc.alloc_sbuf_tensor_at(name, shape, dt, offset=base + off)

    a_x, a_h, a_w = 0, 32 * KB, 96 * KB
    a_a = a_w + 32 * KB
    a_t = a_a + 24 * KB
    a_s = a_t + 34 * KB

    xT = at("xT", a_x, [P, KD, L])
    hT_hi = at("hT_hi", a_h, [P, KD, L], F32R)
    hT_lo = at("hT_lo", a_h + 32 * KB, [P, KD, L], F32R)
    x_in = [at("x_in0", a_h + 32 * KB, [P, 4, D]), at("x_in1", a_w + 32 * KB, [P, 4, D])]
    w_hi = [at(f"w_hi{s}", a_w + 4 * KB * s, [P, 1024], F32R) for s in range(WS)]
    w_lo = [at(f"w_lo{s}", a_w + 12 * KB + 4 * KB * s, [P, 1024], F32R) for s in range(WS)]
    raw = [at(f"raw{s}", a_w + 24 * KB + 4 * KB * s, [P, 1024]) for s in range(RS)]
    aT_hi = at("aT_hi", a_a, [P, 4, HALF], F32R)
    aT_lo = at("aT_lo", a_a + 8 * KB, [P, 4, HALF], F32R)
    sg = at("sg", a_a + 16 * KB, [P, 4, HALF])
    htmps = [at("htmp0", a_t + 18 * KB, [P, 3, HALF]), at("htmp1", a_t, [P, 3, HALF])]
    dgts = [at("dgt0", a_t + 24 * KB, [P, 4, P]), at("dgt1", a_t + 6 * KB, [P, 4, P])]
    gend = at("gend", a_t + 8 * KB, [P, D])
    qT = at("qT", a_a, [P, L // CHUNK, GQ, CHUNK])
    kTp = at("kTp", a_a + 16 * KB, [P, CHUNK + L])
    CL = at("CL", a_t, [P, 2, NJ, (T + 1) * GH])
    Et = at("Et", a_t + 18 * KB, [P, NJ, 2, P])
    vTp = at("vTp", a_t + 18 * KB, [P, CHUNK + L])
    yT = at("yT", a_t + 18 * KB, [P, 4, L])
    u8 = at("u8", a_h, [P, NG, NC])
    Mt = at("Mt", a_h + 16 * KB, [P, NG, P])
    tr = at("tr", a_h + 32 * KB, [P, NJ, NC])
    ti = at("ti", a_h + 40 * KB, [P, NJ, NC])
    kst = at("kst", a_h + 16 * KB, [GH, NG, P])
    csn = at("csn", a_h + 48 * KB, [P, 2, NJ, NC])
    ebs = at("ebs", a_h + 32 * KB, [P, 2, NJ, P])
    off = [a_s]

    def small(name, shape, dt=F32):
        t = at(name, off[0], shape, dt)
        n = 4
        for s in shape[1:]:
            n *= s
        off[0] += (n + 31) // 32 * 32
        return t

    ident = small("ident", [P, P])
    ones = small("ones", [P, P])
    gains = small("gains", [P, 40])
    G_COL = {N_FF1: 0, N_MIX: 8, N_ATT: 16, N_SSM: 20, N_FF2: 24, N_END: 32}
    eps_t = small("eps_t", [P, 1])
    bglu = small("bglu", [P, 4])
    bglu_h = small("bglu_h", [P, 4])
    sinkt = small("sinkt", [P, 2, 2, 2])
    par = small("par", [P, 3, NJ])
    NPAR = 40
    pw = at("pw", a_t + 26 * KB, [P, NPAR, NJ])
    pwi = at("pwi", a_t + 29 * KB, [P, 2, NJ], I32)
    ivt = small("ivt", [P, 4, NJ])
    lam = small("lam", [P, 3, T + 1, NJ])
    rot8 = small("rot8", [P, 2, NJ])
    dec8 = small("dec8", [P, NJ])
    dsk = small("dsk", [GH, NG])
    zero = small("zero", [P, (T - 1) * GH])
    unit = small("unit", [P, 2, 4, 1])
    mark = small("mark", [P, 1])
    Bb = small("Bb", [P, 2, NJ, GH])
    std4 = small("std4", [P, 4])
    nv4 = small("nv4", [P, 4])
    nt4 = small("nt4", [P, 2, 4])
    rms4 = small("rms4", [P, 2, 4])
    mx = small("mx", [P, 8])
    nm = small("nm", [P, 2, 8])
    esk = small("esk", [P, 2, 8])
    ssum = small("ssum", [P, 2, 8])
    rden = small("rden", [P, 8])
    a_v = off[0]
    b_raw = at("b_raw", a_v, [P, 2, NJ, GH])
    c_in = at("c_in", a_t + 30 * KB, [P, 2, 4, 2, NS])
    CT = at("CT", a_v + 6 * KB, [P, 2, NJ, GH])
    ptmp = at("ptmp", a_v + 8 * KB, [P, 2, 256])
    EBb = at("EBb", a_v + 2 * KB, [P, 2, 4, P])
    ssq = at("ssq", a_v + 10 * KB, [P, L])
    sqt = at("sqt", a_v + 2 * KB, [P, 2, HALF])
    cur = at("cur", a_v, [P, 2, 4, GH + T + 1 + 1])
    bc_tmp = at("bc_tmp", a_v + 8 * KB, [P, 2, NJ, GH])
    gth = at("gth", a_v + 6 * KB, [P, 2, HALF])
    ust = [at(f"ust{i}", a_a + 4 * KB * i, [P, T, NC]) for i in range(3)]
    dgl = at("dgl", a_v + 12 * KB, [GH, NG, GH])
    vwin = at("vwin", a_v, [P, 2 * 8, P])
    biast = at("biast", a_a + 20 * KB + 512, [P, NKV, 256])
    sco = [at(f"sco{i}", a_w + 12 * KB * i, [P, 2, 2, 2, P]) for i in range(2)]
    pts = at("pts", a_w + 24 * KB, [P, 2, 2, 2, P])
    rtm = at("rtm", a_v + 8 * KB, [P, 2, HALF])
    btm = [at(f"btm{i}", a_w + o, [P, HALF]) for i, o in enumerate((8 * KB, 10 * KB, 20 * KB))]
    osb = at("osb", a_h, [P, 2, D])
    assert base + a_v + 14 * KB <= nc.sbuf_usable_end, (base + a_v + 14 * KB, nc.sbuf_usable_end)

    def htmp(norm, c):
        return htmps[norm >= N_ATT][:, c % 3, :]

    def dgt(norm):
        return dgts[norm >= N_ATT]

    bank = [ctx.enter_context(nc.psum_tensor(f"bank{i}", [P, HALF], F32)) for i in range(8)]

    u_d = nc.dram_tensor("u_scratch", (DS, T, NC), F32, kind="Internal").ap()
    y_d = nc.dram_tensor("y_scratch", (DS, T, NC), F32, kind="Internal").ap()
    eb_d = nc.dram_tensor("eb_scratch", (P, 2, NJ, P), F32, kind="Internal").ap()
    cs_d = nc.dram_tensor("cs_scratch", (P, 2, NJ, NC), F32, kind="Internal").ap()
    k_d = nc.dram_tensor("k_scratch", (NG, GH, (2 * T - 1) * GH), F32, kind="Internal").ap()

    def sem(name):
        return ctx.enter_context(nc.semaphore(name))

    x_loaded = [sem(f"x_loaded{h}") for h in range(2)]
    consts_loaded = sem("consts_loaded")
    ident_loaded = sem("ident_loaded")
    params_loaded = sem("params_loaded")
    c_loaded = sem("c_loaded")
    consts_set = sem("consts_set")
    raw_loaded = [sem(f"raw_loaded{s}") for s in range(RS)]
    w_hi_done = sem("w_hi_done")
    w_lo_done = sem("w_lo_done")
    xt_done = sem("xt_done")
    xt_act = sem("xt_act")
    xt_dve = sem("xt_dve")
    sq_done = sem("sq_done")
    ssq_done = sem("ssq_done")
    sum_ready = sem("sum_ready")
    std_done = sem("std_done")
    rms_done = sem("rms_done")
    diag_done = sem("diag_done")
    rb_ready = sem("rb_ready")
    gend_loaded = sem("gend_loaded")
    h_tmp = sem("h_tmp")
    h_hi = sem("h_hi")
    h_lo = sem("h_lo")
    ff_out = sem("ff_out")
    gate_taken = sem("gate_taken")
    up_taken = sem("up_taken")
    a_hi_done = sem("a_hi_done")
    a_lo_done = sem("a_lo_done")
    down_taken = sem("down_taken")
    ct_ready = sem("ct_ready")
    ct_taken = sem("ct_taken")
    prep_chain = sem("prep_chain")
    newton = sem("newton")
    inv_done = sem("inv_done")
    gains_set = sem("gains_set")
    pads_set = sem("pads_set")
    pool_chain = sem("pool_chain")
    eb_stored = sem("eb_stored")
    zero_stored = sem("zero_stored")
    proj_out = sem("proj_out")
    proj_taken = sem("proj_taken")
    u_stored = sem("u_stored")
    u8_loaded = sem("u8_loaded")
    eb_loaded = sem("eb_loaded")
    cs_loaded = sem("cs_loaded")
    bias_loaded = sem("bias_loaded")
    v_ready = sem("v_ready")
    v_taken = sem("v_taken")
    e_ready = sem("e_ready")
    e_taken = sem("e_taken")
    k_ready = sem("k_ready")
    k_taken = sem("k_taken")
    k_act = sem("k_act")
    diag_chain = sem("diag_chain")
    k_stored = sem("k_stored")
    m_loaded = sem("m_loaded")
    inj_ready = sem("inj_ready")
    inj_taken = sem("inj_taken")
    state_chain = sem("state_chain")
    scanned = sem("scanned")
    back_chain = sem("back_chain")
    state_done = sem("state_done")
    y_ready = sem("y_ready")
    y_taken = sem("y_taken")
    y_stored = sem("y_stored")
    yt_loaded = sem("yt_loaded")
    s_ready = sem("s_ready")
    s_biased = sem("s_biased")
    att_chain = sem("att_chain")
    max_done = sem("max_done")
    exp_done = sem("exp_done")
    p_done = sem("p_done")
    pt_ready = sem("pt_ready")
    pt_taken = sem("pt_taken")
    o_ready = sem("o_ready")
    o_taken = sem("o_taken")
    z_done = sem("z_done")
    z_hi = sem("z_hi")
    z_lo = sem("z_lo")
    glu_out = sem("glu_out")
    glu_tanh = sem("glu_tanh")
    glu_done = sem("glu_done")
    mix_out = sem("mix_out")
    mix_taken = sem("mix_taken")
    fin_ready = sem("fin_ready")
    fin_taken = sem("fin_taken")
    out_stored = [sem(f"out_stored{i}") for i in range(2)]

    FF = {0: (ff1_w_gate, ff1_w_up, ff1_w_down), 1: (ff2_w_gate, ff2_w_up, ff2_w_down)}
    U_OF = (U_FF1, U_FF2)
    OUTS_FFN = 24 * NCH

    def wk(t, k):
        return t[:, k * P:(k + 1) * P]

    def hs(h):
        return slice(h * HALF, (h + 1) * HALF)

    block = ctx.enter_context(nc.Block())

    @block.sync
    def _(sp):
        def load_unit(u, src, dst=None, wait=None):
            if wait is not None:
                sp.wait_ge(w_lo_done, wait)
            sp.dma_start(raw[u % RS][:, :] if dst is None else dst, src).then_inc(raw_loaded[u % RS], 16)

        def cols(w, f):
            return w.rearrange("(k p) f -> p k f", p=P)[:, :, f]

        def as3(u):
            return raw[u % RS][:, :].rearrange("p (k m) -> p k m", k=8)

        def gate_or_up(u, w, f, wait):
            load_unit(u, cols(w, bass.ds(f * P, P)), as3(u), wait)

        def down(u, w, f, wait):
            load_unit(u, w[bass.ds(f * P, P), :], None, wait)

        def ffn_loads(which, between=lambda: None):
            wg, wu, wd = (w[0] for w in FF[which])
            b = U_OF[which]
            for n, (w, f) in enumerate(((wg, 0), (wg, 1), (wu, 0), (wu, 1))):
                gate_or_up(b + n, w, f, b + n - RS + 1 if b + n >= RS else None)
                if n == 0:
                    between()
            with sp.Fori(0, NCH - 1) as i:
                b0 = b + 4
                for n, (w, f) in enumerate(((wg, 2), (wg, 3), (wd, 0), (wd, 1), (wu, 2), (wu, 3))):
                    wait = i * 6 + (b0 + n - RS + 1)
                    (down if w is wd else gate_or_up)(b0 + n, w, i * 2 + f, wait)
            for n in range(2):
                u = b + UNITS_FFN - 2 + n
                down(u, wd, 2 * (NCH - 1) + n, u - RS + 1)

        sp.dma_start(ident[:, :], ident_c).then_inc(ident_loaded, 16)
        def load_x(h):
            for t in range(4 * h, 4 * h + 4):
                sp.dma_start(x_in[h][:, t % 4, :], x[0, t * P:(t + 1) * P, :]).then_inc(x_loaded[h], 16)

        load_x(0)
        ffn_loads(0, lambda: load_x(1))

        w = w_in[0]
        for n in range(N_IN):
            u = U_IN + n
            if n < 4:
                load_unit(u, cols(w, slice(768 + n * P, 768 + (n + 1) * P)), as3(u), u - RS + 1)
            elif n < 6:
                load_unit(u, cols(w, slice(512 + (n - 4) * P, 512 + (n - 3) * P)), as3(u), u - RS + 1)
            else:
                sp.wait_ge(w_lo_done, u - RS + 1)
                for kv in range(NKV):
                    c0 = kv * GQ * HD + (n - 6) * HD
                    sp.dma_start(as3(u)[:, :, kv * HD:(kv + 1) * HD],
                                 cols(w, slice(c0, c0 + HD))).then_inc(raw_loaded[u % RS], 16)
            if n == 3:
                sp.wait_ge(proj_out, 1)
                sp.dma_start(biast[:, :, :], bias_c).then_inc(bias_loaded, 16)
            if n >= 4 and n < 8:
                i = n - 4
                sp.wait_ge(proj_taken, END_IN[i])
                sp.dma_start(u_d[i * P:(i + 1) * P, :, :], ust[i % 3][:, :, :]).then_inc(u_stored, 16)
        for n in range(N_GLU):
            u = U_GLU + n
            load_unit(u, cols(w_glu[0], slice(n * 256, (n + 1) * 256)),
                      raw[u % RS][:, :].rearrange("p (k m) -> p k m", k=4), u - RS + 1)
        def load_out_unit(n):
            u = U_OUT + n
            n = n % KD
            sp.wait_ge(w_lo_done, u - RS + 1)
            for kv in range(NKV):
                src = w_out[0][kv * GQ * HD:(kv + 1) * GQ * HD, n * P:(n + 1) * P]
                sp.dma_start(as3(u)[kv * HD:(kv + 1) * HD, 0:4, :],
                             src.rearrange("(g d) m -> d g m", d=HD)).then_inc(raw_loaded[u % RS], 16)
            sp.dma_start(as3(u)[:, 4:8, :],
                         w_out[0][DA:, n * P:(n + 1) * P].rearrange("(k p) m -> p k m", p=P)
                         ).then_inc(raw_loaded[u % RS], 16)

        sp.wait_ge(proj_out, 2 * N_IN)
        sp.wait_ge(eb_stored, 4 * 32)
        sp.dma_start(ebs[:, :, :, :], eb_d).then_inc(eb_loaded, 16)
        sp.wait_ge(u_stored, 64)
        u_v = u_d.rearrange("(g h) t c -> t h g c", h=GH)
        for t in range(T):
            sp.dma_start(u8[t * GH:(t + 1) * GH, :, :], u_v[t]).then_inc(u8_loaded, 16)
        sp.dma_start(csn[:, :, :, :], cs_d).then_inc(cs_loaded, 16)
        sp.wait_ge(k_taken, 8)
        sp.wait_ge(zero_stored, 64)
        sp.dma_start(k_d.rearrange("g h c -> h g c")[:, :, (T - 1) * GH:], kst[:, :, :]).then_inc(k_stored, 16)
        sp.wait_ge(k_stored, 16)
        for t in range(T):
            c0 = (T - 1 - t) * GH
            sp.dma_start(Mt[t * GH:(t + 1) * GH, :, :],
                         k_d.rearrange("g h c -> h g c")[:, :, c0:c0 + P]).then_inc(m_loaded, 16)
        y_v = y_d.rearrange("(g h) t c -> t h g c", h=GH)
        for b in range(4):
            gs = slice(8 * b, 8 * b + 8)
            sp.wait_ge(y_taken, 2 * b + 2)
            for t in range(T):
                sp.dma_start(y_v[t][:, gs], u8[t * GH:(t + 1) * GH, gs, :]).then_inc(y_stored, 16)
            if b == 0:
                sp.wait_ge(inj_ready, 4)
            sp.wait_ge(y_stored, 16 * T * (b + 1))
            sp.dma_start(yT[:, b, :].rearrange("p (t c) -> p t c", t=T),
                         y_d[b * P:(b + 1) * P, :, :]).then_inc(yt_loaded, 16)
        sp.wait_ge(o_ready, 8)
        for n in range(N_OUT):
            load_out_unit(n)
        sp.wait_ge(y_ready, 8)
        sp.dma_start(gend[:, :], final_norm.partition_broadcast(P)).then_inc(gend_loaded, 16)
        ffn_loads(1)
        for t in range(KD):
            sp.wait_ge(fin_taken, 2 * t + 2)
            sp.dma_start(out[0, t * P:(t + 1) * P, :], osb[:, t % 2, :]).then_inc(out_stored[t % 2], 16)
        for i in range(2):
            sp.wait_ge(out_stored[i], 16 * KD // 2)

    @block.tensor
    def _(pe):
        def mm3(o, wh, wl, rh, rl, first, last):
            nc.tensor.matmul(o, wl, rh, start=first, stop=False)
            nc.tensor.matmul(o, wh, rl, start=False, stop=False)
            return nc.tensor.matmul(o, wh, rh, start=False, stop=last)

        def norm_sum(norm, h):
            kt = NORM_TILES[norm]
            pe.wait_ge(ssq_done, squares_before(norm) + (h + 1) * kt)
            before = split_before(norm) + (h * kt if norm != N_END else 0)
            if before:
                pe.wait_ge(h_tmp, before)
            if norm == N_END and h:
                pe.wait_ge(rms_done, 2 * norm + 1)
            for i in range(4):
                last = nc.tensor.matmul(bank[7][:, i:i + 1], ssq[:, h * HALF + i * P:h * HALF + (i + 1) * P],
                                        ones[:, 0:1], start=True, stop=True)
            last.then_inc(sum_ready, 1)

        def norm_spread(norm, h):
            pe.wait_ge(diag_done, 2 * norm + h + 1)
            nc.tensor.matmul(bank[7][:, :], ones[:, :], dgt(norm)[:, :, :].rearrange("p a b -> p (a b)"),
                             start=True, stop=True).then_inc(rb_ready, 1)

        def half_unit(unit_count, slot, h, o, waits, done, tiles=None):
            for s, v in waits:
                pe.wait_ge(s, v)
            pe.wait_ge(w_lo_done, unit_count)
            for k in range(KD):
                if tiles is not None:
                    pe.wait_ge(h_lo, tiles(k))
                last = mm3(o, wk(w_hi[slot], k), wk(w_lo[slot], k), hT_hi[:, k, hs(h)], hT_lo[:, k, hs(h)],
                           k == 0, k == KD - 1)
            last.then_inc(done, 1)

        def wide_unit(unit_count, slot, banks, waits, done):
            for h in range(2):
                half_unit(unit_count, slot, h, bank[banks[h]][:, :], waits[h], done)

        def ffn(which, norm, between, after):
            b = U_OF[which]
            g0 = 4 * NCH * which
            d0 = 16 * NCH * which
            seen = set()
            for n, (kind, f, h) in enumerate(FIRST):
                u = b + f + (2 if kind == "U" else 0)
                waits = [(gate_taken, g0 + FIRST_GATES[2 * f + h])] if kind == "U" else []
                tiles = None
                if h not in seen:
                    seen.add(h)
                    tiles = lambda k, h=h: split_before(norm) + h * KD + k + 1
                half_unit(u + 1, u % WS, h, bank[2 * f + h][:, :], waits, ff_out, tiles)
                between(n)

            def down(units_ready, slots, a_ready, d_base, after=lambda n: None):
                pe.wait_ge(w_lo_done, units_ready)
                pe.wait_ge(a_lo_done, a_ready)
                for n in range(16):
                    d, h = n % KD, n // KD
                    if n >= 3:
                        pe.wait_ge(down_taken, d_base + (n - 2))
                    o = bank[4 + n % 3][:, :]
                    for f in range(2):
                        last = mm3(o, wk(w_hi[slots[f]], d), wk(w_lo[slots[f]], d),
                                   aT_hi[:, 2 * f + h, :], aT_lo[:, 2 * f + h, :], f == 0, f == 1)
                    last.then_inc(ff_out, 1)
                    after(n)

            def body(i, dbase):
                ub = b + 4
                for f in range(2):
                    waits = [[(up_taken, i * 4 + (g0 + 2 * f + h + 1))] for h in range(2)]
                    wide_unit(i * 6 + (ub + f + 1), (ub + f) % WS, (2 * f, 2 * f + 1), waits, ff_out)
                down(i * 6 + (ub + 4), ((ub + 2) % WS, (ub + 3) % WS), i * 4 + (g0 + 4), dbase)
                for f in range(2):
                    waits = [[(gate_taken, i * 4 + (g0 + 4 + 2 * f + h + 1))] for h in range(2)]
                    wide_unit(i * 6 + (ub + 4 + f + 1), (ub + 4 + f) % WS, (2 * f, 2 * f + 1), waits, ff_out)

            with pe.Fori(0, NCH - 1) as i:
                body(i, i * 16 + d0)
            u = b + UNITS_FFN - 2
            down(u + 2, (u % WS, (u + 1) % WS), g0 + 4 * NCH, d0 + 16 * (NCH - 1), after)

        pe.wait_ge(ident_loaded, 16)
        def x_tiles(h):
            for t in range(4 * h, 4 * h + 4):
                pe.wait_ge(x_loaded[h], 64)
                for kh in range(2):
                    if t == 7:
                        pe.wait_ge((xt_act, xt_dve)[kh], 5)
                    for kk in range(4):
                        k = 4 * kh + kk
                        last = nc.tensor.transpose(bank[X_BANK[2 * t + kh]][:, kk * P:(kk + 1) * P],
                                                   x_in[h][:, t % 4, k * P:(k + 1) * P], ident[:, :])
                    last.then_inc(xt_done, 1)

        def c_tiles():
            pe.wait_ge(c_loaded, 64)
            for ri in range(2):
                for i in range(4):
                    last = nc.tensor.transpose(bank[ri][:, i * P:(i + 1) * P],
                                               c_in[:, ri, i, :, :].rearrange("p a s -> p (a s)"), ident[:, :])
                last.then_inc(ct_ready, 1)

        def second_half(norm):
            def between(n):
                if n == 0:
                    norm_sum(norm, 1)
                elif n == 1:
                    norm_spread(norm, 1)
            return between

        def first_half(norm):
            def after(n):
                if n == 9:
                    norm_sum(norm, 0)
                elif n == 11:
                    norm_spread(norm, 0)
            return after

        x_tiles(0)
        pe.wait_ge(xt_act, 4)
        pe.wait_ge(xt_dve, 4)
        c_tiles()
        pe.wait_ge(ct_taken, 4)
        pe.wait_ge(consts_set, 1)
        norm_sum(N_FF1, 0)
        norm_spread(N_FF1, 0)

        def start(n):
            if n == 0:
                x_tiles(1)
                pe.wait_ge(xt_act, 8)
                pe.wait_ge(xt_dve, 8)
            elif n == 1:
                norm_sum(N_FF1, 1)
            elif n == 2:
                norm_spread(N_FF1, 1)

        ffn(0, N_FF1, start, first_half(N_MIX))

        seen = set()
        for o, (n, h) in enumerate(IN_ORDER):
            u = U_IN + n
            waits = [(proj_taken, o - 3)] if o >= 4 else []
            if o == 0:
                waits = [(up_taken, 4 * NCH)]
            tiles = None
            if h not in seen:
                seen.add(h)
                tiles = lambda k, h=h: split_before(N_MIX) + h * KD + k + 1
            half_unit(u + 1, u % WS, h, bank[o % 4][:, :], waits, proj_out, tiles)
            second_half(N_MIX)(o)
            if 13 <= o < 17:
                b = o - 13
                pe.wait_ge(proj_taken, END_IN[5])
                pe.wait_ge(pads_set, 1)
                for m in range(4):
                    n = 4 * b + m
                    last = nc.tensor.transpose(bank[4 + b][:, m * P:(m + 1) * P],
                                               vTp[:, CHUNK * n:CHUNK * n + P], ident[:, :])
                last.then_inc(v_ready, 1)

        def round_free(kind, b, i=0):
            n = ROUND.index(((kind, b), i))
            if n < 3:
                pe.wait_ge(v_taken, 4)
                return
            (kind, b), i = ROUND[n - 3]
            if kind == "K":
                pe.wait_ge(k_taken, b + 1)
            elif kind == "E":
                pe.wait_ge(e_taken, b + 1)
            elif kind == "I":
                pe.wait_ge(inj_taken, b + 1)
            else:
                pe.wait_ge(y_taken, 2 * b + i + 1)

        def blocks_k(b):
            j0, g2 = 4 * (b // 2), b % 2
            r = slice(g2 * NS, (g2 + 1) * NS)
            round_free("K", b)
            for jj in range(4):
                for ri in range(2):
                    last = nc.tensor.matmul(bank[round_bank("K", b)][0:GH, jj * P:(jj + 1) * P],
                                            Bb[r, ri, j0 + jj, :], CL[r, ri, j0 + jj, 0:P],
                                            start=ri == 0, stop=ri == 1)
            last.then_inc(k_ready, 1)

        def transposes_e(b):
            pe.wait_ge(eb_loaded, 16)
            round_free("E", b)
            for jj in range(2):
                for ri in range(2):
                    m = 2 * jj + ri
                    last = nc.tensor.transpose(bank[round_bank("E", b)][:, m * P:(m + 1) * P],
                                               ebs[:, ri, 2 * b + jj, :], ident[:, :])
            last.then_inc(e_ready, 1)

        def inject(b):
            pe.wait_ge(e_taken, 2 * b + 2)
            pe.wait_ge(u8_loaded, 16 * T)
            for ri in range(2):
                round_free("I", b, ri)
                for jj in range(4):
                    j = 4 * b + jj
                    for g2 in range(2):
                        last = nc.tensor.matmul(
                            bank[round_bank("I", b, ri)][g2 * NS:(g2 + 1) * NS, jj * P:(jj + 1) * P],
                            Et[:, j, ri, g2 * NS:(g2 + 1) * NS], u8[:, 2 * j + g2, :], start=True, stop=True)
            last.then_inc(inj_ready, 1)

        def outputs_y(b):
            pe.wait_ge(m_loaded, 16 * T)
            pe.wait_ge(state_done, b + 1)
            for g2 in range(2):
                round_free("Y", b, g2)
                for jj in range(4):
                    j = 4 * b + jj
                    g = 2 * j + g2
                    r = slice(g2 * NS, (g2 + 1) * NS)
                    o = bank[round_bank("Y", b, g2)][:, jj * P:(jj + 1) * P]
                    nc.tensor.matmul(o, Mt[:, g, :], u8[:, g, :], start=True, stop=False)
                    nc.tensor.matmul(o, CL[r, 0, j, GH:], tr[r, j, :], start=False, stop=False)
                    last = nc.tensor.matmul(o, CL[r, 1, j, GH:], ti[r, j, :], start=False, stop=True)
                last.then_inc(y_ready, 1)

        def scores(m):
            for kv in range(NKV):
                if m:
                    pe.wait_ge(s_biased, 2 * m + kv - 1)
                else:
                    pe.wait_ge(proj_taken, 2 * N_IN)
                r = slice(kv * HD, (kv + 1) * HD)
                for nn in range(2):
                    n = 2 * m + nn
                    for a in range(2):
                        o = bank[kv][:, (2 * nn + a) * P:(2 * nn + a + 1) * P]
                        last = nc.tensor.matmul(o, qT[r, n, 2 * a:2 * a + 2, :].rearrange("p g q -> p (g q)"),
                                                kTp[r, n * CHUNK:n * CHUNK + P], start=True, stop=True)
                last.then_inc(s_ready, 1)

        def transposes_p(m):
            pe.wait_ge(p_done, m + 1)
            if m:
                pe.wait_ge(pt_taken, 2 * m)
            for kv in range(NKV):
                for nn in range(2):
                    for a in range(2):
                        o = bank[2 + kv][:, (2 * nn + a) * P:(2 * nn + a + 1) * P]
                        last = nc.tensor.transpose(o, sco[m % 2][:, kv, nn, a, :], ident[:, :])
                last.then_inc(pt_ready, 1)

        def weighted(m):
            pe.wait_ge(v_taken, 4)
            if m:
                pe.wait_ge(o_taken, m)
            pe.wait_ge(pt_taken, 2 * m + 2)
            for nn in range(2):
                for kv in range(NKV):
                    last = nc.tensor.matmul(bank[4][kv * HD:(kv + 1) * HD, nn * 256:(nn + 1) * 256],
                                            vwin[:, 2 * m + nn, kv * HD:(kv + 1) * HD],
                                            pts[:, kv, nn, :, :].rearrange("p a q -> p (a q)"),
                                            start=True, stop=True)
            last.then_inc(o_ready, 1)

        step = {"K": blocks_k, "E": transposes_e, "I": inject, "Y": outputs_y,
                "S": scores, "T": transposes_p, "V": weighted}
        for kind, b in MIXER_PE:
            step[kind](b)

        def glu(o):
            n, mm, h = o // 4, o // 2 % 2, o % 2
            u = U_GLU + n
            pe.wait_ge(w_lo_done, u + 1)
            if o == 0:
                pe.wait_ge(s_biased, 16)
                pe.wait_ge(y_taken, 8)
            if o >= 4:
                pe.wait_ge(glu_tanh, o - 3)
            for k in range(4):
                pe.wait_ge(z_lo, 2 * k + 2)
                c0 = k * 256 + mm * P
                last = mm3(bank[o % 4][:, :], w_hi[u % WS][:, c0:c0 + P], w_lo[u % WS][:, c0:c0 + P],
                           hT_hi[:, 4 + k, hs(h)], hT_lo[:, 4 + k, hs(h)], k == 0, k == 3)
            last.then_inc(glu_out, 1)

        def out_part(o, ks):
            u = U_OUT + o
            pe.wait_ge(w_lo_done, u + 1)
            for k in ks:
                if k < 4:
                    pe.wait_ge(h_lo, split_before(N_ATT) + k + 1)
                else:
                    pe.wait_ge(h_lo, split_before(N_FF2))
                last = mm3(bank[o % 4][:, :], wk(w_hi[u % WS], k), wk(w_lo[u % WS], k),
                           hT_hi[:, k, hs(0)], hT_lo[:, k, hs(0)], k == 0, k == KD - 1)
            return last

        for o in range(8):
            glu(o)
            if o == 1 or o == 4:
                norm_sum(N_ATT, o // 4)
            elif o == 2 or o == 5:
                norm_spread(N_ATT, o // 4)
        pe.wait_ge(glu_tanh, 8)
        out_part(0, range(4))
        norm_sum(N_SSM, 0)
        out_part(1, range(4))
        norm_spread(N_SSM, 0)
        out_part(2, range(4))
        norm_sum(N_SSM, 1)
        norm_spread(N_SSM, 1)
        for o in range(N_OUT):
            u, h = U_OUT + o, o // KD
            if o < 3:
                out_part(o, range(4, KD)).then_inc(mix_out, 1)
                continue
            waits = [(mix_taken, o - 3)] if o >= 4 else []
            half_unit(u + 1, u % WS, h, bank[o % 4][:, :], waits, mix_out, tiles)
            first_half(N_FF2)(o)

        def out_tile(t):
            pe.wait_ge(down_taken, 32 * NCH - 8 + 8 * (t // 4))
            for kh in range(2):
                if t >= 2:
                    pe.wait_ge(fin_taken, 2 * t + kh - 3)
                for kk in range(4):
                    k = 4 * kh + kk
                    last = nc.tensor.transpose(bank[2 * (t % 2) + kh][:, kk * P:(kk + 1) * P],
                                               xT[:, k, t * P:(t + 1) * P], ident[:, :])
                last.then_inc(fin_ready, 1)

        def finish(n):
            if n == 9:
                norm_sum(N_END, 0)
            elif n in (11, 13, 15):
                out_tile((n - 11) // 2)

        ffn(1, N_FF2, second_half(N_FF2), finish)
        out_tile(3)
        norm_sum(N_END, 1)
        for t in range(4, KD):
            out_tile(t)

    @block.scalar
    def _(act):
        def split_hi(u, wait_out, raw_value):
            act.wait_ge(raw_loaded[u % RS], raw_value)
            for s, v in wait_out:
                act.wait_ge(s, v)
            act.activation(w_hi[u % WS][:, :], raw[u % RS][:, :], ACT.Copy).then_inc(w_hi_done, 1)

        def square(norm, n, src, as_src=lambda v: v):
            c = squares_before(norm) + n
            if c >= 2:
                act.wait_ge(ssq_done, c - 1)
            act.activation(as_src(sqt[:, c % 2, :]), src, ACT.Square).then_inc(sq_done, 1)

        def norm_std(norm, h):
            act.wait_ge(sum_ready, 2 * norm + h + 1)
            act.activation(std4[:, :], bank[7][:, 0:4], ACT.Sqrt, bias=eps_t[:, 0:1],
                           scale=NORM_SCALE[norm]).then_inc(std_done, 1)

        def norm_hi(norm, i, tile0=0, permuted=False):
            c = split_before(norm) + i
            h, k = i // NORM_TILES[norm], i % NORM_TILES[norm]
            act.wait_ge(h_tmp, c + 1)
            act.activation(dst_of(hT_hi, tile0 + k, h, permuted), src_of(htmp(norm, c), permuted),
                           ACT.Copy).then_inc(h_hi, 1)

        def norm(which, src, **where):
            for kind, i in norm_order(which):
                if kind == "S":
                    square(which, i, *src(i))
                elif kind == "R":
                    norm_std(which, i)
                else:
                    norm_hi(which, i, **where)

        def ffn(which):
            b = U_OF[which]
            o0 = OUTS_FFN * which
            g0 = 4 * NCH * which

            def take_gate(i4, bnk, ob):
                act.wait_ge(ff_out, ob)
                if not (isinstance(i4, int) and i4 == 0):
                    act.wait_ge(a_lo_done, i4 - 4 + bnk + 1)
                act.activation(sg[:, bnk, :], bank[bnk][:, :], ACT.Silu).then_inc(gate_taken, 1)

            def a_hi(i4, bnk):
                act.wait_ge(up_taken, i4 + bnk + 1)
                act.activation(aT_hi[:, bnk, :], sg[:, bnk, :], ACT.Copy).then_inc(a_hi_done, 1)

            def split(off_u, i, ob):
                u = b + off_u
                split_hi(u, [(ff_out, ob)], i * 48 + loads_until(u))

            for n, (kind, f, h) in enumerate(FIRST):
                if kind == "G":
                    if n:
                        take_gate(g0, 2 * f + h, o0 + n + 1)
                    if (f, h) == (0, 1):
                        split_hi(b + 3, [(ff_out, o0 + 4)], loads_until(b + 3))
                    if (f, h) == (1, 1):
                        split_hi(b + 4, [(ff_out, o0 + 5)], loads_until(b + 4))
            a_hi(g0, 0)
            split_hi(b + 5, [(ff_out, o0 + 6)], loads_until(b + 5))
            for n in range(1, 4):
                a_hi(g0, n)

            with act.Fori(0, NCH - 1) as i:
                ob = i * 24 + (o0 + 8)
                i4 = i * 4 + (g0 + 4)
                split(6, i, ob)
                for h in range(2):
                    take_gate(i4, h, ob + h + 1)
                split(7, i, ob + 2)
                for h in range(2):
                    take_gate(i4, 2 + h, ob + 2 + h + 1)
                split(8, i, ob + 4)
                split(9, i, ob + 20)
                split(10, i, ob + 20)
                for h in range(2):
                    a_hi(i4, h)
                split(11, i, ob + 22)
                for h in range(2):
                    a_hi(i4, 2 + h)

        for col, g, kt in ((0, ff1_norm[0], 8), (8, mix_norm[0], 8), (20, ssm_out_norm[0], 4),
                           (24, ff2_norm[0], 8), (32, final_norm, 8)):
            act.dma_start(gains[:, col:col + kt], g.rearrange("(k p) -> p k", p=P)).then_inc(consts_loaded, 16)
        for kv in range(NKV):
            act.dma_start(gains[kv * HD:(kv + 1) * HD, 16:20],
                          attn_out_norm[0][kv * 256:(kv + 1) * 256].rearrange("(g d) -> d g", d=HD)
                          ).then_inc(consts_loaded, 16)
        act.dma_start(bglu[:, :], b_glu[0].rearrange("(k p) -> p k", p=P)).then_inc(consts_loaded, 16)
        for g2 in range(2):
            for nn in range(2):
                for kv in range(NKV):
                    src = sink[0].rearrange("(v a g) -> g v a", v=2, g=2)[g2, kv].partition_broadcast(HD)
                    act.dma_start(sinkt[g2 * HD:(g2 + 1) * HD, kv, nn, :], src).then_inc(consts_loaded, 16)
        act.dma_start(dsk[:, :], d_skip[0].rearrange("(g h) -> h g", h=GH)).then_inc(consts_loaded, 16)
        for n, a in enumerate((a_re, a_im)):
            for g2 in range(2):
                act.dma_start(par[g2 * NS:(g2 + 1) * NS, n, :],
                              a[0].rearrange("(j g) p -> g p j", g=2)[g2]).then_inc(params_loaded, 16)
        for g2 in range(2):
            act.dma_start(par[g2 * NS:(g2 + 1) * NS, 2, :],
                          log_dt[0].rearrange("(j g) -> g j", g=2)[g2].partition_broadcast(NS)
                          ).then_inc(params_loaded, 16)
        for n, b in enumerate((b_re, b_im)):
            for g2 in range(2):
                act.dma_start(b_raw[g2 * NS:(g2 + 1) * NS, n, :, :],
                              b[0].rearrange("(j g) p h -> g p j h", g=2)[g2]).then_inc(params_loaded, 16)
        for n, c in enumerate((c_re, c_im)):
            for a in range(2):
                act.dma_start(c_in[:, n, :, a, :],
                              c[0].rearrange("(i g) h p -> (g h) i p", g=8)).then_inc(c_loaded, 16)

        def x_out(h):
            for t in range(4 * h, 4 * h + 4):
                act.wait_ge(xt_done, 2 * t + 1)
                act.activation(xT[:, 0:4, t * P:(t + 1) * P],
                               bank[X_BANK[2 * t]][:, :].rearrange("p (k m) -> p k m", k=4), ACT.Copy
                               ).then_inc(xt_act, 1)

        x_out(0)
        for ri in range(2):
            act.wait_ge(ct_ready, ri + 1)
            for g2 in range(2):
                r = slice(g2 * NS, (g2 + 1) * NS)
                src = bank[ri][r, :].rearrange("p (j g h) -> p g j h", g=2, h=GH)[:, g2]
                act.activation(CT[r, ri, :, :], src, ACT.Copy).then_inc(ct_taken, 1)

        def x_src(i):
            h, k = i // KD, i % KD
            if i == KD:
                x_out(1)
            if i % KD == 0:
                act.wait_ge(xt_act, 4 * h + 4)
                act.wait_ge(xt_dve, 4 * h + 4)
            return (xT[:, k, hs(h)],)

        def first_gate(o0, g0):
            act.wait_ge(ff_out, o0 + 1)
            if g0:
                act.wait_ge(a_lo_done, g0)
            act.activation(sg[:, 0, :], bank[0][:, :], ACT.Silu).then_inc(gate_taken, 1)

        act.wait_ge(consts_set, 1)
        for kind, i in norm_order(N_FF1):
            if kind == "S":
                square(N_FF1, i, *x_src(i))
            elif kind == "R":
                norm_std(N_FF1, i)
                if i == 0:
                    split_hi(0, [], loads_until(0))
                else:
                    first_gate(0, 0)
                    split_hi(2, [], loads_until(2))
            else:
                norm_hi(N_FF1, i)
                if i == 7:
                    split_hi(1, [], loads_until(1))
        ffn(0)

        def down_src(base):
            def src(i):
                act.wait_ge(down_taken, base + i + 1)
                return (xT[:, i % KD, hs(i // KD)],)
            return src

        split_hi(U_IN, [(ff_out, OUTS_FFN - 16)], loads_until(U_IN))
        act.wait_ge(eb_stored, 4 * 32)
        src = down_src(16 * (NCH - 1))
        for kind, i in norm_order(N_MIX):
            if kind == "S":
                square(N_MIX, i, *src(i))
            elif kind == "R":
                norm_std(N_MIX, i)
                if i == 1:
                    for m in (1, 2):
                        split_hi(U_IN + m, [(ff_out, OUTS_FFN)], loads_until(U_IN + m))
            else:
                norm_hi(N_MIX, i)

        for o, (n, h) in enumerate(IN_ORDER):
            act.wait_ge(proj_out, o + 1)
            src = bank[o % 4][:, :]
            if n < 4:
                if n == 3:
                    act.wait_ge(u_stored, 16)
                dst = ust[n % 3][:, :, h * 64:(h + 1) * 64]
                src = src.rearrange("p (c t) -> p t c", t=T)
            elif n < 6:
                dst = (kTp, vTp)[n - 4][:, CHUNK + h * HALF:CHUNK + (h + 1) * HALF]
            else:
                if n == 6 and h == 0:
                    act.wait_ge(u_stored, 64)
                dst = att_tile(qT, n - 6, h)
                src = by_chunk(src)
            act.activation(dst, src, ACT.Copy).then_inc(proj_taken, 1)
            if o + 1 == END_IN[n] and n < N_IN - 2:
                nxt = U_IN + n + WS
                split_hi(nxt, [(proj_out, o + 1)], loads_until(nxt))

        def k_out(b):
            act.wait_ge(k_ready, b + 1)
            j0, g2 = 4 * (b // 2), b % 2
            dst = kst[:, :, :].rearrange("p (j g) m -> p g j m", g=2)[:, g2, j0:j0 + 4, GH:]
            src = bank[round_bank("K", b)][0:GH, :].rearrange("p (j m) -> p j m", j=4)[:, :, GH:]
            act.activation(dst, src, ACT.Copy).then_inc(k_act, 1)

        def e_out(b):
            act.wait_ge(e_ready, b + 1)
            act.activation(Et[:, 2 * b:2 * b + 2, :, :],
                           bank[round_bank("E", b)][:, :].rearrange("p (j r m) -> p j r m", j=2, r=2), ACT.Copy
                           ).then_inc(e_taken, 1)

        def y_out(b):
            for g2 in range(2):
                act.wait_ge(y_ready, 2 * b + g2 + 1)
                dst = u8[:, :, :].rearrange("p (j g) c -> p g j c", g=2)[:, g2, 4 * b:4 * b + 4, :]
                act.activation(dst, bank[round_bank("Y", b, g2)][:, :].rearrange("p (j c) -> p j c", j=4),
                               ACT.Copy).then_inc(y_taken, 1)

        def exponentials(m):
            act.wait_ge(max_done, m + 1)
            for s in range(8):
                kv, nn, a = s // 4, s // 2 % 2, s % 2
                v = sco[m % 2][:, kv, nn, a, :]
                act.activation(v, v, ACT.Exp, bias=nm[:, m % 2, s:s + 1], scale=1.0,
                               accum_out=ssum[:, m % 2, s:s + 1])
            act.activation(esk[:, m % 2, :], esk[:, m % 2, :], ACT.Exp).then_inc(exp_done, 1)

        def p_out(m):
            for kv in range(NKV):
                act.wait_ge(pt_ready, 2 * m + kv + 1)
                if m:
                    act.wait_ge(o_ready, m)
                act.activation(pts[:, kv, :, :, :].rearrange("p n a q -> p (n a q)"), bank[2 + kv][:, :],
                               ACT.Copy).then_inc(pt_taken, 1)

        def o_out(m):
            act.wait_ge(o_ready, m + 1)
            act.activation(qT[:, 2 * m:2 * m + 2, :, :].rearrange("p n g q -> p (n g q)"), bank[4][:, :], ACT.Copy
                           ).then_inc(o_taken, 1)

        def gelu(k):
            act.wait_ge(yt_loaded, 16 * k + 16)
            for h in range(2):
                act.activation(yT[:, k, hs(h)], yT[:, k, hs(h)], ACT.Gelu_apprx_tanh).then_inc(z_done, 1)
            for h in range(2):
                act.wait_ge(z_done, 2 * k + h + 1)
                act.activation(hT_hi[:, 4 + k, hs(h)], yT[:, k, hs(h)], ACT.Copy).then_inc(z_hi, 1)

        step = {"k": k_out, "e": e_out, "y": y_out, "X": exponentials, "C": p_out, "O": o_out, "g": gelu}
        for kind, b in MIXER_ACT:
            step[kind](b)

        split_hi(U_GLU + 1, [(state_done, 4)], loads_until(U_GLU + 1))
        split_hi(U_OUT, [(o_ready, 8)], loads_until(U_OUT))

        def glu_half_sigmoid(o):
            mt = o // 2
            act.wait_ge(glu_out, o + 1)
            if o >= 2:
                act.wait_ge(glu_done, o - 1)
            act.activation(gth[:, o % 2, :], bank[o % 4][:, :], ACT.Tanh, bias=bglu_h[:, mt:mt + 1],
                           scale=0.5).then_inc(glu_tanh, 1)

        for kind, *at_ in GATED:
            if kind == "G":
                glu_half_sigmoid(*at_)
            elif kind == "W":
                u = U_OUT + at_[0]
                split_hi(u, [(glu_out, 4 * at_[0])], loads_until(u))
            elif kind == "R":
                norm_std(*at_)
            elif kind == "A":
                ssm = at_[0] == N_SSM
                norm_hi(*at_, tile0=4 if ssm else 0, permuted=ssm)
            elif at_[0] == N_ATT:
                act.wait_ge(o_taken, 8)
                square(*at_, att_tile(qT, at_[1] % 4, at_[1] // 4), by_chunk)
            else:
                h, k = at_[1] // 4, at_[1] % 4
                act.wait_ge(glu_done, 2 * k + h + 1)
                square(*at_, yT[:, k, hs(h)])

        def mix_src(i):
            act.wait_ge(mix_taken, i + 1)
            if i < N_OUT - 1 + 1:
                nxt = U_OUT + i + WS
                split_hi(nxt, [(mix_out, i + 1)], loads_until(nxt))
            return (xT[:, i % KD, hs(i // KD)],)

        norm(N_FF2, mix_src)
        first_gate(OUTS_FFN, 4 * NCH)
        ffn(1)
        src = down_src(16 * (2 * NCH - 1))
        for kind, i in norm_order(N_END):
            if kind == "S":
                square(N_END, i, *src(i))
            else:
                norm_std(N_END, i)

    @block.vector
    def _(dve):
        def split_lo(u, count):
            dve.wait_ge(w_hi_done, count)
            dve.tensor_tensor(w_lo[u % WS][:, :], raw[u % RS][:, :], w_hi[u % WS][:, :].bitcast(F32),
                              ALU.subtract).then_inc(w_lo_done, 1)

        def norm_rms(norm, h):
            r = rms4[:, h, :]
            n0 = 5 * (2 * norm + h)
            dve.wait_ge(std_done, 2 * norm + h + 1)
            dve.tensor_scalar(nv4[:, :], bank[7][:, 0:4], NORM_SCALE[norm], EPS, ALU.mult, ALU.add
                              ).then_inc(newton, 1)
            dve.reciprocal(r, std4[:, :]).then_inc(newton, 1)
            dve.wait_ge(newton, n0 + 2)
            dve.tensor_tensor(nt4[:, 0, :], r, r, ALU.mult).then_inc(newton, 1)
            dve.wait_ge(newton, n0 + 3)
            dve.tensor_tensor(nt4[:, 1, :], nt4[:, 0, :], nv4[:, :], ALU.mult).then_inc(newton, 1)
            dve.wait_ge(newton, n0 + 4)
            dve.tensor_scalar(nt4[:, 0, :], nt4[:, 1, :], -0.5, 1.5, ALU.mult, ALU.add).then_inc(newton, 1)
            dve.wait_ge(newton, n0 + 5)
            dve.tensor_tensor(r, r, nt4[:, 0, :], ALU.mult).then_inc(rms_done, 1)
            dve.wait_ge(rms_done, 2 * norm + h + 1)
            if norm != N_END:
                dve.tensor_tensor(dgt(norm)[:, :, :], ident[:, :].unsqueeze(1).to_broadcast([P, 4, P]),
                                  r.unsqueeze(2).to_broadcast([P, 4, P]), ALU.mult).then_inc(diag_done, 1)

        def norm_scale(norm, i, src, v=lambda t: t):
            kt = NORM_TILES[norm]
            h, k = i // kt, i % kt
            c = split_before(norm) + i
            g = gains[:, G_COL[norm] + k:G_COL[norm] + k + 1]
            if k == 0:
                dve.wait_ge(rb_ready, 2 * norm + h + 1)
            if c >= 3:
                dve.wait_ge(h_lo, c - 2)
            dve.scalar_tensor_tensor(v(htmp(norm, c)), src, g, v(bank[7][:, :]),
                                     ALU.mult, ALU.mult).then_inc(h_tmp, 1)

        def norm(which, src, before=lambda i: None):
            for kind, i in norm_order(which):
                if kind == "S":
                    before(i)
                elif kind == "R":
                    norm_rms(which, i)
                else:
                    norm_scale(which, i, *src(i))

        def x_tile(i):
            return (xT[:, i % KD, hs(i // KD)],)

        def ffn(which):
            b = U_OF[which]
            o0 = OUTS_FFN * which
            g0 = 4 * NCH * which
            d0 = 16 * NCH * which

            def take_up(i4, bnk, ob, gates=None):
                dve.wait_ge(ff_out, ob)
                dve.wait_ge(gate_taken, i4 + (bnk + 1 if gates is None else gates))
                dve.tensor_tensor(sg[:, bnk, :], sg[:, bnk, :], bank[bnk][:, :], ALU.mult).then_inc(up_taken, 1)

            def a_lo(i4, bnk):
                dve.wait_ge(a_hi_done, i4 + bnk + 1)
                dve.tensor_tensor(aT_lo[:, bnk, :], sg[:, bnk, :], aT_hi[:, bnk, :].bitcast(F32),
                                  ALU.subtract).then_inc(a_lo_done, 1)

            def take_down(n, ob):
                dve.wait_ge(ff_out, ob + (n + 1))
                xs = xT[:, n % KD, hs(n // KD)]
                dve.scalar_tensor_tensor(xs, bank[4 + n % 3][:, :], 0.5, xs, ALU.mult, ALU.add
                                         ).then_inc(down_taken, 1)

            def ups(i4, ob, middle):
                take_up(i4, 0, ob + 1)
                take_up(i4, 1, ob + 2)
                a_lo(i4, 0)
                a_lo(i4, 1)
                middle()
                take_up(i4, 2, ob + 3)
                take_up(i4, 3, ob + 4)
                a_lo(i4, 2)
                a_lo(i4, 3)

            take_up(g0, 0, o0 + 3, 1)
            split_lo(b + 3, b + 4)
            split_lo(b + 4, b + 5)
            a_lo(g0, 0)
            take_up(g0, 1, o0 + 6, 3)
            split_lo(b + 5, b + 6)
            take_up(g0, 2, o0 + 7, 4)
            a_lo(g0, 1)
            take_up(g0, 3, o0 + 8, 4)
            a_lo(g0, 2)
            a_lo(g0, 3)
            with dve.Fori(0, NCH - 1) as i:
                ob = i * 24 + (o0 + 8)
                i4 = i * 4 + (g0 + 4)
                for n in (6, 7, 8):
                    split_lo(b + n, i * 6 + (b + n + 1))
                for n in range(16):
                    take_down(n, ob + 4)
                for n in (9, 10):
                    split_lo(b + n, i * 6 + (b + n + 1))
                ups(i4, ob + 20, lambda: split_lo(b + 11, i * 6 + (b + 12)))
            if which == 0:
                split_lo(U_IN, U_IN + 1)
            return lambda n: take_down(n, o0 + OUTS_FFN - 16)

        def x_out(h):
            for t in range(4 * h, 4 * h + 4):
                dve.wait_ge(xt_done, 2 * t + 2)
                dve.tensor_copy(xT[:, 4:8, t * P:(t + 1) * P],
                                bank[X_BANK[2 * t + 1]][:, :].rearrange("p (k m) -> p k m", k=4)
                                ).then_inc(xt_dve, 1)

        x_out(0)
        dve.wait_ge(consts_loaded, CONST_DMAS * 16)
        dve.tensor_scalar(bglu_h[:, :], bglu[:, :], 0.5, None, ALU.mult)
        dve.tensor_scalar(gains[:, 20:24], gains[:, 20:24], 0.5, None, ALU.mult).then_inc(gains_set, 1)
        dve.wait_ge(gains_set, 1)
        for kind, i in norm_order(N_FF1):
            if kind == "R":
                norm_rms(N_FF1, i)
                split_lo(2 * i, 2 * i + 1)
            elif kind == "A":
                norm_scale(N_FF1, i, *x_tile(i))
                if i == 7:
                    split_lo(1, 2)
                    x_out(1)
        dve.wait_ge(params_loaded, 16 * 10)
        for n in range(2):
            dve.tensor_tensor(ivt[:, n, :], par[:, n, :], par[:, n, :], ALU.mult).then_inc(inv_done, 1)
        dve.wait_ge(inv_done, 2)
        dve.tensor_tensor(ivt[:, 3, :], ivt[:, 0, :], ivt[:, 1, :], ALU.add).then_inc(inv_done, 1)
        dve.wait_ge(inv_done, 3)
        dve.reciprocal(ivt[:, 2, :], ivt[:, 3, :]).then_inc(inv_done, 1)
        take = ffn(0)
        for kind, i in norm_order(N_MIX):
            if kind == "S":
                take(i)
            elif kind == "R":
                norm_rms(N_MIX, i)
                if i == 1:
                    split_lo(U_IN + 1, U_IN + 2)
                    split_lo(U_IN + 2, U_IN + 3)
            else:
                norm_scale(N_MIX, i, *x_tile(i))
        def v_out(b):
            dve.wait_ge(v_ready, b + 1)
            dve.tensor_copy(vwin[:, 4 * b:4 * b + 4, :], bank[4 + b][:, :].rearrange("p (n m) -> p n m", n=4)
                            ).then_inc(v_taken, 1)

        for n in range(3, N_IN):
            split_lo(U_IN + n, U_IN + n + 1)
        v_out(0)
        v_out(1)
        split_lo(U_GLU, U_GLU + 1)
        v_out(2)
        v_out(3)
        dve.tensor_tensor(dgl[:, :, :], ident[0:GH, 0:GH].unsqueeze(1).to_broadcast([GH, NG, GH]),
                          dsk[:, :].unsqueeze(2).to_broadcast([GH, NG, GH]), ALU.mult).then_inc(diag_chain, 1)
        dve.wait_ge(diag_chain, 1)

        def k_first(b):
            dve.wait_ge(k_ready, b + 1)
            dve.wait_ge(k_act, b + 1)
            j0, g2 = 4 * (b // 2), b % 2
            dst = kst[:, :, :].rearrange("p (j g) m -> p g j m", g=2)[:, g2, j0:j0 + 4, 0:GH]
            dg = dgl[:, :, :].rearrange("p (j g) m -> p g j m", g=2)[:, g2, j0:j0 + 4, :]
            src = bank[round_bank("K", b)][0:GH, :].rearrange("p (j m) -> p j m", j=4)[:, :, 0:GH]
            dve.tensor_tensor(dst, src, dg, ALU.add).then_inc(k_taken, 1)

        sc = [0]

        def step(ins):
            sc[0] += 1
            ins.then_inc(state_chain, 1)

        def steps_done():
            dve.wait_ge(state_chain, sc[0])

        def recurrence(b):
            js = slice(4 * b, 4 * b + 4)
            re, im = (bank[round_bank("I", b, i)][:, :] for i in range(2))
            c_ = csn[:, 0, js, :].rearrange("p j c -> p (j c)")
            s_ = csn[:, 1, js, :].rearrange("p j c -> p (j c)")
            trb = tr[:, js, :].rearrange("p j c -> p (j c)")
            tib = ti[:, js, :].rearrange("p j c -> p (j c)")
            r0, r1 = rtm[:, 0, :], rtm[:, 1, :]
            if b == 0:
                dve.wait_ge(cs_loaded, 16)
                dve.wait_ge(e_taken, 8)
                dve.wait_ge(k_stored, 16)
            dve.wait_ge(inj_ready, b + 1)
            step(dve.tensor_tensor(trb, c_, re, ALU.mult))
            step(dve.tensor_tensor(r0, s_, im, ALU.mult))
            step(dve.tensor_tensor(tib, c_, im, ALU.mult))
            step(dve.tensor_tensor(r1, s_, re, ALU.mult))
            steps_done()
            dve.tensor_tensor(trb, trb, r0, ALU.add).then_inc(inj_taken, 1)
            step(dve.tensor_tensor(tib, tib, r1, ALU.subtract))
            steps_done()
            dve.wait_ge(inj_taken, b + 1)
            for j in range(4 * b, 4 * b + 4):
                for t_ in (tr, ti):
                    last = dve.tensor_tensor_scan(t_[:, j, :], dec8[:, j:j + 1].to_broadcast([P, NC]),
                                                  t_[:, j, :], 0.0, ALU.mult, ALU.add)
                    last.then_inc(scanned, 1)

        ac = [0]

        def astep(ins):
            ac[0] += 1
            ins.then_inc(att_chain, 1)
            dve.wait_ge(att_chain, ac[0])

        sink8 = sinkt[:, :, :, :].rearrange("p v n a -> p (v n a)")

        def wide_scores(m):
            return sco[m % 2][:, :, :, :, :].rearrange("p v n a k -> p (v n a) k")

        def maxima(m):
            if m == 0:
                dve.wait_ge(bias_loaded, 16)
            if m >= 2:
                dve.wait_ge(pt_ready, 2 * m - 2)
            for kv in range(NKV):
                dve.wait_ge(s_ready, 2 * m + kv + 1)
                dve.scalar_tensor_tensor(sco[m % 2][:, kv, :, :, :].rearrange("p n a k -> p n (a k)"),
                                         bank[kv][:, :].rearrange("p (n k) -> p n k", n=2), HD ** -0.5,
                                         biast[:, kv, :].unsqueeze(1).to_broadcast([P, 2, 256]),
                                         ALU.mult, ALU.add).then_inc(s_biased, 1)
            dve.wait_ge(s_biased, 2 * m + 2)
            if m == 0:
                astep(dve.memset(sco[0][:, :, 0, :, 0:CHUNK], -1e30))
            astep(dve.reduce_max(mx[:, :], wide_scores(m), AX.X))
            astep(dve.tensor_tensor(mx[:, :], mx[:, :], sink8, ALU.max))
            astep(dve.tensor_scalar(nm[:, m % 2, :], mx[:, :], -1.0, None, ALU.mult))
            dve.tensor_tensor(esk[:, m % 2, :], sink8, mx[:, :], ALU.subtract).then_inc(max_done, 1)

        def normalise(m):
            dve.wait_ge(exp_done, m + 1)
            astep(dve.tensor_tensor(ssum[:, m % 2, :], ssum[:, m % 2, :], esk[:, m % 2, :], ALU.add))
            astep(dve.reciprocal(rden[:, :], ssum[:, m % 2, :]))
            dve.tensor_tensor(wide_scores(m), wide_scores(m), rden[:, :].unsqueeze(2).to_broadcast([P, 8, P]),
                              ALU.mult).then_inc(p_done, 1)

        def z_low(k):
            if k == 0:
                dve.wait_ge(state_done, 4)
            for h in range(2):
                dve.wait_ge(z_hi, 2 * k + h + 1)
                dve.tensor_tensor(hT_lo[:, 4 + k, hs(h)], yT[:, k, hs(h)], hT_hi[:, 4 + k, hs(h)].bitcast(F32),
                                  ALU.subtract).then_inc(z_lo, 1)

        mixer_step = {"d": k_first, "R": recurrence, "A": maxima, "B": normalise, "z": z_low}
        for kind, b in MIXER_DVE:
            mixer_step[kind](b)

        split_lo(U_GLU + 1, U_GLU + 2)
        split_lo(U_OUT, U_OUT + 1)
        for kind, *at_ in GATED:
            if kind == "G":
                o = at_[0]
                zs = yT[:, o // 2, hs(o % 2)]
                dve.wait_ge(glu_tanh, o + 1)
                dve.scalar_tensor_tensor(zs, gth[:, o % 2, :], 1.0, zs, ALU.add, ALU.mult).then_inc(glu_done, 1)
            elif kind == "W":
                split_lo(U_OUT + at_[0], U_OUT + at_[0] + 1)
            elif kind == "R":
                norm_rms(*at_)
            elif kind == "A":
                i = at_[1]
                if at_[0] == N_ATT:
                    norm_scale(*at_, att_tile(qT, i % 4, i // 4), by_chunk)
                else:
                    norm_scale(*at_, yT[:, i % 4, hs(i // 4)])

        def take_mix(i):
            dve.wait_ge(mix_out, i + 1)
            xs = xT[:, i % KD, hs(i // KD)]
            dve.tensor_tensor(xs, xs, bank[i % 4][:, :], ALU.add).then_inc(mix_taken, 1)
            split_lo(U_OUT + i + WS, U_OUT + i + WS + 1)

        norm(N_FF2, x_tile, take_mix)
        take = ffn(1)

        def out_rows(t):
            if t == 0:
                dve.wait_ge(gend_loaded, 16)
            for kh in range(2):
                dve.wait_ge(fin_ready, 2 * t + kh + 1)
                if t >= 2 and kh == 0:
                    dve.wait_ge(out_stored[t % 2], 16 * (t // 2))
                cs = slice(kh * HALF, (kh + 1) * HALF)
                dve.scalar_tensor_tensor(osb[:, t % 2, cs], bank[2 * (t % 2) + kh][:, :],
                                         rms4[:, t // 4, t % 4:t % 4 + 1], gend[:, cs], ALU.mult, ALU.mult
                                         ).then_inc(fin_taken, 1)

        for kind, i in norm_order(N_END):
            if kind == "S":
                take(i)
                if i in (11, 13, 15):
                    out_rows((i - 11) // 2)
            elif i == 0:
                norm_rms(N_END, 0)
        out_rows(3)
        norm_rms(N_END, 1)
        for t in range(4, KD):
            out_rows(t)

    @block.gpsimd
    def _(pool):
        def add_square(norm, n):
            kt = NORM_TILES[norm]
            h, first = n // kt, n % kt == 0
            c = squares_before(norm) + n
            pool.wait_ge(sq_done, c + 1)
            if first and norm:
                pool.wait_ge(sum_ready, 2 * norm)
            s = sqt[:, c % 2, :]
            if first:
                pool.tensor_copy(ssq[:, hs(h)], s).then_inc(ssq_done, 1)
            else:
                pool.wait_ge(ssq_done, c)
                pool.tensor_tensor(ssq[:, hs(h)], ssq[:, hs(h)], s, ALU.add).then_inc(ssq_done, 1)

        def take_lo(norm, i, tile0=0, permuted=False):
            h, k = i // NORM_TILES[norm], i % NORM_TILES[norm]
            c = split_before(norm) + i
            pool.wait_ge(h_hi, c + 1)
            pool.tensor_tensor(dst_of(hT_lo, tile0 + k, h, permuted), src_of(htmp(norm, c), permuted),
                               dst_of(hT_hi, tile0 + k, h, permuted).bitcast(F32), ALU.subtract
                               ).then_inc(h_lo, 1)

        def norm(which):
            for kind, i in norm_order(which):
                if kind == "S":
                    add_square(which, i)
                elif kind == "A":
                    take_lo(which, i)

        pool.memset(ones[:, :], 1.0)
        pool.memset(zero[:, :], 0.0)
        pool.memset(unit[:, 0, :, :], 1.0)
        pool.memset(unit[:, 1, :, :], 0.0)
        pool.memset(eps_t[:, :], EPS).then_inc(consts_set, 1)
        pool.wait_ge(consts_set, 1)
        zv = k_d.rearrange("(n g) h c -> n (g h) c", g=8)
        for n in range(4):
            pool.dma_start(zv[n][:, 0:(T - 1) * GH], zero[:, :]).then_inc(zero_stored, 16)
        norm(N_FF1)

        chain = [0]

        def link(ins):
            chain[0] += 1
            ins.then_inc(prep_chain, 1)
            pool.wait_ge(prep_chain, chain[0])

        slot = [0]

        def new():
            slot[0] += 1
            assert slot[0] <= NPAR, slot
            return pw[:, slot[0] - 1, :]

        def tt(o, a, b_, op):
            link(pool.tensor_tensor(o, a, b_, op))

        def ts(o, a, s1, op1, s2=None, op2=None):
            if op2 is None:
                link(pool.tensor_scalar(o, a, s1, None, op1))
            else:
                link(pool.tensor_scalar(o, a, s1, s2, op1, op2))

        def stt(o, a, s1, b_, op1, op2):
            ts(tmp, a, s1, op1)
            tt(o, tmp, b_, op2)

        t0, t1, t2, tmp = new(), new(), new(), new()
        nrm, red, pol, two = new(), new(), new(), new()

        def exp_parts(xv):
            ts(t0, xv, -150.0, ALU.max, 100.0, ALU.min)
            ts(nrm, t0, 1 / math.log(2.0), ALU.mult, MAGIC, ALU.add)
            ts(nrm, nrm, MAGIC, ALU.subtract)
            stt(red, nrm, -LN2_1, t0, ALU.mult, ALU.add)
            stt(red, nrm, -LN2_2, red, ALU.mult, ALU.add)
            ts(pol, red, 1 / 5040, ALU.mult)
            for c in (1 / 720, 1 / 120, 1 / 24, 1 / 6, 1 / 2, 1.0):
                stt(pol, pol, c, red, ALU.add, ALU.mult)
            ts(t1, nrm, -126.0, ALU.max, 127.0, ALU.min)
            tt(t2, nrm, t1, ALU.subtract)
            ts(pwi[:, 0, :], t1, 127.0, ALU.add, 2.0 ** 23, ALU.mult)
            ts(pwi[:, 1, :], t2, 127.0, ALU.add, 2.0 ** 23, ALU.mult)
            tt(two, pwi[:, 0, :].bitcast(F32), pwi[:, 1, :].bitcast(F32), ALU.mult)

        pool.wait_ge(params_loaded, 16 * 10)
        are, aim = par[:, 0, :], par[:, 1, :]
        dt, xr, th = new(), new(), new()
        exp_parts(par[:, 2, :])
        stt(dt, pol, 1.0, two, ALU.add, ALU.mult)
        tt(xr, are, dt, ALU.mult)
        tt(th, aim, dt, ALU.mult)
        exp_parts(xr)
        em1, mag = new(), new()
        tt(t0, two, pol, ALU.mult)
        stt(em1, two, -1.0, t0, ALU.add, ALU.add)
        tt(mag, two, t0, ALU.add)
        ts(nrm, th, 1 / (2 * math.pi), ALU.mult, MAGIC, ALU.add)
        ts(nrm, nrm, MAGIC, ALU.subtract)
        stt(red, nrm, -TWO_PI_1, th, ALU.mult, ALU.add)
        stt(red, nrm, -TWO_PI_2, red, ALU.mult, ALU.add)
        stt(red, nrm, -TWO_PI_3, red, ALU.mult, ALU.add)
        ts(red, red, 3.2, ALU.min, -3.2, ALU.max)
        q, q2, sn, cs = new(), new(), new(), new()
        ts(q, red, 0.25, ALU.mult)
        tt(q2, q, q, ALU.mult)
        ts(sn, q2, 1 / 362880, ALU.mult)
        for c in (-1 / 5040, 1 / 120, -1 / 6):
            stt(sn, sn, c, q2, ALU.add, ALU.mult)
        stt(sn, sn, 1.0, q, ALU.add, ALU.mult)
        ts(cs, q2, -1 / 3628800, ALU.mult)
        for c in (1 / 40320, -1 / 720, 1 / 24, -1 / 2):
            stt(cs, cs, c, q2, ALU.add, ALU.mult)
        ts(cs, cs, 1.0, ALU.add)
        s2_, c2_, sth, cth, cm1 = new(), new(), new(), new(), new()
        stt(s2_, sn, 2.0, cs, ALU.mult, ALU.mult)
        tt(t0, sn, sn, ALU.mult)
        ts(c2_, t0, -2.0, ALU.mult, 1.0, ALU.add)
        stt(sth, s2_, 2.0, c2_, ALU.mult, ALU.mult)
        tt(t0, s2_, s2_, ALU.mult)
        ts(cm1, t0, -2.0, ALU.mult)
        ts(cth, cm1, 1.0, ALU.add)
        er, ei, cr, ci = new(), new(), new(), new()
        tt(t0, em1, cth, ALU.mult)
        tt(er, t0, cm1, ALU.add)
        tt(ei, mag, sth, ALU.mult)
        lr = [lam[:, 0, k, :] for k in range(T + 1)]
        li = [lam[:, 1, k, :] for k in range(T + 1)]
        link(pool.memset(lr[0], 1.0))
        link(pool.memset(li[0], 0.0))
        tt(lr[1], mag, cth, ALU.mult)
        tt(li[1], mag, sth, ALU.mult)
        for k in range(1, T):
            tt(t0, lr[k], lr[1], ALU.mult)
            tt(t1, li[k], li[1], ALU.mult)
            tt(lr[k + 1], t0, t1, ALU.subtract)
            tt(t0, lr[k], li[1], ALU.mult)
            tt(t1, li[k], lr[1], ALU.mult)
            tt(li[k + 1], t0, t1, ALU.add)
        ts(lam[:, 2, :, :], lam[:, 1, :, :], -1.0, ALU.mult)
        pool.wait_ge(inv_done, 4)
        inv = ivt[:, 2, :]
        tt(t0, er, are, ALU.mult)
        tt(t1, ei, aim, ALU.mult)
        tt(t0, t0, t1, ALU.add)
        tt(cr, t0, inv, ALU.mult)
        tt(t0, ei, are, ALU.mult)
        tt(t1, er, aim, ALU.mult)
        tt(t0, t0, t1, ALU.subtract)
        tt(ci, t0, inv, ALU.mult)
        pr, pi = cth, sth
        for n in range(3):
            nr = rot8[:, 0, :] if n == 2 else new()
            ni = rot8[:, 1, :] if n == 2 else new()
            tt(t0, pr, pr, ALU.mult)
            tt(t1, pi, pi, ALU.mult)
            tt(nr, t0, t1, ALU.subtract)
            stt(ni, pr, 2.0, pi, ALU.mult, ALU.mult)
            pr, pi = nr, ni
        tt(t0, mag, mag, ALU.mult)
        tt(t0, t0, t0, ALU.mult)
        tt(dec8[:, :], t0, t0, ALU.mult)

        def wide(v, n=GH):
            return v.unsqueeze(2).to_broadcast([P, NJ, n])

        for o, (c0, c1, op) in enumerate(((cr, ci, ALU.subtract), (ci, cr, ALU.add))):
            tt(bc_tmp[:, 0, :, :], b_raw[:, 0, :, :], wide(c0), ALU.mult)
            tt(bc_tmp[:, 1, :, :], b_raw[:, 1, :, :], wide(c1), ALU.mult)
            tt(Bb[:, o, :, :], bc_tmp[:, 0, :, :], bc_tmp[:, 1, :, :], op)

        pc = [0]

        def link(ins):
            pc[0] += 1
            ins.then_inc(pool_chain, 1)
            pool.wait_ge(pool_chain, pc[0])

        def over_h(v, n):
            return v.unsqueeze(2).to_broadcast([P, n, GH])

        pool.wait_ge(ct_taken, 4)
        pt = [ptmp[:, i, :].rearrange("p (j h) -> p j h", h=GH) for i in range(2)]
        for k in range(T + 1):
            for o, (n0, n1) in enumerate(((0, 1), (2, 0))):
                link(pool.tensor_tensor(pt[0], CT[:, 0, :, :], over_h(lam[:, n0, k, :], NJ), ALU.mult))
                link(pool.tensor_tensor(pt[1], CT[:, 1, :, :], over_h(lam[:, n1, k, :], NJ), ALU.mult))
                link(pool.tensor_tensor(CL[:, o, :, k * GH:(k + 1) * GH], pt[0], pt[1], ALU.subtract))
        base_links = pc[0]

        cB = cur[:, :, :, 0:GH]
        cL = cur[:, :, :, GH:GH + T + 1]
        cR = cur[:, :, :, GH + T + 1]
        per = LINKS_PER_BATCH
        with pool.Fori(0, NJ // 4) as i:
            nl = [0]

            def ilink(ins):
                nl[0] += 1
                ins.then_inc(pool_chain, 1)
                pool.wait_ge(pool_chain, i * per + (base_links + nl[0]))

            def passed():
                pool.tensor_tensor(mark[:, :], unit[:, 0, 0, :], unit[:, 0, 0, :], ALU.mult)

            for ri in range(2):
                ilink(pool.tensor_copy(cB[:, ri], Bb[:, ri, bass.ds(i * 4, 4), :]))
                ilink(pool.tensor_copy(cL[:, ri].rearrange("p j k -> p k j"),
                                       lam[:, ri, :, bass.ds(i * 4, 4)]))
                ilink(pool.tensor_copy(cR[:, ri], rot8[:, ri, bass.ds(i * 4, 4)]))
            q = [ptmp[:, n, 0:4 * GH].rearrange("p (j h) -> p j h", h=GH) for n in range(2)]
            for t in range(T):
                e = T - 1 - t
                for o, (n0, n1, op) in enumerate(((0, 1, ALU.subtract), (1, 0, ALU.add))):
                    ilink(pool.tensor_tensor(q[0], cB[:, 0], over_h(cL[:, n0, :, e], 4), ALU.mult))
                    ilink(pool.tensor_tensor(q[1], cB[:, 1], over_h(cL[:, n1, :, e], 4), ALU.mult))
                    ilink(pool.tensor_tensor(EBb[:, o, :, t * GH:(t + 1) * GH], q[0], q[1], op))
            passed()
            pool.dma_start(eb_d[:, :, bass.ds(i * 4, 4), :], EBb[:, :, :, :]).then_inc(eb_stored, 16)
            pool.wait_ge(eb_stored, i * 32 + 16)
            ilink(pool.tensor_tensor(EBb[:, :, :, 0:1], unit[:, :, :, :], unit[:, :, :, :], ALU.mult))
            n = 1
            while n < NC:
                v = [ptmp[:, m, 0:4 * n].rearrange("p (j c) -> p j c", j=4) for m in range(2)]
                w = [cR[:, m, :].unsqueeze(2).to_broadcast([P, 4, n]) for m in range(2)]
                R = [EBb[:, m, :, 0:n] for m in range(2)]
                for o, (n0, n1, op) in enumerate(((0, 1, ALU.subtract), (1, 0, ALU.add))):
                    ilink(pool.tensor_tensor(v[0], R[0], w[n0], ALU.mult))
                    ilink(pool.tensor_tensor(v[1], R[1], w[n1], ALU.mult))
                    ilink(pool.tensor_tensor(EBb[:, o, :, n:2 * n], v[0], v[1], op))
                if 2 * n < NC:
                    a, b_ = ptmp[:, 0, 0:4], ptmp[:, 1, 0:4]
                    c_ = ptmp[:, 0, 4:8]
                    ilink(pool.tensor_tensor(a, cR[:, 0], cR[:, 0], ALU.mult))
                    ilink(pool.tensor_tensor(b_, cR[:, 1], cR[:, 1], ALU.mult))
                    ilink(pool.tensor_tensor(c_, cR[:, 0], cR[:, 1], ALU.mult))
                    ilink(pool.tensor_tensor(cR[:, 0], a, b_, ALU.subtract))
                    ilink(pool.tensor_tensor(cR[:, 1], c_, c_, ALU.add))
                n *= 2
            passed()
            pool.dma_start(cs_d[:, :, bass.ds(i * 4, 4), :], EBb[:, :, :, :]).then_inc(eb_stored, 16)
            pool.wait_ge(eb_stored, i * 32 + 32)
            assert nl[0] == per, nl

        norm(N_MIX)
        pool.wait_ge(h_lo, split_before(N_ATT))
        pool.memset(kTp[:, 0:CHUNK], 0.0)
        pool.memset(vTp[:, 0:CHUNK], 0.0).then_inc(pads_set, 1)

        bc = [0]

        def back(ins):
            bc[0] += 1
            ins.then_inc(back_chain, 1)

        def back_done():
            pool.wait_ge(back_chain, bc[0])

        def to_next(o, a, b_, op):
            back(pool.tensor_tensor(o[:, :, 1:], a.rearrange("p (j c) -> p j c", j=4)[:, :, 0:NC - 1],
                                    b_.rearrange("p (j c) -> p j c", j=4)[:, :, 0:NC - 1], op))
            back(pool.memset(o[:, :, 0:1], 0.0))

        w0, w1, w2 = (t[:, :] for t in btm)
        for b in range(4):
            js = slice(4 * b, 4 * b + 4)
            c_ = csn[:, 0, js, :].rearrange("p j c -> p (j c)")
            s_ = csn[:, 1, js, :].rearrange("p j c -> p (j c)")
            trb = tr[:, js, :].rearrange("p j c -> p (j c)")
            tib = ti[:, js, :].rearrange("p j c -> p (j c)")
            pool.wait_ge(scanned, 8 * b + 8)
            back(pool.tensor_tensor(w0, s_, trb, ALU.mult))
            back(pool.tensor_tensor(w1, s_, tib, ALU.mult))
            back(pool.tensor_tensor(w2, c_, trb, ALU.mult))
            back_done()
            to_next(tr[:, js, :], w2, w1, ALU.subtract)
            back_done()
            back(pool.tensor_tensor(w2, c_, tib, ALU.mult))
            back_done()
            to_next(ti[:, js, :], w0, w2, ALU.add)
            back_done()
            pool.tensor_copy(mark[:, :], unit[:, 0, 0, :]).then_inc(state_done, 1)

        for kind, *at_ in GATED:
            if kind == "S":
                add_square(*at_)
            elif kind == "A":
                take_lo(*at_, tile0=4 * (at_[0] - N_ATT), permuted=at_[0] == N_SSM)
        norm(N_FF2)
        norm(N_END)

    ctx.close()


_INS = ["x", "ff1_norm", "ff1_w_gate", "ff1_w_up", "ff1_w_down", "mix_norm", "w_in", "sink", "a_re", "a_im",
        "b_re", "b_im", "c_re", "c_im", "d_skip", "log_dt", "w_glu", "b_glu", "attn_out_norm",
        "ssm_out_norm", "w_out", "ff2_norm", "ff2_w_gate", "ff2_w_up", "ff2_w_down", "final_norm"]


def alibi_bias():
    q = np.arange(CHUNK)[:, None]
    key = np.arange(2 * CHUNK)[None, :] - CHUNK
    dist = np.abs(q - key).astype(np.float32)
    out = np.zeros((2, CHUNK, NKV, 2, 2 * CHUNK), np.float32)
    for g2 in range(2):
        for kv in range(NKV):
            for a in range(2):
                head = kv * GQ + 2 * a + g2
                out[g2, :, kv, a, :] = -np.float32(2.0 ** -(head + 1)) * dist
    return out.reshape(P, NKV, 2 * 2 * CHUNK)


def kernel(**inputs):
    import numpy as _np
    import concourse.bacc as _bacc
    from concourse import mybir as _mybir
    from concourse.bass_utils import run_bass_kernel_spmd as _run

    nc = _bacc.Bacc("TRN2", target_bir_lowering=False, num_devices=1)
    arrays, args = {}, []
    host = [(name, _np.ascontiguousarray(inputs[name])) for name in _INS]
    host += [("ident", _np.eye(P, dtype=_np.float32)), ("bias", alibi_bias())]
    for name, a in host:
        arrays[f"in_{name}_dram"] = a
        args.append(nc.dram_tensor(f"in_{name}_dram", a.shape, _mybir.dt.from_np(a.dtype),
                                   kind="ExternalInput").ap())
    args.append(nc.dram_tensor("out_0_dram", (1, L, D), _mybir.dt.float32, kind="ExternalOutput").ap())
    block_kernel(nc, *args)
    r = _run(nc, [arrays], core_ids=[0])
    return r.results[0]["out_0_dram"]
```

```python
import math
from contextlib import ExitStack

import numpy as np
import concourse.bass as bass
from concourse import mybir

F32 = mybir.dt.float32
F32R = mybir.dt.float32r
I32 = mybir.dt.int32
ALU = mybir.AluOpType
ACT = mybir.ActivationFunctionType
AX = mybir.AxisListType

P = 128
D = 1024
L = 1024
F = 2816
KD = D // P
HALF = 512
NCH = F // P // 2
HD = 64
NKV = 2
GQ = 4
CHUNK = 64
DA = 512
DS = 512
NG = 32
GH = 16
NS = 64
NJ = NG // 2
T = P // GH
NC = L // T
EPS = 1e-6

WS = 3
RS = 2
HTMP = 4

UNITS_FFN = 6 * NCH
U_FF1 = 0
U_IN = U_FF1 + UNITS_FFN
N_IN = 10
U_GLU = U_IN + N_IN
N_GLU = 2
U_OUT = U_GLU + N_GLU
OUT_COLS = list(range(KD)) + list(range(3, KD))
N_OUT = len(OUT_COLS)
U_FF2 = U_OUT + N_OUT
N_UNITS = U_FF2 + UNITS_FFN

UNIT_DMAS = [1] * N_UNITS
for _u in range(U_IN + 6, U_IN + N_IN):
    UNIT_DMAS[_u] = 2
for _u in range(U_OUT, U_OUT + N_OUT):
    UNIT_DMAS[_u] = 3


def loads_until(unit):
    return 16 * sum(UNIT_DMAS[u] for u in range(unit % RS, unit + 1, RS))


NORM_TILES = [KD, KD, DA // P, DS // P, KD, KD]
N_FF1, N_MIX, N_ATT, N_SSM, N_FF2, N_END = range(6)


def squares_before(norm):
    return sum(2 * t for t in NORM_TILES[1:norm])


def adds_before(norm):
    return sum(2 * (t - 1) for t in NORM_TILES[1:norm])


def sums_before(norm):
    return 2 * (norm - 1)


NORMED = [N_FF1, N_MIX, N_ATT, N_SSM, N_FF2]


def norm_order(norm):
    kt = NORM_TILES[norm]
    sq = [("S", i) for i in range(2 * kt)]
    ap = [("A", i) for i in range(2 * kt)]
    if norm == N_FF1:
        return [("R", 0)] + ap[:kt] + [("R", 1)] + ap[kt:]
    if norm == N_END:
        return sq[:10] + [("R", 0)] + sq[10:] + [("R", 1)]
    first = 10 if norm == N_MIX else LAST_IN_0 + 2
    out = sq[:first] + [("R", 0)]
    for i in range(2 * kt - first):
        out += [ap[i], sq[first + i]]
    return out + ap[2 * kt - first:kt] + [("R", 1)] + ap[kt:]


def steps(text):
    return [(s[0], int(s[1])) for s in text.split()]


MIXER_PE = steps("S0 K0 S1 K1 K2 K3 E0 S2 E1 T0 E2 E3 K4 K5 V0 E4 E5 S3 E6 K6 E7 T1 K7 I0 S4 T2 I1 S5 V1 I2 V2 T3 "
    "Y0 S6 I3 T4 V3 Y1 Y2 T5 S7 V4 Y3 V5 T6 V6 T7 V7")
MIXER_ACT = steps("k0 X0 k1 k2 X1 k3 e0 e1 C0 e2 k4 e3 k5 X2 O0 e4 e5 e6 e7 k6 k7 C1 X3 X4 O1 C2 y0 C3 O2 X5 g0 C4 "
    "y1 O3 X6 y2 O4 C5 X7 y3 g1 O5 C6 g2 O6 C7 g3 O7")
MIXER_DVE = steps("A0 d0 A1 d1 d2 B0 d3 B1 A2 d4 d5 d6 A3 d7 B2 R0 A4 R1 B3 R2 A5 B4 R3 A6 B5 A7 z0 B6 B7 z1 z2 z3")
ROUND = [(step, i) for step in MIXER_PE if step[0] in "KEIY" for i in range(1 if step[0] in "KE" else 2)]


def round_bank(kind, b, i=0):
    return 5 + ROUND.index(((kind, b), i)) % 3


GATED = ([("S", N_ATT, i) for i in range(4)] + [("G", 0), ("S", N_ATT, 4), ("S", N_ATT, 5), ("G", 1)]
         + [("S", N_ATT, 6), ("S", N_ATT, 7), ("G", 2), ("R", N_ATT, 0), ("G", 3), ("G", 4)]
         + [("A", N_ATT, i) for i in range(4)] + [("W", 1), ("G", 5), ("G", 6), ("R", N_ATT, 1)]
         + [("S", N_SSM, i) for i in range(4)] + [("G", 7)] + [("A", N_ATT, i) for i in range(4, 8)]
         + [("S", N_SSM, 4), ("S", N_SSM, 5), ("R", N_SSM, 0), ("S", N_SSM, 6), ("S", N_SSM, 7), ("W", 2)]
         + [("A", N_SSM, i) for i in range(4)] + [("R", N_SSM, 1)]
         + [("A", N_SSM, i) for i in range(4, 8)])

OUT_ORDER = [(n, 0) for n in range(3)] + [(n, 1) for n in range(3)] + [(n, h) for h in range(2) for n in range(3, KD)]
OUT_BANK = [0, 1, 2, 4, 5, 6]
LAST_IN_0 = max(i for i, (n, h) in enumerate(OUT_ORDER) if h == 0)


def out_unit(i):
    return i if i < 3 else i - 3


def half_and_tile(norm, i):
    if norm == N_FF2:
        return OUT_ORDER[i][1], OUT_ORDER[i][0]
    return i // NORM_TILES[norm], i % NORM_TILES[norm]


def add_number(norm, i):
    begun = sum(half_and_tile(norm, n)[1] == 0 for n in range(i + 1))
    return adds_before(norm) + i - begun


LATE = (4,)

X_BANK = [0, 1, 2, 3, 4, 5, 6, 7] + [1, 2, 3, 4, 5, 6, 1, 2]

IN_ORDER = [(0, 0), (1, 0), (2, 0), (0, 1), (1, 1), (2, 1)] + [(n, h) for n in range(3, N_IN) for h in range(2)]
END_IN = [IN_ORDER.index((n, 1)) + 1 for n in range(N_IN)]
FIRST = [("G", 0, 0), ("G", 1, 0), ("U", 0, 0), ("G", 0, 1), ("G", 1, 1), ("U", 0, 1), ("U", 1, 0), ("U", 1, 1)]
FIRST_GATES = {0: 1, 2: 2, 1: 3, 3: 4}


def split_before(norm):
    return sum(2 * NORM_TILES[n] for n in NORMED if n < norm)


TWO_PI_1 = 6.28125
TWO_PI_2 = 0.00193500518798828125
TWO_PI_3 = 2 * math.pi - TWO_PI_1 - TWO_PI_2
LN2_1 = 0.693359375
LN2_2 = math.log(2.0) - LN2_1
MAGIC = 1.5 * 2 ** 23

LINKS_PER_BATCH = 127
NORM_SCALE = [1 / D, 1 / D, 1 / DA, 0.25 / DS, 1 / D, 1 / D]
CONST_DMAS = 4 + 2 + 1 + 8 + 1


def src_of(tile, permuted):
    return tile.rearrange("p (t c) -> p t c", c=NC) if permuted else tile


def by_chunk(tile):
    return tile.rearrange("p (n q) -> p n q", q=CHUNK)


def att_tile(q, g, h):
    return q[:, h * 8:(h + 1) * 8, g, :]


def dst_of(tensor, k, h, permuted):
    if permuted:
        return tensor[:, k, :].rearrange("p (c t) -> p t c", t=T)[:, 4 * h:4 * h + 4, :]
    return tensor[:, k, h * HALF:(h + 1) * HALF]


def block_kernel(nc, x, ff1_norm, ff1_w_gate, ff1_w_up, ff1_w_down, mix_norm, w_in, sink, a_re, a_im,
                 b_re, b_im, c_re, c_im, d_skip, log_dt, w_glu, b_glu, attn_out_norm, ssm_out_norm,
                 w_out, ff2_norm, ff2_w_gate, ff2_w_up, ff2_w_down, final_norm, ident_c, bias_c, out):
    ctx = ExitStack()

    ctx.enter_context(nc.allow_non_contiguous_dma(reason="vectors of a few KB"))

    base = (nc.sbuf_base + 31) // 32 * 32
    KB = 1024

    def at(name, off, shape, dt=F32):
        return nc.alloc_sbuf_tensor_at(name, shape, dt, offset=base + off)

    a_x, a_h, a_w = 0, 32 * KB, 96 * KB
    a_a = a_w + 32 * KB
    a_t = a_a + 24 * KB
    a_s = a_t + 34 * KB

    xT = at("xT", a_x, [P, KD, L])
    hT_hi = at("hT_hi", a_h, [P, KD, L], F32R)
    hT_lo = at("hT_lo", a_h + 32 * KB, [P, KD, L], F32R)
    x_in = [at("x_in0", a_h + 32 * KB, [P, 4, D]), at("x_in1", a_w + 32 * KB, [P, 4, D])]
    w_hi = [at(f"w_hi{s}", a_w + 4 * KB * s, [P, 1024], F32R) for s in range(WS)]
    w_lo = [at(f"w_lo{s}", a_w + 12 * KB + 4 * KB * s, [P, 1024], F32R) for s in range(WS)]
    raw = [at(f"raw{s}", a_w + 24 * KB + 4 * KB * s, [P, 1024]) for s in range(RS)]
    aT_hi = at("aT_hi", a_a, [P, 4, HALF], F32R)
    aT_lo = at("aT_lo", a_a + 8 * KB, [P, 4, HALF], F32R)
    sg = at("sg", a_a + 16 * KB, [P, 4, HALF])
    htmps = [at("htmp0", a_t + 18 * KB, [P, HTMP, HALF]), at("htmp1", a_t, [P, HTMP, HALF])]
    dgts = [at("dgt0", a_t + 26 * KB, [P, 4, P]), at("dgt1", a_t + 8 * KB, [P, 4, P])]
    gend = at("gend", a_t + 10 * KB, [P, D])
    qT = at("qT", a_a, [P, L // CHUNK, GQ, CHUNK])
    kTp = at("kTp", a_a + 16 * KB, [P, CHUNK + L])
    CL = at("CL", a_t, [P, 2, NJ, (T + 1) * GH])
    Et = at("Et", a_t + 18 * KB, [P, NJ, 2, P])
    vTp = at("vTp", a_t + 18 * KB, [P, CHUNK + L])
    yT = at("yT", a_t + 18 * KB, [P, 4, L])
    u8 = at("u8", a_h, [P, NG, NC])
    Mt = at("Mt", a_h + 16 * KB, [P, NG, P])
    tr = at("tr", a_h + 32 * KB, [P, NJ, NC])
    ti = at("ti", a_h + 40 * KB, [P, NJ, NC])
    kst = at("kst", a_h + 16 * KB, [GH, NG, P])
    csn = at("csn", a_h + 48 * KB, [P, 2, NJ, NC])
    ebs = at("ebs", a_h + 32 * KB, [P, 2, NJ, P])
    off = [a_s]

    def small(name, shape, dt=F32):
        t = at(name, off[0], shape, dt)
        n = 4
        for s in shape[1:]:
            n *= s
        off[0] += (n + 31) // 32 * 32
        return t

    ident = small("ident", [P, P])
    ones = small("ones", [P, P])
    gains = small("gains", [P, 40])
    G_COL = {N_FF1: 0, N_MIX: 8, N_ATT: 16, N_SSM: 20, N_FF2: 24, N_END: 32}
    eps_t = small("eps_t", [P, 1])
    bglu = small("bglu", [P, 4])
    bglu_h = small("bglu_h", [P, 4])
    sinkt = small("sinkt", [P, 2, 2, 2])
    par = small("par", [P, 3, NJ])
    NPAR = 40
    pw = at("pw", a_t + 26 * KB, [P, NPAR, NJ])
    pwi = at("pwi", a_t + 29 * KB, [P, 2, NJ], I32)
    ivt = small("ivt", [P, 4, NJ])
    lam = small("lam", [P, 3, T + 1, NJ])
    rot8 = small("rot8", [P, 2, NJ])
    dec8 = small("dec8", [P, NJ])
    dsk = small("dsk", [GH, NG])
    zero = small("zero", [P, (T - 1) * GH])
    unit = small("unit", [P, 2, 4, 1])
    mark = small("mark", [P, 1])
    Bb = small("Bb", [P, 2, NJ, GH])
    std4 = small("std4", [P, 4])
    nv4 = small("nv4", [P, 4])
    nt4 = small("nt4", [P, 2, 4])
    ms4 = small("ms4", [P, 2, 4])
    rms4 = small("rms4", [P, 2, 4])
    mx = small("mx", [P, 8])
    nm = small("nm", [P, 2, 8])
    esk = small("esk", [P, 2, 8])
    ssum = small("ssum", [P, 2, 8])
    rden = small("rden", [P, 8])
    a_v = off[0]
    b_raw = at("b_raw", a_v, [P, 2, NJ, GH])
    c_in = at("c_in", a_t + 30 * KB, [P, 2, 4, 2, NS])
    CT = at("CT", a_v + 6 * KB, [P, 2, NJ, GH])
    ptmp = at("ptmp", a_v + 8 * KB, [P, 2, 256])
    EBb = at("EBb", a_v + 2 * KB, [P, 2, 4, P])
    ssq = at("ssq", a_v + 10 * KB, [P, L])
    sqt = at("sqt", a_v + 2 * KB, [P, 2, HALF])
    cur = at("cur", a_v, [P, 2, 4, GH + T + 1 + 1])
    bc_tmp = at("bc_tmp", a_v + 8 * KB, [P, 2, NJ, GH])
    gth = at("gth", a_v + 6 * KB, [P, 2, HALF])
    ust = [at(f"ust{i}", a_a + 4 * KB * i, [P, T, NC]) for i in range(3)]
    dgl = at("dgl", a_v + 12 * KB, [GH, NG, GH])
    vwin = at("vwin", a_v, [P, 2 * 8, P])
    biast = at("biast", a_a + 20 * KB + 512, [P, NKV, 256])
    sco = [at(f"sco{i}", a_w + 12 * KB * i, [P, 2, 2, 2, P]) for i in range(2)]
    pts = at("pts", a_w + 24 * KB, [P, 2, 2, 2, P])
    rtm = at("rtm", a_v + 8 * KB, [P, 2, HALF])
    btm = [at(f"btm{i}", a_w + o, [P, HALF]) for i, o in enumerate((8 * KB, 10 * KB, 20 * KB))]
    osb = at("osb", a_h, [P, KD, D])
    assert base + a_v + 14 * KB <= nc.sbuf_usable_end, (base + a_v + 14 * KB, nc.sbuf_usable_end)

    def htmp(norm, c):
        return htmps[norm >= N_ATT][:, c % HTMP, :]

    def dgt(norm):
        return dgts[norm >= N_ATT]

    bank = [ctx.enter_context(nc.psum_tensor(f"bank{i}", [P, HALF], F32)) for i in range(8)]

    u_d = nc.dram_tensor("u_scratch", (DS, T, NC), F32, kind="Internal").ap()
    y_d = nc.dram_tensor("y_scratch", (DS, T, NC), F32, kind="Internal").ap()
    eb_d = nc.dram_tensor("eb_scratch", (P, 2, NJ, P), F32, kind="Internal").ap()
    cs_d = nc.dram_tensor("cs_scratch", (P, 2, NJ, NC), F32, kind="Internal").ap()
    k_d = nc.dram_tensor("k_scratch", (NG, GH, (2 * T - 1) * GH), F32, kind="Internal").ap()

    def sem(name):
        return ctx.enter_context(nc.semaphore(name))

    x_loaded = [sem(f"x_loaded{t}") for t in range(KD)]
    consts_loaded = sem("consts_loaded")
    gain_loaded = sem("gain_loaded")
    x_squared = sem("x_squared")
    ident_loaded = sem("ident_loaded")
    params_loaded = sem("params_loaded")
    c_loaded = sem("c_loaded")
    consts_set = sem("consts_set")
    raw_loaded = [sem(f"raw_loaded{s}") for s in range(RS)]
    w_hi_done = sem("w_hi_done")
    w_lo_done = sem("w_lo_done")
    xt_done = sem("xt_done")
    xt_act = sem("xt_act")
    xt_dve = sem("xt_dve")
    sq_done = sem("sq_done")
    ssq_done = sem("ssq_done")
    sum_ready = sem("sum_ready")
    std_done = sem("std_done")
    rms_done = sem("rms_done")
    diag_done = sem("diag_done")
    rb_ready = sem("rb_ready")
    gend_loaded = sem("gend_loaded")
    h_tmp = sem("h_tmp")
    h_hi = sem("h_hi")
    h_lo_even = sem("h_lo_even")
    h_lo_odd = sem("h_lo_odd")
    ff_out = sem("ff_out")
    gate_taken = sem("gate_taken")
    up_taken = sem("up_taken")
    a_hi_done = sem("a_hi_done")
    a_lo_done = sem("a_lo_done")
    down_taken = sem("down_taken")
    ct_ready = sem("ct_ready")
    ct_taken = sem("ct_taken")
    prep_chain = sem("prep_chain")
    newton = sem("newton")
    inv_done = sem("inv_done")
    gains_set = sem("gains_set")
    pads_set = sem("pads_set")
    pool_chain = sem("pool_chain")
    eb_stored = sem("eb_stored")
    zero_stored = sem("zero_stored")
    proj_out = sem("proj_out")
    proj_taken = sem("proj_taken")
    u_stored = sem("u_stored")
    u8_loaded = sem("u8_loaded")
    eb_loaded = sem("eb_loaded")
    cs_loaded = sem("cs_loaded")
    bias_loaded = sem("bias_loaded")
    v_ready = sem("v_ready")
    v_taken = sem("v_taken")
    e_ready = sem("e_ready")
    e_taken = sem("e_taken")
    k_ready = sem("k_ready")
    k_taken = sem("k_taken")
    k_act = sem("k_act")
    diag_chain = sem("diag_chain")
    k_stored = sem("k_stored")
    m_loaded = sem("m_loaded")
    inj_ready = sem("inj_ready")
    inj_taken = sem("inj_taken")
    state_chain = sem("state_chain")
    scanned = sem("scanned")
    back_chain = sem("back_chain")
    state_done = sem("state_done")
    y_ready = sem("y_ready")
    y_taken = sem("y_taken")
    y_stored = sem("y_stored")
    yt_loaded = sem("yt_loaded")
    s_ready = sem("s_ready")
    s_biased = sem("s_biased")
    att_chain = sem("att_chain")
    max_done = sem("max_done")
    exp_done = sem("exp_done")
    p_done = sem("p_done")
    pt_ready = sem("pt_ready")
    pt_taken = sem("pt_taken")
    o_ready = sem("o_ready")
    o_taken = sem("o_taken")
    z_done = sem("z_done")
    z_hi = sem("z_hi")
    z_lo = sem("z_lo")
    glu_out = sem("glu_out")
    glu_tanh = sem("glu_tanh")
    glu_done = sem("glu_done")
    mix_out = sem("mix_out")
    mix_taken = sem("mix_taken")
    fin_ready = sem("fin_ready")
    fin_taken = sem("fin_taken")
    rows_scaled = sem("rows_scaled")
    out_stored = sem("out_stored")

    FF = {0: (ff1_w_gate, ff1_w_up, ff1_w_down), 1: (ff2_w_gate, ff2_w_up, ff2_w_down)}
    U_OF = (U_FF1, U_FF2)
    OUTS_FFN = 24 * NCH

    def wk(t, k):
        return t[:, k * P:(k + 1) * P]

    def hs(h):
        return slice(h * HALF, (h + 1) * HALF)

    def wait_lo(eng, tiles):
        eng.wait_ge(h_lo_even, (tiles + 1) // 2)
        if tiles >= 2:
            eng.wait_ge(h_lo_odd, tiles // 2)

    block = ctx.enter_context(nc.Block())

    @block.sync
    def _(sp):
        def load_unit(u, src, dst=None, wait=None):
            if wait is not None:
                sp.wait_ge(w_lo_done, wait)
            sp.dma_start(raw[u % RS][:, :] if dst is None else dst, src).then_inc(raw_loaded[u % RS], 16)

        def cols(w, f):
            return w.rearrange("(k p) f -> p k f", p=P)[:, :, f]

        def as3(u):
            return raw[u % RS][:, :].rearrange("p (k m) -> p k m", k=8)

        def gate_or_up(u, w, f, wait):
            load_unit(u, cols(w, bass.ds(f * P, P)), as3(u), wait)

        def down(u, w, f, wait):
            load_unit(u, w[bass.ds(f * P, P), :], None, wait)

        def ffn_loads(which, between=lambda n: None):
            wg, wu, wd = (w[0] for w in FF[which])
            b = U_OF[which]
            for n, (w, f) in enumerate(((wg, 0), (wg, 1), (wu, 0), (wu, 1))):
                gate_or_up(b + n, w, f, b + n - RS + 1 if b + n >= RS else None)
                between(n)
            with sp.Fori(0, NCH - 1) as i:
                b0 = b + 4
                for n, (w, f) in enumerate(((wg, 2), (wg, 3), (wd, 0), (wd, 1), (wu, 2), (wu, 3))):
                    wait = i * 6 + (b0 + n - RS + 1)
                    (down if w is wd else gate_or_up)(b0 + n, w, i * 2 + f, wait)
            for n in range(2):
                u = b + UNITS_FFN - 2 + n
                down(u, wd, 2 * (NCH - 1) + n, u - RS + 1)

        sp.dma_start(ident[:, :], ident_c).then_inc(ident_loaded, 16)
        def load_x(h):
            for t in range(4 * h, 4 * h + 4):
                sp.dma_start(x_in[h][:, t % 4, :], x[0, t * P:(t + 1) * P, :]).then_inc(x_loaded[t], 16)

        def small_loads():
            for col, g, kt in ((8, mix_norm[0], 8), (20, ssm_out_norm[0], 4),
                               (24, ff2_norm[0], 8), (32, final_norm, 8)):
                sp.dma_start(gains[:, col:col + kt], g.rearrange("(k p) -> p k", p=P)).then_inc(consts_loaded, 16)
            for kv in range(NKV):
                sp.dma_start(gains[kv * HD:(kv + 1) * HD, 16:20],
                              attn_out_norm[0][kv * 256:(kv + 1) * 256].rearrange("(g d) -> d g", d=HD)
                              ).then_inc(consts_loaded, 16)
            sp.dma_start(bglu[:, :], b_glu[0].rearrange("(k p) -> p k", p=P)).then_inc(consts_loaded, 16)
            for g2 in range(2):
                for nn in range(2):
                    for kv in range(NKV):
                        src = sink[0].rearrange("(v a g) -> g v a", v=2, g=2)[g2, kv].partition_broadcast(HD)
                        sp.dma_start(sinkt[g2 * HD:(g2 + 1) * HD, kv, nn, :], src).then_inc(consts_loaded, 16)
            sp.dma_start(dsk[:, :], d_skip[0].rearrange("(g h) -> h g", h=GH)).then_inc(consts_loaded, 16)
            for n, a in enumerate((a_re, a_im)):
                for g2 in range(2):
                    sp.dma_start(par[g2 * NS:(g2 + 1) * NS, n, :],
                                  a[0].rearrange("(j g) p -> g p j", g=2)[g2]).then_inc(params_loaded, 16)
            for g2 in range(2):
                sp.dma_start(par[g2 * NS:(g2 + 1) * NS, 2, :],
                              log_dt[0].rearrange("(j g) -> g j", g=2)[g2].partition_broadcast(NS)
                              ).then_inc(params_loaded, 16)
            for n, b in enumerate((b_re, b_im)):
                for g2 in range(2):
                    sp.dma_start(b_raw[g2 * NS:(g2 + 1) * NS, n, :, :],
                                  b[0].rearrange("(j g) p h -> g p j h", g=2)[g2]).then_inc(params_loaded, 16)
            for n, c in enumerate((c_re, c_im)):
                for a in range(2):
                    sp.dma_start(c_in[:, n, :, a, :],
                                  c[0].rearrange("(i g) h p -> (g h) i p", g=8)).then_inc(c_loaded, 16)

        def among(n):
            if n == 0:
                load_x(1)
            elif n == 2:
                small_loads()

        load_x(0)
        sp.dma_start(gains[:, 0:8], ff1_norm[0].rearrange("(k p) -> p k", p=P)).then_inc(gain_loaded, 16)
        ffn_loads(0, among)

        w = w_in[0]
        for n in range(N_IN):
            u = U_IN + n
            if n < 4:
                load_unit(u, cols(w, slice(768 + n * P, 768 + (n + 1) * P)), as3(u), u - RS + 1)
            elif n < 6:
                load_unit(u, cols(w, slice(512 + (n - 4) * P, 512 + (n - 3) * P)), as3(u), u - RS + 1)
            else:
                sp.wait_ge(w_lo_done, u - RS + 1)
                for kv in range(NKV):
                    c0 = kv * GQ * HD + (n - 6) * HD
                    sp.dma_start(as3(u)[:, :, kv * HD:(kv + 1) * HD],
                                 cols(w, slice(c0, c0 + HD))).then_inc(raw_loaded[u % RS], 16)
            if n == 3:
                sp.wait_ge(proj_out, 1)
                sp.dma_start(biast[:, :, :], bias_c).then_inc(bias_loaded, 16)
            if n >= 4 and n < 8:
                i = n - 4
                sp.wait_ge(proj_taken, END_IN[i])
                sp.dma_start(u_d[i * P:(i + 1) * P, :, :], ust[i % 3][:, :, :]).then_inc(u_stored, 16)
        for n in range(N_GLU):
            u = U_GLU + n
            load_unit(u, cols(w_glu[0], slice(n * 256, (n + 1) * 256)),
                      raw[u % RS][:, :].rearrange("p (k m) -> p k m", k=4), u - RS + 1)
        def load_out_unit(n):
            u = U_OUT + n
            n = OUT_COLS[n]
            sp.wait_ge(w_lo_done, u - RS + 1)
            for kv in range(NKV):
                src = w_out[0][kv * GQ * HD:(kv + 1) * GQ * HD, n * P:(n + 1) * P]
                sp.dma_start(as3(u)[kv * HD:(kv + 1) * HD, 0:4, :],
                             src.rearrange("(g d) m -> d g m", d=HD)).then_inc(raw_loaded[u % RS], 16)
            sp.dma_start(as3(u)[:, 4:8, :],
                         w_out[0][DA:, n * P:(n + 1) * P].rearrange("(k p) m -> p k m", p=P)
                         ).then_inc(raw_loaded[u % RS], 16)

        sp.wait_ge(proj_out, 2 * N_IN)
        sp.wait_ge(eb_stored, 4 * 32)
        sp.dma_start(ebs[:, :, :, :], eb_d).then_inc(eb_loaded, 16)
        sp.wait_ge(u_stored, 64)
        u_v = u_d.rearrange("(g h) t c -> t h g c", h=GH)
        for t in range(T):
            sp.dma_start(u8[t * GH:(t + 1) * GH, :, :], u_v[t]).then_inc(u8_loaded, 16)
        sp.dma_start(csn[:, :, :, :], cs_d).then_inc(cs_loaded, 16)
        sp.wait_ge(k_taken, 8)
        sp.wait_ge(zero_stored, 64)
        sp.dma_start(k_d.rearrange("g h c -> h g c")[:, :, (T - 1) * GH:], kst[:, :, :]).then_inc(k_stored, 16)
        sp.wait_ge(k_stored, 16)
        for t in range(T):
            c0 = (T - 1 - t) * GH
            sp.dma_start(Mt[t * GH:(t + 1) * GH, :, :],
                         k_d.rearrange("g h c -> h g c")[:, :, c0:c0 + P]).then_inc(m_loaded, 16)
        y_v = y_d.rearrange("(g h) t c -> t h g c", h=GH)
        for b in range(4):
            gs = slice(8 * b, 8 * b + 8)
            sp.wait_ge(y_taken, 2 * b + 2)
            for t in range(T):
                sp.dma_start(y_v[t][:, gs], u8[t * GH:(t + 1) * GH, gs, :]).then_inc(y_stored, 16)
            if b == 0:
                sp.wait_ge(inj_ready, 4)
            sp.wait_ge(y_stored, 16 * T * (b + 1))
            sp.dma_start(yT[:, b, :].rearrange("p (t c) -> p t c", t=T),
                         y_d[b * P:(b + 1) * P, :, :]).then_inc(yt_loaded, 16)
        sp.wait_ge(o_ready, 8)
        for n in range(N_OUT):
            load_out_unit(n)
        sp.wait_ge(y_ready, 8)
        sp.dma_start(gend[:, :], final_norm.partition_broadcast(P)).then_inc(gend_loaded, 16)
        ffn_loads(1)
        for t in range(KD):
            sp.wait_ge(fin_taken, 2 * t + 2)
            if t in LATE:
                sp.wait_ge(rows_scaled, LATE.index(t) + 1)
            sp.dma_start(out[0, t * P:(t + 1) * P, :], osb[:, t, :]).then_inc(out_stored, 16)
        sp.wait_ge(out_stored, 16 * KD)

    @block.tensor
    def _(pe):
        def mm3(o, wh, wl, rh, rl, first, last):
            nc.tensor.matmul(o, wl, rh, start=first, stop=False)
            nc.tensor.matmul(o, wh, rl, start=False, stop=False)
            return nc.tensor.matmul(o, wh, rh, start=False, stop=last)

        def norm_sum(norm, h):
            kt = NORM_TILES[norm]
            last = max(i for i in range(2 * kt) if half_and_tile(norm, i)[0] == h)
            pe.wait_ge(ssq_done, add_number(norm, last) + 1)
            before = split_before(norm) + (h * kt if norm != N_END else 0)
            if before:
                pe.wait_ge(h_tmp, before)
            if norm == N_END and h:
                pe.wait_ge(rms_done, 2 * norm + 1)
            for i in range(4):
                last = nc.tensor.matmul(bank[7][:, i:i + 1], ssq[:, h * HALF + i * P:h * HALF + (i + 1) * P],
                                        ones[:, 0:1], start=True, stop=True)
            last.then_inc(sum_ready, 1)

        def norm_spread(norm, h):
            pe.wait_ge(diag_done, 2 * norm + h + 1)
            nc.tensor.matmul(bank[7][:, :], ones[:, :], dgt(norm)[:, :, :].rearrange("p a b -> p (a b)"),
                             start=True, stop=True).then_inc(rb_ready, 1)

        def half_unit(unit_count, slot, h, o, waits, done, tiles=None):
            for s, v in waits:
                pe.wait_ge(s, v)
            pe.wait_ge(w_lo_done, unit_count)
            for k in range(KD):
                if tiles is not None:
                    wait_lo(pe, tiles(k))
                last = mm3(o, wk(w_hi[slot], k), wk(w_lo[slot], k), hT_hi[:, k, hs(h)], hT_lo[:, k, hs(h)],
                           k == 0, k == KD - 1)
            last.then_inc(done, 1)

        def wide_unit(unit_count, slot, banks, waits, done):
            for h in range(2):
                half_unit(unit_count, slot, h, bank[banks[h]][:, :], waits[h], done)

        def ffn(which, norm, between, after):
            b = U_OF[which]
            g0 = 4 * NCH * which
            d0 = 16 * NCH * which
            seen = set()
            for n, (kind, f, h) in enumerate(FIRST):
                u = b + f + (2 if kind == "U" else 0)
                waits = [(gate_taken, g0 + FIRST_GATES[2 * f + h])] if kind == "U" else []
                tiles = None
                if h not in seen:
                    seen.add(h)
                    tiles = lambda k, h=h: split_before(norm) + h * KD + k + 1
                half_unit(u + 1, u % WS, h, bank[2 * f + h][:, :], waits, ff_out, tiles)
                between(n)

            def down(units_ready, slots, a_ready, d_base, after=lambda n: None):
                pe.wait_ge(w_lo_done, units_ready)
                pe.wait_ge(a_lo_done, a_ready - 1)
                for n in range(16):
                    d, h = n % KD, n // KD
                    if n == KD:
                        pe.wait_ge(a_lo_done, a_ready)
                    if n >= 3:
                        pe.wait_ge(down_taken, d_base + (n - 2))
                    o = bank[4 + n % 3][:, :]
                    for f in range(2):
                        last = mm3(o, wk(w_hi[slots[f]], d), wk(w_lo[slots[f]], d),
                                   aT_hi[:, 2 * f + h, :], aT_lo[:, 2 * f + h, :], f == 0, f == 1)
                    last.then_inc(ff_out, 1)
                    after(n)

            def body(i, dbase):
                ub = b + 4
                for f in range(2):
                    waits = [[(up_taken, i * 4 + (g0 + 2 * f + h + 1))] for h in range(2)]
                    wide_unit(i * 6 + (ub + f + 1), (ub + f) % WS, (2 * f, 2 * f + 1), waits, ff_out)
                down(i * 6 + (ub + 4), ((ub + 2) % WS, (ub + 3) % WS), i * 4 + (g0 + 4), dbase)
                for f in range(2):
                    waits = [[(gate_taken, i * 4 + (g0 + 4 + 2 * f + h + 1))] for h in range(2)]
                    wide_unit(i * 6 + (ub + 4 + f + 1), (ub + 4 + f) % WS, (2 * f, 2 * f + 1), waits, ff_out)

            with pe.Fori(0, NCH - 1) as i:
                body(i, i * 16 + d0)
            u = b + UNITS_FFN - 2
            down(u + 2, (u % WS, (u + 1) % WS), g0 + 4 * NCH, d0 + 16 * (NCH - 1), after)

        pe.wait_ge(ident_loaded, 16)
        def x_tiles(h):
            for t in range(4 * h, 4 * h + 4):
                pe.wait_ge(x_loaded[t], 16)
                for kh in range(2):
                    if t == 7:
                        pe.wait_ge((xt_act, xt_dve)[kh], 5)
                    for kk in range(4):
                        k = 4 * kh + kk
                        last = nc.tensor.transpose(bank[X_BANK[2 * t + kh]][:, kk * P:(kk + 1) * P],
                                                   x_in[h][:, t % 4, k * P:(k + 1) * P], ident[:, :])
                    last.then_inc(xt_done, 1)

        def c_tiles():
            pe.wait_ge(c_loaded, 64)
            for ri in range(2):
                for i in range(4):
                    last = nc.tensor.transpose(bank[4 + ri][:, i * P:(i + 1) * P],
                                               c_in[:, ri, i, :, :].rearrange("p a s -> p (a s)"), ident[:, :])
                last.then_inc(ct_ready, 1)

        def second_half(norm):
            def between(n):
                if n == 0:
                    norm_sum(norm, 1)
                elif n == 1:
                    norm_spread(norm, 1)
            return between

        def first_half(norm):
            def after(n):
                if n == 9:
                    norm_sum(norm, 0)
                elif n == 11:
                    norm_spread(norm, 0)
            return after

        x_tiles(0)
        pe.wait_ge(consts_set, 1)
        pe.wait_ge(xt_dve, 4)
        norm_spread(N_FF1, 0)

        def start(n):
            if n == 0:
                x_tiles(1)
                pe.wait_ge(xt_act, 8)
                pe.wait_ge(xt_dve, 8)
                pe.wait_ge(h_tmp, KD)
            elif n == 1:
                norm_spread(N_FF1, 1)
            elif n == 5:
                c_tiles()

        ffn(0, N_FF1, start, first_half(N_MIX))

        seen = set()
        for o, (n, h) in enumerate(IN_ORDER):
            u = U_IN + n
            waits = [(proj_taken, o - 3)] if o >= 4 else []
            if o == 0:
                waits = [(up_taken, 4 * NCH)]
            tiles = None
            if h not in seen:
                seen.add(h)
                tiles = lambda k, h=h: split_before(N_MIX) + h * KD + k + 1
            half_unit(u + 1, u % WS, h, bank[o % 4][:, :], waits, proj_out, tiles)
            second_half(N_MIX)(o)
            if 13 <= o < 17:
                b = o - 13
                pe.wait_ge(proj_taken, END_IN[5])
                pe.wait_ge(pads_set, 1)
                for m in range(4):
                    n = 4 * b + m
                    last = nc.tensor.transpose(bank[4 + b][:, m * P:(m + 1) * P],
                                               vTp[:, CHUNK * n:CHUNK * n + P], ident[:, :])
                last.then_inc(v_ready, 1)

        def round_free(kind, b, i=0):
            n = ROUND.index(((kind, b), i))
            if n < 3:
                pe.wait_ge(v_taken, 4)
                return
            (kind, b), i = ROUND[n - 3]
            if kind == "K":
                pe.wait_ge(k_taken, b + 1)
            elif kind == "E":
                pe.wait_ge(e_taken, b + 1)
            elif kind == "I":
                pe.wait_ge(inj_taken, b + 1)
            else:
                pe.wait_ge(y_taken, 2 * b + i + 1)

        def blocks_k(b):
            j0, g2 = 4 * (b // 2), b % 2
            r = slice(g2 * NS, (g2 + 1) * NS)
            round_free("K", b)
            for jj in range(4):
                for ri in range(2):
                    last = nc.tensor.matmul(bank[round_bank("K", b)][0:GH, jj * P:(jj + 1) * P],
                                            Bb[r, ri, j0 + jj, :], CL[r, ri, j0 + jj, 0:P],
                                            start=ri == 0, stop=ri == 1)
            last.then_inc(k_ready, 1)

        def transposes_e(b):
            pe.wait_ge(eb_loaded, 16)
            round_free("E", b)
            for jj in range(2):
                for ri in range(2):
                    m = 2 * jj + ri
                    last = nc.tensor.transpose(bank[round_bank("E", b)][:, m * P:(m + 1) * P],
                                               ebs[:, ri, 2 * b + jj, :], ident[:, :])
            last.then_inc(e_ready, 1)

        def inject(b):
            pe.wait_ge(e_taken, 2 * b + 2)
            pe.wait_ge(u8_loaded, 16 * T)
            for ri in range(2):
                round_free("I", b, ri)
                for jj in range(4):
                    j = 4 * b + jj
                    for g2 in range(2):
                        last = nc.tensor.matmul(
                            bank[round_bank("I", b, ri)][g2 * NS:(g2 + 1) * NS, jj * P:(jj + 1) * P],
                            Et[:, j, ri, g2 * NS:(g2 + 1) * NS], u8[:, 2 * j + g2, :], start=True, stop=True)
            last.then_inc(inj_ready, 1)

        def outputs_y(b):
            pe.wait_ge(m_loaded, 16 * T)
            pe.wait_ge(state_done, b + 1)
            for g2 in range(2):
                round_free("Y", b, g2)
                for jj in range(4):
                    j = 4 * b + jj
                    g = 2 * j + g2
                    r = slice(g2 * NS, (g2 + 1) * NS)
                    o = bank[round_bank("Y", b, g2)][:, jj * P:(jj + 1) * P]
                    nc.tensor.matmul(o, Mt[:, g, :], u8[:, g, :], start=True, stop=False)
                    nc.tensor.matmul(o, CL[r, 0, j, GH:], tr[r, j, :], start=False, stop=False)
                    last = nc.tensor.matmul(o, CL[r, 1, j, GH:], ti[r, j, :], start=False, stop=True)
                last.then_inc(y_ready, 1)

        def scores(m):
            for kv in range(NKV):
                if m:
                    pe.wait_ge(s_biased, 2 * m + kv - 1)
                else:
                    pe.wait_ge(proj_taken, 2 * N_IN)
                r = slice(kv * HD, (kv + 1) * HD)
                for nn in range(2):
                    n = 2 * m + nn
                    for a in range(2):
                        o = bank[kv][:, (2 * nn + a) * P:(2 * nn + a + 1) * P]
                        last = nc.tensor.matmul(o, qT[r, n, 2 * a:2 * a + 2, :].rearrange("p g q -> p (g q)"),
                                                kTp[r, n * CHUNK:n * CHUNK + P], start=True, stop=True)
                last.then_inc(s_ready, 1)

        def transposes_p(m):
            pe.wait_ge(p_done, m + 1)
            if m:
                pe.wait_ge(pt_taken, 2 * m)
            for kv in range(NKV):
                for nn in range(2):
                    for a in range(2):
                        o = bank[2 + kv][:, (2 * nn + a) * P:(2 * nn + a + 1) * P]
                        last = nc.tensor.transpose(o, sco[m % 2][:, kv, nn, a, :], ident[:, :])
                last.then_inc(pt_ready, 1)

        def weighted(m):
            pe.wait_ge(v_taken, 4)
            if m:
                pe.wait_ge(o_taken, m)
            pe.wait_ge(pt_taken, 2 * m + 2)
            for nn in range(2):
                for kv in range(NKV):
                    last = nc.tensor.matmul(bank[4][kv * HD:(kv + 1) * HD, nn * 256:(nn + 1) * 256],
                                            vwin[:, 2 * m + nn, kv * HD:(kv + 1) * HD],
                                            pts[:, kv, nn, :, :].rearrange("p a q -> p (a q)"),
                                            start=True, stop=True)
            last.then_inc(o_ready, 1)

        step = {"K": blocks_k, "E": transposes_e, "I": inject, "Y": outputs_y,
                "S": scores, "T": transposes_p, "V": weighted}
        for kind, b in MIXER_PE:
            step[kind](b)

        def glu(o):
            n, mm, h = o // 4, o // 2 % 2, o % 2
            u = U_GLU + n
            pe.wait_ge(w_lo_done, u + 1)
            if o == 0:
                pe.wait_ge(s_biased, 16)
                pe.wait_ge(y_taken, 8)
            if o >= 4:
                pe.wait_ge(glu_tanh, o - 3)
            for k in range(4):
                pe.wait_ge(z_lo, 2 * k + 2)
                c0 = k * 256 + mm * P
                last = mm3(bank[o % 4][:, :], w_hi[u % WS][:, c0:c0 + P], w_lo[u % WS][:, c0:c0 + P],
                           hT_hi[:, 4 + k, hs(h)], hT_lo[:, 4 + k, hs(h)], k == 0, k == 3)
            last.then_inc(glu_out, 1)

        def out_part(i, ks):
            (_, h), u = OUT_ORDER[i], U_OUT + out_unit(i)
            pe.wait_ge(w_lo_done, u + 1)
            if i < 3:
                pe.wait_ge(glu_tanh, i + 5)
            for k in ks:
                if k < 4:
                    wait_lo(pe, split_before(N_ATT) + 4 * h + k + 1)
                else:
                    wait_lo(pe, split_before(N_FF2))
                last = mm3(bank[OUT_BANK[i]][:, :], wk(w_hi[u % WS], k), wk(w_lo[u % WS], k),
                           hT_hi[:, k, hs(h)], hT_lo[:, k, hs(h)], k == 0, k == KD - 1)
            return last

        for o in range(8):
            glu(o)
            if o == 2 or o == 6:
                norm_sum(N_ATT, o // 6)
            elif o == 4 or o == 7:
                norm_spread(N_ATT, o // 7)
        pe.wait_ge(o_taken, 8)
        out_part(0, range(4))
        norm_sum(N_SSM, 0)
        out_part(1, range(4))
        norm_spread(N_SSM, 0)
        out_part(3, range(4))
        norm_sum(N_SSM, 1)
        out_part(4, range(4))
        norm_spread(N_SSM, 1)
        out_part(2, range(4))
        out_part(5, range(4))
        for i in range(2 * KD):
            u, h = U_OUT + out_unit(i), OUT_ORDER[i][1]
            if i < 6:
                out_part(i, range(4, KD)).then_inc(mix_out, 1)
                continue
            half_unit(u + 1, u % WS, h, bank[OUT_BANK[i % 6]][:, :], [(mix_taken, i - 5)], mix_out)
            if i == LAST_IN_0 + 1:
                norm_sum(N_FF2, 0)
            elif i == LAST_IN_0 + 2:
                norm_spread(N_FF2, 0)

        def out_tile(t):
            pe.wait_ge(down_taken, 32 * NCH - 8 + 8 * (t // 4))
            for kh in range(2):
                if t >= 2:
                    pe.wait_ge(fin_taken, 2 * t + kh - 3)
                for kk in range(4):
                    k = 4 * kh + kk
                    last = nc.tensor.transpose(bank[2 * (t % 2) + kh][:, kk * P:(kk + 1) * P],
                                               xT[:, k, t * P:(t + 1) * P], ident[:, :])
                last.then_inc(fin_ready, 1)

        def finish(n):
            if n == 9:
                norm_sum(N_END, 0)
            elif n in (11, 13, 15):
                out_tile((n - 11) // 2)

        ffn(1, N_FF2, second_half(N_FF2), finish)
        out_tile(3)
        out_tile(4)
        norm_sum(N_END, 1)
        for t in range(5, KD):
            out_tile(t)

    @block.scalar
    def _(act):
        def split_hi(u, wait_out, raw_value):
            act.wait_ge(raw_loaded[u % RS], raw_value)
            for s, v in wait_out:
                act.wait_ge(s, v)
            act.activation(w_hi[u % WS][:, :], raw[u % RS][:, :], ACT.Copy).then_inc(w_hi_done, 1)

        def square(norm, n, src, as_src=lambda v: v):
            h, k = half_and_tile(norm, n)
            if k == 0:
                if sums_before(norm):
                    act.wait_ge(sum_ready, sums_before(norm))
                dst = ssq[:, hs(h)]
            else:
                a = add_number(norm, n)
                if a >= 2:
                    act.wait_ge(ssq_done, a - 1)
                dst = sqt[:, a % 2, :]
            act.activation(as_src(dst), src, ACT.Square).then_inc(sq_done, 1)

        def norm_std(norm, h):
            if norm == N_FF1:
                act.wait_ge(x_squared, 4 * h + 4)
                src = ms4[:, h, :]
            else:
                act.wait_ge(sum_ready, sums_before(norm) + h + 1)
                src = bank[7][:, 0:4]
            act.activation(std4[:, :], src, ACT.Sqrt, bias=eps_t[:, 0:1],
                           scale=NORM_SCALE[norm]).then_inc(std_done, 1)

        def norm_hi(norm, i, tile0=0, permuted=False):
            c = split_before(norm) + i
            h, k = i // NORM_TILES[norm], i % NORM_TILES[norm]
            act.wait_ge(h_tmp, c + 1)
            act.activation(dst_of(hT_hi, tile0 + k, h, permuted), src_of(htmp(norm, c), permuted),
                           ACT.Copy).then_inc(h_hi, 1)

        def ffn(which, during=lambda: None):
            b = U_OF[which]
            o0 = OUTS_FFN * which
            g0 = 4 * NCH * which

            def take_gate(i4, bnk, ob):
                act.wait_ge(ff_out, ob)
                if not (isinstance(i4, int) and i4 == 0):
                    act.wait_ge(a_lo_done, i4 - 4 + bnk + 1)
                act.activation(sg[:, bnk, :], bank[bnk][:, :], ACT.Silu).then_inc(gate_taken, 1)

            def a_hi(i4, bnk):
                act.wait_ge(up_taken, i4 + bnk + 1)
                act.activation(aT_hi[:, bnk, :], sg[:, bnk, :], ACT.Copy).then_inc(a_hi_done, 1)

            def split(off_u, i, ob):
                u = b + off_u
                split_hi(u, [(ff_out, ob)], i * 48 + loads_until(u))

            for n, (kind, f, h) in enumerate(FIRST):
                if kind == "G":
                    if n:
                        take_gate(g0, 2 * f + h, o0 + n + 1)
                    if (f, h) == (0, 1):
                        split_hi(b + 3, [(ff_out, o0 + 4)], loads_until(b + 3))
                    if (f, h) == (1, 1):
                        split_hi(b + 4, [(ff_out, o0 + 5)], loads_until(b + 4))
            a_hi(g0, 0)
            split_hi(b + 5, [(ff_out, o0 + 6)], loads_until(b + 5))
            during()
            for n in range(1, 4):
                a_hi(g0, n)

            with act.Fori(0, NCH - 1) as i:
                ob = i * 24 + (o0 + 8)
                i4 = i * 4 + (g0 + 4)
                split(6, i, ob)
                for h in range(2):
                    take_gate(i4, h, ob + h + 1)
                split(7, i, ob + 2)
                for h in range(2):
                    take_gate(i4, 2 + h, ob + 2 + h + 1)
                split(8, i, ob + 4)
                split(9, i, ob + 20)
                split(10, i, ob + 20)
                for h in range(2):
                    a_hi(i4, h)
                split(11, i, ob + 22)
                for h in range(2):
                    a_hi(i4, 2 + h)

        def x_squares(h):
            for t in range(4 * h, 4 * h + 4):
                act.wait_ge(x_loaded[t], 16)
                if t:
                    act.wait_ge(x_squared, t)
                act.activation(sqt[:, :, :].rearrange("p a c -> p (a c)"), x_in[h][:, t % 4, :], ACT.Square,
                               accum_out=ms4[:, h, t % 4:t % 4 + 1]).then_inc(x_squared, 1)

        def x_out(h):
            for t in range(4 * h, 4 * h + 4):
                act.wait_ge(xt_done, 2 * t + 1)
                act.activation(xT[:, 0:4, t * P:(t + 1) * P],
                               bank[X_BANK[2 * t]][:, :].rearrange("p (k m) -> p k m", k=4), ACT.Copy
                               ).then_inc(xt_act, 1)


        def c_out():
            for ri in range(2):
                act.wait_ge(ct_ready, ri + 1)
                for g2 in range(2):
                    r = slice(g2 * NS, (g2 + 1) * NS)
                    src = bank[4 + ri][r, :].rearrange("p (j g h) -> p g j h", g=2, h=GH)[:, g2]
                    act.activation(CT[r, ri, :, :], src, ACT.Copy).then_inc(ct_taken, 1)

        def first_gate(o0, g0):
            act.wait_ge(ff_out, o0 + 1)
            if g0:
                act.wait_ge(a_lo_done, g0)
            act.activation(sg[:, 0, :], bank[0][:, :], ACT.Silu).then_inc(gate_taken, 1)

        act.wait_ge(consts_set, 1)
        for kind, i in norm_order(N_FF1):
            if kind == "R":
                x_squares(i)
                norm_std(N_FF1, i)
                x_out(i)
                if i == 0:
                    split_hi(0, [], loads_until(0))
                else:
                    first_gate(0, 0)
                    split_hi(2, [], loads_until(2))
            else:
                norm_hi(N_FF1, i)
                if i == 7:
                    split_hi(1, [], loads_until(1))
        ffn(0, c_out)

        def down_src(base):
            def src(i):
                act.wait_ge(down_taken, base + i + 1)
                return (xT[:, i % KD, hs(i // KD)],)
            return src

        split_hi(U_IN, [(ff_out, OUTS_FFN - 16)], loads_until(U_IN))
        act.wait_ge(eb_stored, 4 * 32)
        src = down_src(16 * (NCH - 1))
        for kind, i in norm_order(N_MIX):
            if kind == "S":
                square(N_MIX, i, *src(i))
            elif kind == "R":
                norm_std(N_MIX, i)
            else:
                norm_hi(N_MIX, i)
                if i == KD - 1:
                    for m in (1, 2):
                        split_hi(U_IN + m, [(ff_out, OUTS_FFN)], loads_until(U_IN + m))

        for o, (n, h) in enumerate(IN_ORDER):
            act.wait_ge(proj_out, o + 1)
            src = bank[o % 4][:, :]
            if n < 4:
                if n == 3:
                    act.wait_ge(u_stored, 16)
                dst = ust[n % 3][:, :, h * 64:(h + 1) * 64]
                src = src.rearrange("p (c t) -> p t c", t=T)
            elif n < 6:
                dst = (kTp, vTp)[n - 4][:, CHUNK + h * HALF:CHUNK + (h + 1) * HALF]
            else:
                if n == 6 and h == 0:
                    act.wait_ge(u_stored, 64)
                dst = att_tile(qT, n - 6, h)
                src = by_chunk(src)
            act.activation(dst, src, ACT.Copy).then_inc(proj_taken, 1)
            if o + 1 == END_IN[n] and n < N_IN - 2:
                nxt = U_IN + n + WS
                split_hi(nxt, [(proj_out, o + 1)], loads_until(nxt))

        def k_out(b):
            act.wait_ge(k_ready, b + 1)
            j0, g2 = 4 * (b // 2), b % 2
            dst = kst[:, :, :].rearrange("p (j g) m -> p g j m", g=2)[:, g2, j0:j0 + 4, GH:]
            src = bank[round_bank("K", b)][0:GH, :].rearrange("p (j m) -> p j m", j=4)[:, :, GH:]
            act.activation(dst, src, ACT.Copy).then_inc(k_act, 1)

        def e_out(b):
            act.wait_ge(e_ready, b + 1)
            act.activation(Et[:, 2 * b:2 * b + 2, :, :],
                           bank[round_bank("E", b)][:, :].rearrange("p (j r m) -> p j r m", j=2, r=2), ACT.Copy
                           ).then_inc(e_taken, 1)

        def y_out(b):
            for g2 in range(2):
                act.wait_ge(y_ready, 2 * b + g2 + 1)
                dst = u8[:, :, :].rearrange("p (j g) c -> p g j c", g=2)[:, g2, 4 * b:4 * b + 4, :]
                act.activation(dst, bank[round_bank("Y", b, g2)][:, :].rearrange("p (j c) -> p j c", j=4),
                               ACT.Copy).then_inc(y_taken, 1)

        def exponentials(m):
            act.wait_ge(max_done, m + 1)
            for s in range(8):
                kv, nn, a = s // 4, s // 2 % 2, s % 2
                v = sco[m % 2][:, kv, nn, a, :]
                act.activation(v, v, ACT.Exp, bias=nm[:, m % 2, s:s + 1], scale=1.0,
                               accum_out=ssum[:, m % 2, s:s + 1])
            act.activation(esk[:, m % 2, :], esk[:, m % 2, :], ACT.Exp).then_inc(exp_done, 1)

        def p_out(m):
            for kv in range(NKV):
                act.wait_ge(pt_ready, 2 * m + kv + 1)
                if m:
                    act.wait_ge(o_ready, m)
                act.activation(pts[:, kv, :, :, :].rearrange("p n a q -> p (n a q)"), bank[2 + kv][:, :],
                               ACT.Copy).then_inc(pt_taken, 1)

        def o_out(m):
            act.wait_ge(o_ready, m + 1)
            act.activation(qT[:, 2 * m:2 * m + 2, :, :].rearrange("p n g q -> p (n g q)"), bank[4][:, :], ACT.Copy
                           ).then_inc(o_taken, 1)

        def gelu(k):
            act.wait_ge(yt_loaded, 16 * k + 16)
            for h in range(2):
                act.activation(yT[:, k, hs(h)], yT[:, k, hs(h)], ACT.Gelu_apprx_tanh).then_inc(z_done, 1)
            for h in range(2):
                act.wait_ge(z_done, 2 * k + h + 1)
                act.activation(hT_hi[:, 4 + k, hs(h)], yT[:, k, hs(h)], ACT.Copy).then_inc(z_hi, 1)

        step = {"k": k_out, "e": e_out, "y": y_out, "X": exponentials, "C": p_out, "O": o_out, "g": gelu}
        for kind, b in MIXER_ACT:
            step[kind](b)

        split_hi(U_GLU + 1, [(state_done, 4)], loads_until(U_GLU + 1))
        split_hi(U_OUT, [(o_ready, 8)], loads_until(U_OUT))

        def glu_half_sigmoid(o):
            mt = o // 2
            act.wait_ge(glu_out, o + 1)
            if o >= 2:
                act.wait_ge(glu_done, o - 1)
            act.activation(gth[:, o % 2, :], bank[o % 4][:, :], ACT.Tanh, bias=bglu_h[:, mt:mt + 1],
                           scale=0.5).then_inc(glu_tanh, 1)

        for kind, *at_ in GATED:
            if kind == "G":
                glu_half_sigmoid(*at_)
            elif kind == "W":
                u = U_OUT + at_[0]
                split_hi(u, [(glu_out, 4 * at_[0])], loads_until(u))
            elif kind == "R":
                norm_std(*at_)
            elif kind == "A":
                ssm = at_[0] == N_SSM
                norm_hi(*at_, tile0=4 if ssm else 0, permuted=ssm)
            elif at_[0] == N_ATT:
                act.wait_ge(o_taken, 8)
                square(*at_, att_tile(qT, at_[1] % 4, at_[1] // 4), by_chunk)
            else:
                h, k = at_[1] // 4, at_[1] % 4
                act.wait_ge(glu_done, 2 * k + h + 1)
                square(*at_, yT[:, k, hs(h)])

        def mix_src(i):
            act.wait_ge(mix_taken, i + 1)
            h, k = half_and_tile(N_FF2, i)
            if i >= 3:
                nxt = U_OUT + i - 3 + WS
                split_hi(nxt, [(mix_out, i + 1)], loads_until(nxt))
            return (xT[:, k, hs(h)],)

        for kind, i in norm_order(N_FF2):
            if kind == "S":
                square(N_FF2, i, *mix_src(i))
            elif kind == "R":
                norm_std(N_FF2, i)
                if i == 1:
                    first_gate(OUTS_FFN, 4 * NCH)
            else:
                norm_hi(N_FF2, i)
        ffn(1)
        src = down_src(16 * (2 * NCH - 1))
        for kind, i in norm_order(N_END):
            if kind == "S":
                square(N_END, i, *src(i))
            else:
                norm_std(N_END, i)
        for t in LATE:
            act.wait_ge(fin_taken, 2 * t + 2)
            act.wait_ge(rms_done, 2 * N_END + 2)
            act.activation(osb[:, t, :], osb[:, t, :], ACT.Copy, scale=rms4[:, t // 4, t % 4:t % 4 + 1]
                           ).then_inc(rows_scaled, 1)

    @block.vector
    def _(dve):
        def split_lo(u, count):
            dve.wait_ge(w_hi_done, count)
            dve.tensor_tensor(w_lo[u % WS][:, :], raw[u % RS][:, :], w_hi[u % WS][:, :].bitcast(F32),
                              ALU.subtract).then_inc(w_lo_done, 1)

        def norm_rms(norm, h):
            r = rms4[:, h, :]
            n0 = 5 * (2 * norm + h)
            dve.wait_ge(std_done, 2 * norm + h + 1)
            dve.tensor_scalar(nv4[:, :], ms4[:, h, :] if norm == N_FF1 else bank[7][:, 0:4], NORM_SCALE[norm], EPS, ALU.mult, ALU.add
                              ).then_inc(newton, 1)
            dve.reciprocal(r, std4[:, :]).then_inc(newton, 1)
            dve.wait_ge(newton, n0 + 2)
            dve.tensor_tensor(nt4[:, 0, :], r, r, ALU.mult).then_inc(newton, 1)
            dve.wait_ge(newton, n0 + 3)
            dve.tensor_tensor(nt4[:, 1, :], nt4[:, 0, :], nv4[:, :], ALU.mult).then_inc(newton, 1)
            dve.wait_ge(newton, n0 + 4)
            dve.tensor_scalar(nt4[:, 0, :], nt4[:, 1, :], -0.5, 1.5, ALU.mult, ALU.add).then_inc(newton, 1)
            dve.wait_ge(newton, n0 + 5)
            dve.tensor_tensor(r, r, nt4[:, 0, :], ALU.mult).then_inc(rms_done, 1)
            dve.wait_ge(rms_done, 2 * norm + h + 1)
            if norm != N_END:
                dve.tensor_tensor(dgt(norm)[:, :, :], ident[:, :].unsqueeze(1).to_broadcast([P, 4, P]),
                                  r.unsqueeze(2).to_broadcast([P, 4, P]), ALU.mult).then_inc(diag_done, 1)

        def norm_scale(norm, i, src, v=lambda t: t):
            kt = NORM_TILES[norm]
            h, k = i // kt, i % kt
            c = split_before(norm) + i
            g = gains[:, G_COL[norm] + k:G_COL[norm] + k + 1]
            if k == 0:
                dve.wait_ge(rb_ready, 2 * norm + h + 1)
            if c >= HTMP:
                wait_lo(dve, c - HTMP + 1)
            dve.scalar_tensor_tensor(v(htmp(norm, c)), src, g, v(bank[7][:, :]),
                                     ALU.mult, ALU.mult).then_inc(h_tmp, 1)
            if k and c % 2 == 0:
                scaled_lo(norm, i - 1)
            elif k == kt - 1:
                scaled_lo(norm, i)

        def scaled_lo(norm, i):
            h, k = i // NORM_TILES[norm], i % NORM_TILES[norm]
            c = split_before(norm) + i
            tile, permuted = (k + 4, True) if norm == N_SSM else (k, False)
            dve.wait_ge(h_hi, c + 1)
            dve.tensor_tensor(dst_of(hT_lo, tile, h, permuted), src_of(htmp(norm, c), permuted),
                              dst_of(hT_hi, tile, h, permuted).bitcast(F32), ALU.subtract
                              ).then_inc(h_lo_odd, 1)

        def norm(which, src, before=lambda i: None):
            for kind, i in norm_order(which):
                if kind == "S":
                    before(i)
                elif kind == "R":
                    norm_rms(which, i)
                else:
                    norm_scale(which, i, *src(i))

        def x_tile(i):
            return (xT[:, i % KD, hs(i // KD)],)

        def ffn(which):
            b = U_OF[which]
            o0 = OUTS_FFN * which
            g0 = 4 * NCH * which
            d0 = 16 * NCH * which

            def take_up(i4, bnk, ob, gates=None):
                dve.wait_ge(ff_out, ob)
                dve.wait_ge(gate_taken, i4 + (bnk + 1 if gates is None else gates))
                dve.tensor_tensor(sg[:, bnk, :], sg[:, bnk, :], bank[bnk][:, :], ALU.mult).then_inc(up_taken, 1)

            def a_lo(i4, bnk):
                dve.wait_ge(a_hi_done, i4 + bnk + 1)
                dve.tensor_tensor(aT_lo[:, bnk, :], sg[:, bnk, :], aT_hi[:, bnk, :].bitcast(F32),
                                  ALU.subtract).then_inc(a_lo_done, 1)

            def take_down(n, ob):
                dve.wait_ge(ff_out, ob + (n + 1))
                xs = xT[:, n % KD, hs(n // KD)]
                dve.scalar_tensor_tensor(xs, bank[4 + n % 3][:, :], 0.5, xs, ALU.mult, ALU.add
                                         ).then_inc(down_taken, 1)

            def ups(i4, ob, middle):
                take_up(i4, 0, ob + 1)
                take_up(i4, 1, ob + 2)
                a_lo(i4, 0)
                a_lo(i4, 1)
                middle()
                take_up(i4, 2, ob + 3)
                take_up(i4, 3, ob + 4)
                a_lo(i4, 2)
                a_lo(i4, 3)

            take_up(g0, 0, o0 + 3, 1)
            split_lo(b + 3, b + 4)
            split_lo(b + 4, b + 5)
            a_lo(g0, 0)
            take_up(g0, 1, o0 + 6, 3)
            split_lo(b + 5, b + 6)
            take_up(g0, 2, o0 + 7, 4)
            a_lo(g0, 1)
            take_up(g0, 3, o0 + 8, 4)
            a_lo(g0, 2)
            a_lo(g0, 3)
            with dve.Fori(0, NCH - 1) as i:
                ob = i * 24 + (o0 + 8)
                i4 = i * 4 + (g0 + 4)
                for n in (6, 7, 8):
                    split_lo(b + n, i * 6 + (b + n + 1))
                for n in range(16):
                    take_down(n, ob + 4)
                for n in (9, 10):
                    split_lo(b + n, i * 6 + (b + n + 1))
                ups(i4, ob + 20, lambda: split_lo(b + 11, i * 6 + (b + 12)))
            if which == 0:
                split_lo(U_IN, U_IN + 1)
            return lambda n: take_down(n, o0 + OUTS_FFN - 16)

        def x_out(h):
            for t in range(4 * h, 4 * h + 4):
                dve.wait_ge(xt_done, 2 * t + 2)
                dve.tensor_copy(xT[:, 4:8, t * P:(t + 1) * P],
                                bank[X_BANK[2 * t + 1]][:, :].rearrange("p (k m) -> p k m", k=4)
                                ).then_inc(xt_dve, 1)

        x_out(0)
        dve.wait_ge(ident_loaded, 16)
        dve.wait_ge(gain_loaded, 16)
        for kind, i in norm_order(N_FF1):
            if kind == "R":
                norm_rms(N_FF1, i)
                split_lo(2 * i, 2 * i + 1)
                dve.wait_ge(xt_act, 4 * i + 4)
                dve.wait_ge(xt_dve, 4 * i + 4)
            elif kind == "A":
                norm_scale(N_FF1, i, *x_tile(i))
                if i == 7:
                    split_lo(1, 2)
                    x_out(1)
        dve.wait_ge(consts_loaded, CONST_DMAS * 16)
        dve.tensor_scalar(bglu_h[:, :], bglu[:, :], 0.5, None, ALU.mult)
        dve.tensor_scalar(gains[:, 20:24], gains[:, 20:24], 0.5, None, ALU.mult).then_inc(gains_set, 1)
        dve.wait_ge(gains_set, 1)
        dve.wait_ge(params_loaded, 16 * 10)
        for n in range(2):
            dve.tensor_tensor(ivt[:, n, :], par[:, n, :], par[:, n, :], ALU.mult).then_inc(inv_done, 1)
        dve.wait_ge(inv_done, 2)
        dve.tensor_tensor(ivt[:, 3, :], ivt[:, 0, :], ivt[:, 1, :], ALU.add).then_inc(inv_done, 1)
        dve.wait_ge(inv_done, 3)
        dve.reciprocal(ivt[:, 2, :], ivt[:, 3, :]).then_inc(inv_done, 1)
        take = ffn(0)
        for kind, i in norm_order(N_MIX):
            if kind == "S":
                take(i)
            elif kind == "R":
                norm_rms(N_MIX, i)
            else:
                norm_scale(N_MIX, i, *x_tile(i))
                if i == KD - 1:
                    split_lo(U_IN + 1, U_IN + 2)
                    split_lo(U_IN + 2, U_IN + 3)

        def v_out(b):
            dve.wait_ge(v_ready, b + 1)
            dve.tensor_copy(vwin[:, 4 * b:4 * b + 4, :], bank[4 + b][:, :].rearrange("p (n m) -> p n m", n=4)
                            ).then_inc(v_taken, 1)

        for n in range(3, N_IN):
            split_lo(U_IN + n, U_IN + n + 1)
        v_out(0)
        v_out(1)
        split_lo(U_GLU, U_GLU + 1)
        v_out(2)
        v_out(3)
        dve.tensor_tensor(dgl[:, :, :], ident[0:GH, 0:GH].unsqueeze(1).to_broadcast([GH, NG, GH]),
                          dsk[:, :].unsqueeze(2).to_broadcast([GH, NG, GH]), ALU.mult).then_inc(diag_chain, 1)
        dve.wait_ge(diag_chain, 1)

        def k_first(b):
            dve.wait_ge(k_ready, b + 1)
            dve.wait_ge(k_act, b + 1)
            j0, g2 = 4 * (b // 2), b % 2
            dst = kst[:, :, :].rearrange("p (j g) m -> p g j m", g=2)[:, g2, j0:j0 + 4, 0:GH]
            dg = dgl[:, :, :].rearrange("p (j g) m -> p g j m", g=2)[:, g2, j0:j0 + 4, :]
            src = bank[round_bank("K", b)][0:GH, :].rearrange("p (j m) -> p j m", j=4)[:, :, 0:GH]
            dve.tensor_tensor(dst, src, dg, ALU.add).then_inc(k_taken, 1)

        sc = [0]

        def step(ins):
            sc[0] += 1
            ins.then_inc(state_chain, 1)

        def steps_done():
            dve.wait_ge(state_chain, sc[0])

        def recurrence(b):
            js = slice(4 * b, 4 * b + 4)
            re, im = (bank[round_bank("I", b, i)][:, :] for i in range(2))
            c_ = csn[:, 0, js, :].rearrange("p j c -> p (j c)")
            s_ = csn[:, 1, js, :].rearrange("p j c -> p (j c)")
            trb = tr[:, js, :].rearrange("p j c -> p (j c)")
            tib = ti[:, js, :].rearrange("p j c -> p (j c)")
            r0, r1 = rtm[:, 0, :], rtm[:, 1, :]
            if b == 0:
                dve.wait_ge(cs_loaded, 16)
                dve.wait_ge(e_taken, 8)
            dve.wait_ge(inj_ready, b + 1)
            step(dve.tensor_tensor(trb, c_, re, ALU.mult))
            step(dve.tensor_tensor(r0, s_, im, ALU.mult))
            step(dve.tensor_tensor(tib, c_, im, ALU.mult))
            step(dve.tensor_tensor(r1, s_, re, ALU.mult))
            steps_done()
            dve.tensor_tensor(trb, trb, r0, ALU.add).then_inc(inj_taken, 1)
            step(dve.tensor_tensor(tib, tib, r1, ALU.subtract))
            steps_done()
            dve.wait_ge(inj_taken, b + 1)
            for j in range(4 * b, 4 * b + 4):
                for t_ in (tr, ti):
                    last = dve.tensor_tensor_scan(t_[:, j, :], dec8[:, j:j + 1].to_broadcast([P, NC]),
                                                  t_[:, j, :], 0.0, ALU.mult, ALU.add)
                    last.then_inc(scanned, 1)

        ac = [0]

        def astep(ins):
            ac[0] += 1
            ins.then_inc(att_chain, 1)
            dve.wait_ge(att_chain, ac[0])

        sink8 = sinkt[:, :, :, :].rearrange("p v n a -> p (v n a)")

        def wide_scores(m):
            return sco[m % 2][:, :, :, :, :].rearrange("p v n a k -> p (v n a) k")

        def maxima(m):
            if m == 0:
                dve.wait_ge(bias_loaded, 16)
            if m >= 2:
                dve.wait_ge(pt_ready, 2 * m - 2)
            for kv in range(NKV):
                dve.wait_ge(s_ready, 2 * m + kv + 1)
                dve.scalar_tensor_tensor(sco[m % 2][:, kv, :, :, :].rearrange("p n a k -> p n (a k)"),
                                         bank[kv][:, :].rearrange("p (n k) -> p n k", n=2), HD ** -0.5,
                                         biast[:, kv, :].unsqueeze(1).to_broadcast([P, 2, 256]),
                                         ALU.mult, ALU.add).then_inc(s_biased, 1)
            dve.wait_ge(s_biased, 2 * m + 2)
            if m == 0:
                astep(dve.memset(sco[0][:, :, 0, :, 0:CHUNK], -1e30))
            astep(dve.reduce_max(mx[:, :], wide_scores(m), AX.X))
            astep(dve.tensor_tensor(mx[:, :], mx[:, :], sink8, ALU.max))
            astep(dve.tensor_scalar(nm[:, m % 2, :], mx[:, :], -1.0, None, ALU.mult))
            dve.tensor_tensor(esk[:, m % 2, :], sink8, mx[:, :], ALU.subtract).then_inc(max_done, 1)

        def normalise(m):
            dve.wait_ge(exp_done, m + 1)
            astep(dve.tensor_tensor(ssum[:, m % 2, :], ssum[:, m % 2, :], esk[:, m % 2, :], ALU.add))
            astep(dve.reciprocal(rden[:, :], ssum[:, m % 2, :]))
            dve.tensor_tensor(wide_scores(m), wide_scores(m), rden[:, :].unsqueeze(2).to_broadcast([P, 8, P]),
                              ALU.mult).then_inc(p_done, 1)

        def z_low(k):
            if k == 0:
                dve.wait_ge(state_done, 4)
            for h in range(2):
                dve.wait_ge(z_hi, 2 * k + h + 1)
                dve.tensor_tensor(hT_lo[:, 4 + k, hs(h)], yT[:, k, hs(h)], hT_hi[:, 4 + k, hs(h)].bitcast(F32),
                                  ALU.subtract).then_inc(z_lo, 1)

        mixer_step = {"d": k_first, "R": recurrence, "A": maxima, "B": normalise, "z": z_low}
        for kind, b in MIXER_DVE:
            mixer_step[kind](b)

        split_lo(U_GLU + 1, U_GLU + 2)
        split_lo(U_OUT, U_OUT + 1)
        for kind, *at_ in GATED:
            if kind == "G":
                o = at_[0]
                zs = yT[:, o // 2, hs(o % 2)]
                dve.wait_ge(glu_tanh, o + 1)
                dve.scalar_tensor_tensor(zs, gth[:, o % 2, :], 1.0, zs, ALU.add, ALU.mult).then_inc(glu_done, 1)
            elif kind == "W":
                split_lo(U_OUT + at_[0], U_OUT + at_[0] + 1)
            elif kind == "R":
                norm_rms(*at_)
            elif kind == "A":
                i = at_[1]
                if at_[0] == N_ATT:
                    norm_scale(*at_, att_tile(qT, i % 4, i // 4), by_chunk)
                else:
                    norm_scale(*at_, yT[:, i % 4, hs(i // 4)])

        def take_mix(i):
            h, k = half_and_tile(N_FF2, i)
            dve.wait_ge(mix_out, i + 1)
            xs = xT[:, k, hs(h)]
            dve.tensor_tensor(xs, xs, bank[OUT_BANK[i % 6]][:, :], ALU.add).then_inc(mix_taken, 1)
            if i >= 3:
                split_lo(U_OUT + i - 3 + WS, U_OUT + i - 3 + WS + 1)

        norm(N_FF2, x_tile, take_mix)
        take = ffn(1)

        def out_rows(t):
            if t == 0:
                dve.wait_ge(gend_loaded, 16)
            for kh in range(2):
                dve.wait_ge(fin_ready, 2 * t + kh + 1)
                src, cs = bank[2 * (t % 2) + kh][:, :], slice(kh * HALF, (kh + 1) * HALF)
                if t in LATE:
                    ins = dve.tensor_tensor(osb[:, t, cs], src, gend[:, cs], ALU.mult)
                else:
                    ins = dve.scalar_tensor_tensor(osb[:, t, cs], src, rms4[:, t // 4, t % 4:t % 4 + 1],
                                                   gend[:, cs], ALU.mult, ALU.mult)
                ins.then_inc(fin_taken, 1)

        for kind, i in norm_order(N_END):
            if kind == "S":
                take(i)
                if i in (11, 13, 15):
                    out_rows((i - 11) // 2)
            elif i == 0:
                norm_rms(N_END, 0)
        out_rows(3)
        for t in LATE:
            out_rows(t)
        norm_rms(N_END, 1)
        for t in range(LATE[-1] + 1, KD):
            out_rows(t)

    @block.gpsimd
    def _(pool):
        def add_square(norm, n):
            h, k = half_and_tile(norm, n)
            if k == 0:
                return
            a = add_number(norm, n)
            pool.wait_ge(sq_done, squares_before(norm) + n + 1)
            if a:
                pool.wait_ge(ssq_done, a)
            pool.tensor_tensor(ssq[:, hs(h)], ssq[:, hs(h)], sqt[:, a % 2, :], ALU.add).then_inc(ssq_done, 1)

        def take_lo(norm, i, tile0=0, permuted=False):
            h, k = i // NORM_TILES[norm], i % NORM_TILES[norm]
            c = split_before(norm) + i
            if c % 2:
                return
            pool.wait_ge(h_hi, c + 1)
            pool.tensor_tensor(dst_of(hT_lo, tile0 + k, h, permuted), src_of(htmp(norm, c), permuted),
                               dst_of(hT_hi, tile0 + k, h, permuted).bitcast(F32), ALU.subtract
                               ).then_inc(h_lo_even, 1)

        def norm(which):
            for kind, i in norm_order(which):
                if kind == "S":
                    add_square(which, i)
                elif kind == "A":
                    take_lo(which, i)

        pool.memset(ones[:, :], 1.0)
        pool.memset(zero[:, :], 0.0)
        pool.memset(unit[:, 0, :, :], 1.0)
        pool.memset(unit[:, 1, :, :], 0.0)
        pool.memset(eps_t[:, :], EPS).then_inc(consts_set, 1)
        pool.wait_ge(consts_set, 1)
        zv = k_d.rearrange("(n g) h c -> n (g h) c", g=8)
        for n in range(4):
            pool.dma_start(zv[n][:, 0:(T - 1) * GH], zero[:, :]).then_inc(zero_stored, 16)
        norm(N_FF1)

        chain = [0]

        def link(ins):
            chain[0] += 1
            ins.then_inc(prep_chain, 1)
            pool.wait_ge(prep_chain, chain[0])

        slot = [0]

        def new():
            slot[0] += 1
            assert slot[0] <= NPAR, slot
            return pw[:, slot[0] - 1, :]

        def tt(o, a, b_, op):
            link(pool.tensor_tensor(o, a, b_, op))

        def ts(o, a, s1, op1, s2=None, op2=None):
            if op2 is None:
                link(pool.tensor_scalar(o, a, s1, None, op1))
            else:
                link(pool.tensor_scalar(o, a, s1, s2, op1, op2))

        def stt(o, a, s1, b_, op1, op2):
            ts(tmp, a, s1, op1)
            tt(o, tmp, b_, op2)

        t0, t1, t2, tmp = new(), new(), new(), new()
        nrm, red, pol, two = new(), new(), new(), new()

        def exp_parts(xv):
            ts(t0, xv, -150.0, ALU.max, 100.0, ALU.min)
            ts(nrm, t0, 1 / math.log(2.0), ALU.mult, MAGIC, ALU.add)
            ts(nrm, nrm, MAGIC, ALU.subtract)
            stt(red, nrm, -LN2_1, t0, ALU.mult, ALU.add)
            stt(red, nrm, -LN2_2, red, ALU.mult, ALU.add)
            ts(pol, red, 1 / 5040, ALU.mult)
            for c in (1 / 720, 1 / 120, 1 / 24, 1 / 6, 1 / 2, 1.0):
                stt(pol, pol, c, red, ALU.add, ALU.mult)
            ts(t1, nrm, -126.0, ALU.max, 127.0, ALU.min)
            tt(t2, nrm, t1, ALU.subtract)
            ts(pwi[:, 0, :], t1, 127.0, ALU.add, 2.0 ** 23, ALU.mult)
            ts(pwi[:, 1, :], t2, 127.0, ALU.add, 2.0 ** 23, ALU.mult)
            tt(two, pwi[:, 0, :].bitcast(F32), pwi[:, 1, :].bitcast(F32), ALU.mult)

        pool.wait_ge(params_loaded, 16 * 10)
        are, aim = par[:, 0, :], par[:, 1, :]
        dt, xr, th = new(), new(), new()
        exp_parts(par[:, 2, :])
        stt(dt, pol, 1.0, two, ALU.add, ALU.mult)
        tt(xr, are, dt, ALU.mult)
        tt(th, aim, dt, ALU.mult)
        exp_parts(xr)
        em1, mag = new(), new()
        tt(t0, two, pol, ALU.mult)
        stt(em1, two, -1.0, t0, ALU.add, ALU.add)
        tt(mag, two, t0, ALU.add)
        ts(nrm, th, 1 / (2 * math.pi), ALU.mult, MAGIC, ALU.add)
        ts(nrm, nrm, MAGIC, ALU.subtract)
        stt(red, nrm, -TWO_PI_1, th, ALU.mult, ALU.add)
        stt(red, nrm, -TWO_PI_2, red, ALU.mult, ALU.add)
        stt(red, nrm, -TWO_PI_3, red, ALU.mult, ALU.add)
        ts(red, red, 3.2, ALU.min, -3.2, ALU.max)
        q, q2, sn, cs = new(), new(), new(), new()
        ts(q, red, 0.25, ALU.mult)
        tt(q2, q, q, ALU.mult)
        ts(sn, q2, 1 / 362880, ALU.mult)
        for c in (-1 / 5040, 1 / 120, -1 / 6):
            stt(sn, sn, c, q2, ALU.add, ALU.mult)
        stt(sn, sn, 1.0, q, ALU.add, ALU.mult)
        ts(cs, q2, -1 / 3628800, ALU.mult)
        for c in (1 / 40320, -1 / 720, 1 / 24, -1 / 2):
            stt(cs, cs, c, q2, ALU.add, ALU.mult)
        ts(cs, cs, 1.0, ALU.add)
        s2_, c2_, sth, cth, cm1 = new(), new(), new(), new(), new()
        stt(s2_, sn, 2.0, cs, ALU.mult, ALU.mult)
        tt(t0, sn, sn, ALU.mult)
        ts(c2_, t0, -2.0, ALU.mult, 1.0, ALU.add)
        stt(sth, s2_, 2.0, c2_, ALU.mult, ALU.mult)
        tt(t0, s2_, s2_, ALU.mult)
        ts(cm1, t0, -2.0, ALU.mult)
        ts(cth, cm1, 1.0, ALU.add)
        er, ei, cr, ci = new(), new(), new(), new()
        tt(t0, em1, cth, ALU.mult)
        tt(er, t0, cm1, ALU.add)
        tt(ei, mag, sth, ALU.mult)
        lr = [lam[:, 0, k, :] for k in range(T + 1)]
        li = [lam[:, 1, k, :] for k in range(T + 1)]
        link(pool.memset(lr[0], 1.0))
        link(pool.memset(li[0], 0.0))
        tt(lr[1], mag, cth, ALU.mult)
        tt(li[1], mag, sth, ALU.mult)
        for k in range(1, T):
            tt(t0, lr[k], lr[1], ALU.mult)
            tt(t1, li[k], li[1], ALU.mult)
            tt(lr[k + 1], t0, t1, ALU.subtract)
            tt(t0, lr[k], li[1], ALU.mult)
            tt(t1, li[k], lr[1], ALU.mult)
            tt(li[k + 1], t0, t1, ALU.add)
        ts(lam[:, 2, :, :], lam[:, 1, :, :], -1.0, ALU.mult)
        pool.wait_ge(inv_done, 4)
        inv = ivt[:, 2, :]
        tt(t0, er, are, ALU.mult)
        tt(t1, ei, aim, ALU.mult)
        tt(t0, t0, t1, ALU.add)
        tt(cr, t0, inv, ALU.mult)
        tt(t0, ei, are, ALU.mult)
        tt(t1, er, aim, ALU.mult)
        tt(t0, t0, t1, ALU.subtract)
        tt(ci, t0, inv, ALU.mult)
        pr, pi = cth, sth
        for n in range(3):
            nr = rot8[:, 0, :] if n == 2 else new()
            ni = rot8[:, 1, :] if n == 2 else new()
            tt(t0, pr, pr, ALU.mult)
            tt(t1, pi, pi, ALU.mult)
            tt(nr, t0, t1, ALU.subtract)
            stt(ni, pr, 2.0, pi, ALU.mult, ALU.mult)
            pr, pi = nr, ni
        tt(t0, mag, mag, ALU.mult)
        tt(t0, t0, t0, ALU.mult)
        tt(dec8[:, :], t0, t0, ALU.mult)

        def wide(v, n=GH):
            return v.unsqueeze(2).to_broadcast([P, NJ, n])

        for o, (c0, c1, op) in enumerate(((cr, ci, ALU.subtract), (ci, cr, ALU.add))):
            tt(bc_tmp[:, 0, :, :], b_raw[:, 0, :, :], wide(c0), ALU.mult)
            tt(bc_tmp[:, 1, :, :], b_raw[:, 1, :, :], wide(c1), ALU.mult)
            tt(Bb[:, o, :, :], bc_tmp[:, 0, :, :], bc_tmp[:, 1, :, :], op)

        pc = [0]

        def link(ins):
            pc[0] += 1
            ins.then_inc(pool_chain, 1)
            pool.wait_ge(pool_chain, pc[0])

        def over_h(v, n):
            return v.unsqueeze(2).to_broadcast([P, n, GH])

        pool.wait_ge(ct_taken, 4)
        pt = [ptmp[:, i, :].rearrange("p (j h) -> p j h", h=GH) for i in range(2)]
        for k in range(T + 1):
            for o, (n0, n1) in enumerate(((0, 1), (2, 0))):
                link(pool.tensor_tensor(pt[0], CT[:, 0, :, :], over_h(lam[:, n0, k, :], NJ), ALU.mult))
                link(pool.tensor_tensor(pt[1], CT[:, 1, :, :], over_h(lam[:, n1, k, :], NJ), ALU.mult))
                link(pool.tensor_tensor(CL[:, o, :, k * GH:(k + 1) * GH], pt[0], pt[1], ALU.subtract))
        base_links = pc[0]

        cB = cur[:, :, :, 0:GH]
        cL = cur[:, :, :, GH:GH + T + 1]
        cR = cur[:, :, :, GH + T + 1]
        per = LINKS_PER_BATCH
        with pool.Fori(0, NJ // 4) as i:
            nl = [0]

            def ilink(ins):
                nl[0] += 1
                ins.then_inc(pool_chain, 1)
                pool.wait_ge(pool_chain, i * per + (base_links + nl[0]))

            def passed():
                pool.tensor_tensor(mark[:, :], unit[:, 0, 0, :], unit[:, 0, 0, :], ALU.mult)

            for ri in range(2):
                ilink(pool.tensor_copy(cB[:, ri], Bb[:, ri, bass.ds(i * 4, 4), :]))
                ilink(pool.tensor_copy(cL[:, ri].rearrange("p j k -> p k j"),
                                       lam[:, ri, :, bass.ds(i * 4, 4)]))
                ilink(pool.tensor_copy(cR[:, ri], rot8[:, ri, bass.ds(i * 4, 4)]))
            q = [ptmp[:, n, 0:4 * GH].rearrange("p (j h) -> p j h", h=GH) for n in range(2)]
            for t in range(T):
                e = T - 1 - t
                for o, (n0, n1, op) in enumerate(((0, 1, ALU.subtract), (1, 0, ALU.add))):
                    ilink(pool.tensor_tensor(q[0], cB[:, 0], over_h(cL[:, n0, :, e], 4), ALU.mult))
                    ilink(pool.tensor_tensor(q[1], cB[:, 1], over_h(cL[:, n1, :, e], 4), ALU.mult))
                    ilink(pool.tensor_tensor(EBb[:, o, :, t * GH:(t + 1) * GH], q[0], q[1], op))
            passed()
            pool.dma_start(eb_d[:, :, bass.ds(i * 4, 4), :], EBb[:, :, :, :]).then_inc(eb_stored, 16)
            pool.wait_ge(eb_stored, i * 32 + 16)
            ilink(pool.tensor_tensor(EBb[:, :, :, 0:1], unit[:, :, :, :], unit[:, :, :, :], ALU.mult))
            n = 1
            while n < NC:
                v = [ptmp[:, m, 0:4 * n].rearrange("p (j c) -> p j c", j=4) for m in range(2)]
                w = [cR[:, m, :].unsqueeze(2).to_broadcast([P, 4, n]) for m in range(2)]
                R = [EBb[:, m, :, 0:n] for m in range(2)]
                for o, (n0, n1, op) in enumerate(((0, 1, ALU.subtract), (1, 0, ALU.add))):
                    ilink(pool.tensor_tensor(v[0], R[0], w[n0], ALU.mult))
                    ilink(pool.tensor_tensor(v[1], R[1], w[n1], ALU.mult))
                    ilink(pool.tensor_tensor(EBb[:, o, :, n:2 * n], v[0], v[1], op))
                if 2 * n < NC:
                    a, b_ = ptmp[:, 0, 0:4], ptmp[:, 1, 0:4]
                    c_ = ptmp[:, 0, 4:8]
                    ilink(pool.tensor_tensor(a, cR[:, 0], cR[:, 0], ALU.mult))
                    ilink(pool.tensor_tensor(b_, cR[:, 1], cR[:, 1], ALU.mult))
                    ilink(pool.tensor_tensor(c_, cR[:, 0], cR[:, 1], ALU.mult))
                    ilink(pool.tensor_tensor(cR[:, 0], a, b_, ALU.subtract))
                    ilink(pool.tensor_tensor(cR[:, 1], c_, c_, ALU.add))
                n *= 2
            passed()
            pool.dma_start(cs_d[:, :, bass.ds(i * 4, 4), :], EBb[:, :, :, :]).then_inc(eb_stored, 16)
            pool.wait_ge(eb_stored, i * 32 + 32)
            assert nl[0] == per, nl

        norm(N_MIX)
        wait_lo(pool, split_before(N_ATT))
        pool.memset(kTp[:, 0:CHUNK], 0.0)
        pool.memset(vTp[:, 0:CHUNK], 0.0).then_inc(pads_set, 1)

        bc = [0]

        def back(ins):
            bc[0] += 1
            ins.then_inc(back_chain, 1)

        def back_done():
            pool.wait_ge(back_chain, bc[0])

        def to_next(o, a, b_, op):
            back(pool.tensor_tensor(o[:, :, 1:], a.rearrange("p (j c) -> p j c", j=4)[:, :, 0:NC - 1],
                                    b_.rearrange("p (j c) -> p j c", j=4)[:, :, 0:NC - 1], op))
            back(pool.memset(o[:, :, 0:1], 0.0))

        w0, w1, w2 = (t[:, :] for t in btm)
        for b in range(4):
            js = slice(4 * b, 4 * b + 4)
            c_ = csn[:, 0, js, :].rearrange("p j c -> p (j c)")
            s_ = csn[:, 1, js, :].rearrange("p j c -> p (j c)")
            trb = tr[:, js, :].rearrange("p j c -> p (j c)")
            tib = ti[:, js, :].rearrange("p j c -> p (j c)")
            pool.wait_ge(scanned, 8 * b + 8)
            back(pool.tensor_tensor(w0, s_, trb, ALU.mult))
            back(pool.tensor_tensor(w1, s_, tib, ALU.mult))
            back(pool.tensor_tensor(w2, c_, trb, ALU.mult))
            back_done()
            to_next(tr[:, js, :], w2, w1, ALU.subtract)
            back_done()
            back(pool.tensor_tensor(w2, c_, tib, ALU.mult))
            back_done()
            to_next(ti[:, js, :], w0, w2, ALU.add)
            back_done()
            pool.tensor_copy(mark[:, :], unit[:, 0, 0, :]).then_inc(state_done, 1)

        for kind, *at_ in GATED:
            if kind == "S":
                add_square(*at_)
            elif kind == "A":
                take_lo(*at_, tile0=4 * (at_[0] - N_ATT), permuted=at_[0] == N_SSM)
        norm(N_FF2)
        norm(N_END)

    ctx.close()


_INS = ["x", "ff1_norm", "ff1_w_gate", "ff1_w_up", "ff1_w_down", "mix_norm", "w_in", "sink", "a_re", "a_im",
        "b_re", "b_im", "c_re", "c_im", "d_skip", "log_dt", "w_glu", "b_glu", "attn_out_norm",
        "ssm_out_norm", "w_out", "ff2_norm", "ff2_w_gate", "ff2_w_up", "ff2_w_down", "final_norm"]


def alibi_bias():
    q = np.arange(CHUNK)[:, None]
    key = np.arange(2 * CHUNK)[None, :] - CHUNK
    dist = np.abs(q - key).astype(np.float32)
    out = np.zeros((2, CHUNK, NKV, 2, 2 * CHUNK), np.float32)
    for g2 in range(2):
        for kv in range(NKV):
            for a in range(2):
                head = kv * GQ + 2 * a + g2
                out[g2, :, kv, a, :] = -np.float32(2.0 ** -(head + 1)) * dist
    return out.reshape(P, NKV, 2 * 2 * CHUNK)


def kernel(**inputs):
    import numpy as _np
    import concourse.bacc as _bacc
    from concourse import mybir as _mybir
    from concourse.bass_utils import run_bass_kernel_spmd as _run

    nc = _bacc.Bacc("TRN2", target_bir_lowering=False, num_devices=1)
    arrays, args = {}, []
    host = [(name, _np.ascontiguousarray(inputs[name])) for name in _INS]
    host += [("ident", _np.eye(P, dtype=_np.float32)), ("bias", alibi_bias())]
    for name, a in host:
        arrays[f"in_{name}_dram"] = a
        args.append(nc.dram_tensor(f"in_{name}_dram", a.shape, _mybir.dt.from_np(a.dtype),
                                   kind="ExternalInput").ap())
    args.append(nc.dram_tensor("out_0_dram", (1, L, D), _mybir.dt.float32, kind="ExternalOutput").ap())
    block_kernel(nc, *args)
    r = _run(nc, [arrays], core_ids=[0])
    return r.results[0]["out_0_dram"]
```
